# Optimizing a Trainium2 kernel written in Bass

```python
import jax, jax.numpy as jnp
from jax import lax
import numpy as np
import math

D_MODEL = 1024
BATCH = 1
SEQ = 512
DEPTH = 1

D_MIX = D_MODEL
D_A = D_MIX // 2
D_B = D_MIX - D_A
HEAD_A = 64
G_A = D_A // HEAD_A
HEAD_B = 64
H_B = D_B // HEAD_B
CHUNK = 128
DECAY_RANK = 64
ICLR_RANK = 64
LN_EPS = 1e-5
GN_EPS = 64e-5
ALPHA = (2 * DEPTH) ** 0.25
BETA = (8 * DEPTH) ** -0.25

N_COLS_A = 3 * D_A
N_COLS_B = 4 * D_B + DECAY_RANK + ICLR_RANK
N_COLS = N_COLS_A + N_COLS_B


def _layer_norm(x, g, b, eps):
    xf = x.astype(jnp.float32)
    mu = jnp.mean(xf, axis=-1, keepdims=True)
    var = jnp.mean(jnp.square(xf - mu), axis=-1, keepdims=True)
    y = (xf - mu) * lax.rsqrt(var + eps)
    return (y * g.astype(jnp.float32) + b.astype(jnp.float32)).astype(x.dtype)

def _token_shift(p, mu):
    prev = jnp.pad(p, ((0, 0), (1, 0), (0, 0)))[:, :-1]
    return p + mu * (prev - p)

def _rwkv7_scan(r, w, k, v, a, b):
    Bsz, T, H, N = r.shape
    seq_first = lambda z: jnp.swapaxes(z, 0, 1)
    xs = tuple(seq_first(z) for z in (r, w, k, v, a, b))

    def step(S, inp):
        r_t, w_t, k_t, v_t, a_t, b_t = inp
        sa = jnp.einsum('bhij,bhj->bhi', S, a_t)
        S = S * w_t[:, :, None, :] + sa[..., None] * b_t[:, :, None, :] + v_t[..., None] * k_t[:, :, None, :]
        y = jnp.einsum('bhij,bhj->bhi', S, r_t)
        return S, y

    S0 = jnp.zeros((Bsz, H, N, N), jnp.float32)
    _, ys = lax.scan(step, S0, xs)
    return jnp.swapaxes(ys, 0, 1)

def _gmlp_branch(p_a, ln_v_g, ln_v_b, w_spatial, b_spatial):
    Bsz, T, _ = p_a.shape
    u = jax.nn.gelu(p_a[..., :D_A])
    v = jax.nn.gelu(p_a[..., D_A:2 * D_A])
    gate = p_a[..., 2 * D_A:]
    v = v.reshape(Bsz, T, G_A, HEAD_A)
    v = _layer_norm(v, ln_v_g, ln_v_b, LN_EPS)
    v = v.reshape(Bsz, T // CHUNK, CHUNK, G_A, HEAD_A)
    causal = jnp.tril(jnp.ones((CHUNK, CHUNK), dtype=bool))
    w_m = jnp.where(causal[None], w_spatial, jnp.zeros((), w_spatial.dtype))
    v = jnp.einsum('gts,bcsgd->bctgd', w_m, v) + jnp.swapaxes(b_spatial, 0, 1)[None, None, :, :, None]
    v = v.reshape(Bsz, T, D_A)
    return u * v * jax.nn.silu(gate)

def _rwkv7_branch(p_b, mu_b, w0, w_up, a0, a_up, k_k, k_a, r_k, gn_g, gn_b):
    Bsz, T, _ = p_b.shape
    p_b = _token_shift(p_b, mu_b)
    o = 0
    r = p_b[..., o:o + D_B]; o += D_B
    k = p_b[..., o:o + D_B]; o += D_B
    v = p_b[..., o:o + D_B]; o += D_B
    gate = p_b[..., o:o + D_B]; o += D_B
    wd = p_b[..., o:o + DECAY_RANK]; o += DECAY_RANK
    ad = p_b[..., o:o + ICLR_RANK]

    w_raw = -jax.nn.softplus(-(w0 + jnp.tanh(wd) @ w_up)) - 0.5
    a = jax.nn.sigmoid(a0 + ad @ a_up)

    heads = lambda z: z.reshape(Bsz, T, H_B, HEAD_B).astype(jnp.float32)
    kk = heads(k * k_k)
    kk = kk * lax.rsqrt(jnp.sum(kk * kk, axis=-1, keepdims=True) + 1e-12)
    k = k * (1 + (a - 1) * k_a)
    rh, kh, vh, ah = heads(r), heads(k), heads(v), heads(a)
    decay = jnp.exp(-jnp.exp(heads(w_raw)))

    y = _rwkv7_scan(rh, decay, kh, vh, -kk, kk * ah)
    y = _layer_norm(y, gn_g, gn_b, GN_EPS)
    bonus = jnp.sum(rh * kh * r_k.astype(jnp.float32), axis=-1, keepdims=True) * vh
    y = (y + bonus).reshape(Bsz, T, D_B).astype(p_b.dtype)
    return y * jax.nn.silu(gate)

def first_inputs(seed: int = 0) -> dict:
    key = jax.random.key(seed)
    ks = jax.random.split(key, 24)
    f32 = jnp.float32
    nrm = lambda k, s, sc: jax.random.normal(k, s, f32) * sc
    return {
        "x": nrm(ks[0], (BATCH, SEQ, D_MODEL), 1.0),
        "c": nrm(ks[1], (BATCH, D_MODEL), 1.0),
        "w_ada": nrm(ks[2], (D_MODEL, 3 * D_MODEL), D_MODEL ** -0.5),
        "b_ada": nrm(ks[3], (3 * D_MODEL,), 0.02),
        "w_in": nrm(ks[4], (D_MODEL, N_COLS), D_MODEL ** -0.5),
        "mu_b": jax.random.uniform(ks[5], (N_COLS_B,), f32),
        "ln_v_g": 1.0 + nrm(ks[6], (G_A, HEAD_A), 0.05),
        "ln_v_b": nrm(ks[7], (G_A, HEAD_A), 0.02),
        "w_spatial": nrm(ks[8], (G_A, CHUNK, CHUNK), CHUNK ** -0.5),
        "b_spatial": 1.0 + nrm(ks[9], (G_A, CHUNK), 0.1),
        "w0": jax.random.uniform(ks[10], (D_B,), f32, -4.0, 1.0),
        "w_up": nrm(ks[11], (DECAY_RANK, D_B), 0.5 * DECAY_RANK ** -0.5),
        "a0": nrm(ks[12], (D_B,), 0.5),
        "a_up": nrm(ks[13], (ICLR_RANK, D_B), 0.5 * ICLR_RANK ** -0.5),
        "k_k": 0.85 + nrm(ks[14], (D_B,), 0.05),
        "k_a": 1.0 + nrm(ks[15], (D_B,), 0.05),
        "r_k": nrm(ks[16], (H_B, HEAD_B), 0.1),
        "gn_g": 1.0 + nrm(ks[17], (H_B, HEAD_B), 0.05),
        "gn_b": nrm(ks[18], (H_B, HEAD_B), 0.02),
        "w_out": nrm(ks[19], (D_MIX, D_MODEL), BETA * D_MIX ** -0.5),
        "ln_g": 1.0 + nrm(ks[20], (D_MODEL,), 0.05),
        "ln_b": nrm(ks[21], (D_MODEL,), 0.02),
    }

def first_block(x, c, w_ada, b_ada, w_in, mu_b, ln_v_g, ln_v_b, w_spatial, b_spatial,
              w0, w_up, a0, a_up, k_k, k_a, r_k, gn_g, gn_b, w_out, ln_g, ln_b):
    mod = jax.nn.silu(c) @ w_ada + b_ada
    shift, scale, gate = [m[:, None, :] for m in jnp.split(mod, 3, axis=-1)]
    for _ in range(DEPTH):
        h = x * (1 + scale) + shift
        p = h @ w_in
        out_a = _gmlp_branch(p[..., :N_COLS_A], ln_v_g, ln_v_b, w_spatial, b_spatial)
        out_b = _rwkv7_branch(p[..., N_COLS_A:], mu_b, w0, w_up, a0, a_up, k_k, k_a, r_k, gn_g, gn_b)
        o = jnp.concatenate([out_a, out_b], axis=-1) @ w_out
        x = _layer_norm(ALPHA * x + gate * o, ln_g, ln_b, LN_EPS)
    return x


DEPTH_2 = 2

CTX_LEN = 256
GRID_W = 64
N_MIXERS = 3
E_BRANCH = 2 * D_MODEL
MLA_HEADS = D_MODEL // 64
MLA_NOPE = 128
MLA_ROPE = 64
MLA_V = 128
MLA_WIDTH = MLA_HEADS * MLA_V
MLA_Q_RANK = D_MODEL // 4
MLA_KV_RANK = D_MODEL // 8
MLA_SPLITS = (MLA_Q_RANK, MLA_Q_RANK + MLA_KV_RANK, MLA_Q_RANK + MLA_KV_RANK + MLA_ROPE)
MLA_IN = MLA_Q_RANK + MLA_KV_RANK + MLA_ROPE + MLA_WIDTH
ROPE_BASE = 10000.0
Q_BLOCK = 128
S5_GROUP = 16
S5_GROUPS = E_BRANCH // S5_GROUP
S5_STATE = 64
S5_CHUNK = 128
DT_MIN = 0.001
DT_MAX = 0.1
CONV_WIDTH = 31
CONV_PAD = CONV_WIDTH // 2
DEEPNORM_ALPHA = (2.0 * DEPTH_2) ** 0.25
DEEPNORM_BETA = (8.0 * DEPTH_2) ** -0.25
NORM_EPS = 1e-6


def _layernorm(x, g, b):
    xf = x.astype(jnp.float32)
    mu = jnp.mean(xf, axis=-1, keepdims=True)
    var = jnp.mean(jnp.square(xf - mu), axis=-1, keepdims=True)
    y = (xf - mu) * lax.rsqrt(var + NORM_EPS) * g.astype(jnp.float32) + b.astype(jnp.float32)
    return y.astype(x.dtype)

def _rmsnorm(x, g):
    xf = x.astype(jnp.float32)
    y = xf * lax.rsqrt(jnp.mean(jnp.square(xf), axis=-1, keepdims=True) + NORM_EPS) * g.astype(jnp.float32)
    return y.astype(x.dtype)

def _axial_rope_tables(rows):
    r, col = jnp.meshgrid(jnp.arange(rows, dtype=jnp.float32), jnp.arange(GRID_W, dtype=jnp.float32), indexing='ij')
    r, col = r.reshape(-1), col.reshape(-1)
    quarter = MLA_ROPE // 4
    inv = ROPE_BASE ** (-jnp.arange(quarter, dtype=jnp.float32) / quarter)
    ang_r = r[:, None] * inv
    ang_c = col[:, None] * inv
    ang = jnp.concatenate([ang_r, ang_r, ang_c, ang_c], axis=-1)
    return jnp.cos(ang), jnp.sin(ang)

def _apply_rope(v, cos, sin):
    x1, x2, x3, x4 = jnp.split(v, 4, axis=-1)
    rot = jnp.concatenate([-x2, x1, -x4, x3], axis=-1)
    return v * cos.astype(v.dtype) + rot * sin.astype(v.dtype)

def _mla_split(h, w_in, kv_norm):
    q_dn, kv_dn, k_rope, gate = jnp.split(h @ w_in, MLA_SPLITS, axis=-1)
    return q_dn, _rmsnorm(kv_dn, kv_norm), k_rope, gate

def _mla_queries(q_dn, q_norm, w_uq, w_uk):
    b, n, _ = q_dn.shape
    q = (_rmsnorm(q_dn, q_norm) @ w_uq).reshape(b, n, MLA_HEADS, MLA_NOPE + MLA_ROPE)
    q_abs = jnp.einsum('bnhd,chd->bnhc', q[..., :MLA_NOPE], w_uk)
    return q_abs, q[..., MLA_NOPE:]

def _mla_output(o_lat, gate, w_uv, w_out):
    b, n = o_lat.shape[:2]
    v = jnp.einsum('bnhc,chv->bnhv', o_lat, w_uv).reshape(b, n, MLA_WIDTH)
    return (v * jax.nn.silu(gate)) @ w_out

def _mla_mixer(h_lat, h_ctx, cos, sin, w_in, q_norm, kv_norm, w_uq, w_uk, w_uv, w_out, with_ctx_out):
    b, s, _ = h_lat.shape
    scale = (MLA_NOPE + MLA_ROPE) ** -0.5
    q_dn_l, ckv_l, kr_l, g_l = _mla_split(h_lat, w_in, kv_norm)
    q_dn_c, ckv_c, kr_c, g_c = _mla_split(h_ctx, w_in, kv_norm)
    qa_l, qr_l = _mla_queries(q_dn_l, q_norm, w_uq, w_uk)
    keys_lat = jnp.concatenate([ckv_l, _apply_rope(kr_l, cos, sin)], axis=-1)
    keys_ctx = jnp.concatenate([ckv_c, kr_c], axis=-1)

    def block(args):
        qa, qr, cs, sn = args
        q_pos = jnp.concatenate([qa, _apply_rope(qr, cs[:, None], sn[:, None])], axis=-1)
        q_free = jnp.concatenate([qa, qr], axis=-1)
        s_all = jnp.concatenate([jnp.einsum('bthd,bkd->bhtk', q_pos, keys_lat),
                                 jnp.einsum('bthd,bkd->bhtk', q_free, keys_ctx)], axis=-1)
        p = jax.nn.softmax(s_all.astype(jnp.float32) * scale, axis=-1).astype(ckv_l.dtype)
        return (jnp.einsum('bhtk,bkc->bthc', p[..., :s], ckv_l)
                + jnp.einsum('bhtk,bkc->bthc', p[..., s:], ckv_c))

    nblk = s // Q_BLOCK
    to_blocks = lambda a: a.reshape(b, nblk, Q_BLOCK, *a.shape[2:]).swapaxes(0, 1)
    o = lax.map(block, (to_blocks(qa_l), to_blocks(qr_l),
                        cos.reshape(nblk, Q_BLOCK, MLA_ROPE), sin.reshape(nblk, Q_BLOCK, MLA_ROPE)))
    o = o.swapaxes(0, 1).reshape(b, s, MLA_HEADS, MLA_KV_RANK)
    y_lat = _mla_output(o, g_l, w_uv, w_out)
    if not with_ctx_out:
        return y_lat, None
    qa_c, qr_c = _mla_queries(q_dn_c, q_norm, w_uq, w_uk)
    q_c = jnp.concatenate([qa_c, qr_c], axis=-1)
    p_c = jax.nn.softmax(jnp.einsum('bthd,bkd->bhtk', q_c, keys_ctx).astype(jnp.float32) * scale,
                         axis=-1).astype(ckv_c.dtype)
    o_c = jnp.einsum('bhtk,bkc->bthc', p_c, ckv_c)
    return y_lat, _mla_output(o_c, g_c, w_uv, w_out)

def _ssm_combine(left, right):
    a_l, b_l = left
    a_r, b_r = right
    return a_r * a_l, a_r * b_l + b_r

def _s5_direction(u_ctx, u_lat, lam, dt, bmat, cmat):
    lam_dt = lam * dt[:, None]
    lam_bar = jnp.exp(lam_dt)
    b_bar = ((lam_bar - 1.0) / lam)[..., None] * bmat
    powers = jnp.exp(lam_dt[None] * jnp.arange(1, S5_CHUNK + 1, dtype=jnp.float32)[:, None, None])

    def step(h, u_chunk):
        bu = jnp.einsum('btgs,gps->btgp', u_chunk.astype(jnp.complex64), b_bar)
        a = jnp.broadcast_to(lam_bar, bu.shape)
        _, xs = lax.associative_scan(_ssm_combine, (a, bu), axis=1)
        xs = xs + powers[None] * h[:, None]
        y = jnp.einsum('btgp,gsp->btgs', xs, cmat).real
        return xs[:, -1], y

    def run(u, h0):
        bsz, n = u.shape[:2]
        nch = n // S5_CHUNK
        chunks = u.reshape(bsz, nch, S5_CHUNK, S5_GROUPS, S5_GROUP).swapaxes(0, 1)
        h_fin, ys = lax.scan(step, h0, chunks)
        return h_fin, ys.swapaxes(0, 1).reshape(bsz, n, S5_GROUPS * S5_GROUP)

    h0 = jnp.zeros((u_lat.shape[0], S5_GROUPS, S5_STATE), jnp.complex64)
    h_ctx, y_ctx = run(u_ctx, h0)
    _, y_lat = run(u_lat, h_ctx)
    return y_ctx, y_lat

def _s5_mixer(h_lat, h_ctx, w_in, lam_re, lam_im, log_dt, b_re, b_im, c_re, c_im, d_skip, w_glu, b_glu, w_out,
              with_ctx_out):
    u_l, g_l = jnp.split(h_lat @ w_in, 2, axis=-1)
    u_c, g_c = jnp.split(h_ctx @ w_in, 2, axis=-1)
    ul, uc = u_l.astype(jnp.float32), u_c.astype(jnp.float32)
    dsk = d_skip.astype(jnp.float32)
    y_l, y_c = dsk * ul, dsk * uc
    f32 = lambda a: a.astype(jnp.float32)
    for direction in range(2):
        lam = lax.complex(jnp.minimum(f32(lam_re[direction]), -1e-4), f32(lam_im[direction]))
        dt = jnp.exp(f32(log_dt[direction]))
        bmat = lax.complex(f32(b_re[direction]), f32(b_im[direction]))
        cmat = lax.complex(f32(c_re[direction]), f32(c_im[direction]))
        if direction == 0:
            yc, yl = _s5_direction(uc, ul, lam, dt, bmat, cmat)
        else:
            yc, yl = _s5_direction(jnp.flip(uc, 1), jnp.flip(ul, 1), lam, dt, bmat, cmat)
            yc, yl = jnp.flip(yc, 1), jnp.flip(yl, 1)
        y_l, y_c = y_l + yl, y_c + yc

    def glu_out(y, g):
        y = jax.nn.gelu(y.astype(g.dtype))
        ya, yb = jnp.split(y @ w_glu + b_glu, 2, axis=-1)
        return ((ya * jax.nn.sigmoid(yb)) * jax.nn.silu(g)) @ w_out

    y_ctx = glu_out(y_c, g_c) if with_ctx_out else None
    return glu_out(y_l, g_l), y_ctx

def _conv_mixer(h_lat, h_ctx, w_in, dw, dw_b, ln_g, ln_b, w_out, with_ctx_out):
    def branch(h):
        a, bgate, g = jnp.split(h @ w_in, 3, axis=-1)
        v = a * jax.nn.sigmoid(bgate)
        v = lax.conv_general_dilated(v, dw[:, None, :], window_strides=(1,), padding=[(CONV_PAD, CONV_PAD)],
                                     dimension_numbers=('NWC', 'WIO', 'NWC'),
                                     feature_group_count=E_BRANCH) + dw_b
        v = jax.nn.silu(_layernorm(v, ln_g, ln_b))
        return (v * jax.nn.silu(g)) @ w_out
    y_ctx = branch(h_ctx) if with_ctx_out else None
    return branch(h_lat), y_ctx

def second_inputs(seed: int = 0) -> dict:
    key = jax.random.key(seed)
    ks = iter(jax.random.split(key, 48))
    f = jnp.float32
    nrm = lambda shape, scale: jax.random.normal(next(ks), shape, f) * scale
    n_a, n_b, n_c = [len(range(k, DEPTH_2, N_MIXERS)) for k in range(N_MIXERS)]
    D, E, G, P, GS = D_MODEL, E_BRANCH, S5_GROUPS, S5_STATE, S5_GROUP
    lam_im = jnp.broadcast_to(math.pi * jnp.arange(P, dtype=f), (n_b, 2, G, P))
    return {
        'x': nrm((BATCH, SEQ, D), 1.0),
        'c': nrm((BATCH, D), 1.0),
        'ctx': nrm((BATCH, CTX_LEN, D), 1.0),
        'c_ctx': nrm((D,), 1.0),
        'w_mod': nrm((DEPTH_2, D, 3 * D), 0.5 * D ** -0.5),
        'b_mod': nrm((DEPTH_2, 3 * D), 0.02),
        'ln_g': 1.0 + nrm((DEPTH_2, D), 0.02),
        'ln_b': nrm((DEPTH_2, D), 0.02),
        'mla_w_in': nrm((n_a, D, MLA_IN), D ** -0.5),
        'mla_q_norm': 1.0 + nrm((n_a, MLA_Q_RANK), 0.02),
        'mla_kv_norm': 1.0 + nrm((n_a, MLA_KV_RANK), 0.02),
        'mla_w_uq': nrm((n_a, MLA_Q_RANK, MLA_HEADS * (MLA_NOPE + MLA_ROPE)), MLA_Q_RANK ** -0.5),
        'mla_w_uk': nrm((n_a, MLA_KV_RANK, MLA_HEADS, MLA_NOPE), MLA_NOPE ** -0.5),
        'mla_w_uv': nrm((n_a, MLA_KV_RANK, MLA_HEADS, MLA_V), MLA_KV_RANK ** -0.5),
        'mla_w_out': nrm((n_a, MLA_WIDTH, D), DEEPNORM_BETA * MLA_WIDTH ** -0.5),
        's5_w_in': nrm((n_b, D, 2 * E), D ** -0.5),
        's5_lam_re': -0.5 + nrm((n_b, 2, G, P), 0.01),
        's5_lam_im': lam_im,
        's5_log_dt': jax.random.uniform(next(ks), (n_b, 2, G), f, math.log(DT_MIN), math.log(DT_MAX)),
        's5_b_re': nrm((n_b, 2, G, P, GS), (2.0 * GS) ** -0.5),
        's5_b_im': nrm((n_b, 2, G, P, GS), (2.0 * GS) ** -0.5),
        's5_c_re': nrm((n_b, 2, G, GS, P), P ** -0.5),
        's5_c_im': nrm((n_b, 2, G, GS, P), P ** -0.5),
        's5_d': nrm((n_b, E), 0.5),
        's5_w_glu': nrm((n_b, E, 2 * E), E ** -0.5),
        's5_b_glu': nrm((n_b, 2 * E), 0.02),
        's5_w_out': nrm((n_b, E, D), DEEPNORM_BETA * E ** -0.5),
        'cv_w_in': nrm((n_c, D, 3 * E), D ** -0.5),
        'cv_dw': nrm((n_c, CONV_WIDTH, E), CONV_WIDTH ** -0.5),
        'cv_dw_b': nrm((n_c, E), 0.02),
        'cv_ln_g': 1.0 + nrm((n_c, E), 0.02),
        'cv_ln_b': nrm((n_c, E), 0.02),
        'cv_w_out': nrm((n_c, E, D), DEEPNORM_BETA * E ** -0.5),
    }

def second_block(x, c, ctx, c_ctx, w_mod, b_mod, ln_g, ln_b,
              mla_w_in, mla_q_norm, mla_kv_norm, mla_w_uq, mla_w_uk, mla_w_uv, mla_w_out,
              s5_w_in, s5_lam_re, s5_lam_im, s5_log_dt, s5_b_re, s5_b_im, s5_c_re, s5_c_im, s5_d,
              s5_w_glu, s5_b_glu, s5_w_out,
              cv_w_in, cv_dw, cv_dw_b, cv_ln_g, cv_ln_b, cv_w_out):
    n_tokens = x.shape[1]
    ROWS = n_tokens // GRID_W
    cos, sin = _axial_rope_tables(ROWS)
    cond = jax.nn.silu(c)
    cond_ctx = jax.nn.silu(c_ctx)
    for i in range(DEPTH_2):
        kind, j = i % N_MIXERS, i // N_MIXERS
        with_ctx_out = i < DEPTH_2 - 1
        sh, sc, gt = jnp.split(cond @ w_mod[i] + b_mod[i], 3, axis=-1)
        sh_c, sc_c, gt_c = jnp.split(cond_ctx @ w_mod[i] + b_mod[i], 3, axis=-1)
        h_lat = x * (1.0 + sc[:, None]) + sh[:, None]
        h_ctx = ctx * (1.0 + sc_c) + sh_c
        if kind == 0:
            y_lat, y_ctx = _mla_mixer(h_lat, h_ctx, cos, sin, mla_w_in[j], mla_q_norm[j], mla_kv_norm[j],
                                      mla_w_uq[j], mla_w_uk[j], mla_w_uv[j], mla_w_out[j], with_ctx_out)
        elif kind == 1:
            y_lat, y_ctx = _s5_mixer(h_lat, h_ctx, s5_w_in[j], s5_lam_re[j], s5_lam_im[j], s5_log_dt[j],
                                     s5_b_re[j], s5_b_im[j], s5_c_re[j], s5_c_im[j], s5_d[j],
                                     s5_w_glu[j], s5_b_glu[j], s5_w_out[j], with_ctx_out)
        else:
            y_lat, y_ctx = _conv_mixer(h_lat, h_ctx, cv_w_in[j], cv_dw[j], cv_dw_b[j], cv_ln_g[j], cv_ln_b[j],
                                       cv_w_out[j], with_ctx_out)
        x = _layernorm(DEEPNORM_ALPHA * x + gt[:, None] * y_lat, ln_g[i], ln_b[i])
        if with_ctx_out:
            ctx = _layernorm(DEEPNORM_ALPHA * ctx + gt_c * y_ctx, ln_g[i], ln_b[i])
    return x


def setup_inputs(seed=0):
    out = dict(first_inputs(seed))
    for name, value in second_inputs(seed + 1).items():
        if name != "x":
            out[name + "_2"] = value
    return out


def reference(
    x, c, w_ada, b_ada, w_in, mu_b, ln_v_g, ln_v_b, w_spatial, b_spatial, w0, w_up, a0, a_up,
    k_k, k_a, r_k, gn_g, gn_b, w_out, ln_g, ln_b, c_2, ctx_2, c_ctx_2, w_mod_2, b_mod_2, ln_g_2,
    ln_b_2, mla_w_in_2, mla_q_norm_2, mla_kv_norm_2, mla_w_uq_2, mla_w_uk_2, mla_w_uv_2,
    mla_w_out_2, s5_w_in_2, s5_lam_re_2, s5_lam_im_2, s5_log_dt_2, s5_b_re_2, s5_b_im_2,
    s5_c_re_2, s5_c_im_2, s5_d_2, s5_w_glu_2, s5_b_glu_2, s5_w_out_2, cv_w_in_2, cv_dw_2,
    cv_dw_b_2, cv_ln_g_2, cv_ln_b_2, cv_w_out_2,
):
    x = first_block(
        x, c, w_ada, b_ada, w_in, mu_b, ln_v_g, ln_v_b, w_spatial, b_spatial, w0, w_up, a0,
        a_up, k_k, k_a, r_k, gn_g, gn_b, w_out, ln_g, ln_b,
    )
    return second_block(
        x, c_2, ctx_2, c_ctx_2, w_mod_2, b_mod_2, ln_g_2, ln_b_2, mla_w_in_2, mla_q_norm_2,
        mla_kv_norm_2, mla_w_uq_2, mla_w_uk_2, mla_w_uv_2, mla_w_out_2, s5_w_in_2, s5_lam_re_2,
        s5_lam_im_2, s5_log_dt_2, s5_b_re_2, s5_b_im_2, s5_c_re_2, s5_c_im_2, s5_d_2,
        s5_w_glu_2, s5_b_glu_2, s5_w_out_2, cv_w_in_2, cv_dw_2, cv_dw_b_2, cv_ln_g_2, cv_ln_b_2,
        cv_w_out_2,
    )


_drawn_inputs = setup_inputs


def setup_inputs(seed=0):
    import zlib

    import numpy as np

    out = dict(_drawn_inputs(seed))
    spreads = {}
    factors = {'b_ada': 3.985,
     'ln_v_g': 8.0,
     'ln_v_b': 8.0,
     'b_spatial': 3.405,
     'w_up': 3.04,
     'k_k': 5.125,
     'k_a': 3.3,
     'gn_g': 7.695,
     'gn_b': 8.0,
     'ln_b': 2.761,
     'c_2': 2.767,
     'ctx_2': 8.0,
     'c_ctx_2': 8.0,
     'b_mod_2': 8.0,
     'mla_w_in_2': 2.946,
     'mla_q_norm_2': 8.0,
     'mla_kv_norm_2': 8.0,
     'mla_w_uq_2': 8.0,
     'mla_w_uk_2': 8.0,
     'mla_w_uv_2': 3.115,
     'mla_w_out_2': 3.155,
     's5_w_in_2': 4.412,
     's5_lam_re_2': 64.0,
     's5_lam_im_2': 64.0,
     's5_log_dt_2': 64.0,
     's5_b_re_2': 64.0,
     's5_b_im_2': 64.0,
     's5_c_re_2': 64.0,
     's5_c_im_2': 64.0,
     's5_d_2': 4.871,
     's5_w_glu_2': 4.421,
     's5_b_glu_2': 51.104,
     's5_w_out_2': 4.358}
    for name, (base, spread) in spreads.items():
        noise = np.random.default_rng([zlib.crc32(name.encode()), seed]).standard_normal(out[name].shape)
        drawn = base * np.exp(spread * noise) if base else spread * noise
        out[name] = __import__('jax').numpy.asarray(drawn.astype(out[name].dtype))
    for name, factor in factors.items():
        out[name] = (out[name] * factor).astype(out[name].dtype)
    return out
```

```python
import math
from contextlib import ExitStack

import numpy as np
import concourse.bass as bass
from concourse import mybir

ALU = mybir.AluOpType
ACT = mybir.ActivationFunctionType
AX = mybir.AxisListType
F32 = mybir.dt.float32

P = 128
BANK = 512
D = 1024
KD = D // P
T = 512
CTX = 256
TC = T + CTX
HALF = TC // 2
TT = T // P

D_A = D_B = D // 2
HEAD = 64
NPAIR = D_B // P
CHUNK = 64
NCHUNK = T // CHUNK
W_IN_TILES = 29
IN_ORDER = [*range(4, 8), *range(0, 4), *range(8, W_IN_TILES)]
LEVELS = 5
LN_EPS, GN_EPS, NORM_EPS = 1e-5, 64e-5, 1e-6
ALPHA_1 = 2.0 ** 0.25
ALPHA_2 = 4.0 ** 0.25

HEADS = 16
Q_RANK, KV_RANK, ROPE = 256, 128, 64
E_BRANCH = 2048
KE = E_BRANCH // P
SOFTMAX_SCALE = (128 + 64) ** -0.5

GROUPS, STATE, GS = 128, 64, 16
PAIRS = GROUPS // 2
STEP = 8
C_LAT, C_CTX = T // STEP, CTX // STEP
C_ALL = C_CTX + C_LAT
TABLE = 8

SLOT = KD * P
RING = 6

MASKS = ["ident", "ones", "block_ones", "dup", "diag2_lower", "diag2_upper", "incl_upper",
         "strict_upper", "level1", "level2", "level3", "level4", "level5"]
TABLES = {"reset": T, "rope": T}

COLUMNS = [
    ("c", KD), ("b_ada", 3 * KD), ("mu_b", 17), ("w0", NPAIR), ("a0", NPAIR), ("k_k", NPAIR),
    ("k_a", NPAIR), ("r_k", NPAIR), ("gn_g", NPAIR), ("gn_b", NPAIR), ("ln_g", KD), ("ln_b", KD),
    ("c_2", KD), ("c_ctx_2", KD), ("b_mod_0", 3 * KD), ("b_mod_1", 3 * KD), ("ln_g_20", KD),
    ("ln_b_20", KD), ("ln_g_21", KD), ("ln_b_21", KD), ("q_norm", 2), ("kv_norm", 1),
    ("s5_d", KE), ("b_glu", 2 * KE),
]
COLUMN_AT, N_COLUMNS = {}, 0
for _name, _n in COLUMNS:
    COLUMN_AT[_name] = (N_COLUMNS, _n)
    N_COLUMNS += _n


def constants():
    r = np.arange(P)
    row, col = r[:, None], r[None, :]
    same = lambda n: row // n == col // n
    masks = {
        "ident": row == col,
        "ones": np.ones((P, P)),
        "block_ones": same(64),
        "dup": row % 64 == col % 64,
        "diag2_lower": same(2) & (col < row),
        "diag2_upper": same(2) & (row < col),
        "incl_upper": same(CHUNK) & (row <= col),
        "strict_upper": same(CHUNK) & (row < col),
    }
    for level in range(1, LEVELS + 1):
        n = 2 ** level
        masks[f"level{level}"] = same(2 * n) & (row // n < col // n)
    out = {k: np.asarray(masks[k], np.float32) for k in MASKS}
    out["reset"] = np.tile((np.arange(T) % CHUNK != 0).astype(np.float32), (P, 1))
    pos = np.arange(T, dtype=np.float32)
    inv = (np.float32(10000.0) ** (-np.arange(16, dtype=np.float32) / np.float32(16))).astype(np.float32)
    ang_r = np.floor(pos / 64)[:, None] * inv
    ang_c = (pos % 64)[:, None] * inv
    ang = np.concatenate([ang_r, ang_r, ang_c, ang_c], axis=-1).astype(np.float32)
    sign = np.repeat(np.array([-1, 1, -1, 1], np.float32), 16)
    out["rope"] = np.concatenate([np.cos(ang).T, (np.sin(ang) * sign).T]).astype(np.float32)
    return np.ascontiguousarray(np.concatenate([out[k] for k in MASKS + list(TABLES)], axis=1))


N_CONST = len(MASKS) * P + sum(TABLES.values())


def weight_stream():
    s = [("w_ada", i, SLOT, ("ada", i)) for i in range(3 * KD)]
    s += [("w_in", i, SLOT, ("in", i)) for i in IN_ORDER]
    s += [("w_out", i, SLOT, ("out", i)) for i in range(KD)]
    s += [("w_mod_0", i, SLOT, ("mod0", i)) for i in range(3 * KD)]
    s += [("mla_in", i, SLOT, ("mla_in", i)) for i in range(4)]
    s += [("mla_in", i, SLOT, ("mla_in", i)) for i in range(4, 20)]
    s += [("mla_head", i, 768, ("head", i)) for i in range(HEADS)]
    s += [("mla_out", i, SLOT, ("mla_out", i)) for i in range(2 * KD)]
    s += [("w_mod_1", i, SLOT, ("mod1", i)) for i in range(3 * KD)]
    s += [("s5_in", i, SLOT, ("s5_in", i)) for i in range(2 * KE)]
    s += [("s5_glu", j, SLOT, ("glu", j)) for i in range(KE) for j in (2 * i, 2 * i + 1, 2 * KE + 2 * i, 2 * KE + 2 * i + 1)]
    s += [("s5_out", i, SLOT, ("s5_out", i)) for i in range(2 * KD)]
    return s


class Count:

    def __init__(self, semaphore, table):
        self.semaphore, self.table, self.value = semaphore, table, 0

    def mark(self, *step):
        self.table[step] = (self.semaphore, self.value)

    def up(self, *step):
        self.value += 1
        if step:
            self.mark(*step)
        return self.value


def build(nc, io, known):
    stream = weight_stream()
    slot_of = {key: n for n, (_, _, _, key) in enumerate(stream)}
    memory = ExitStack()
    with memory:
        psum = memory.enter_context(nc.psum_tensor("psum", [P, 8, BANK], F32))
        pe_done = memory.enter_context(nc.semaphore("pe_done"))
        act_done = memory.enter_context(nc.semaphore("act_done"))
        dve_done = memory.enter_context(nc.semaphore("dve_done"))
        pool_done = memory.enter_context(nc.semaphore("pool_done"))
        done = {"pe": pe_done, "act": act_done, "dve": dve_done, "pool": pool_done}
        steps = {}
        pe_count, act_count = Count("pe", steps), Count("act", steps)
        dve_count, pool_count = Count("dve", steps), Count("pool", steps)

        def at(*step):
            who, count = known.get(step, ("pe", 1))
            return done[who], count

        small_loaded = memory.enter_context(nc.semaphore("small_loaded"))
        x_loaded = memory.enter_context(nc.semaphore("x_loaded"))
        ctx_loaded = memory.enter_context(nc.semaphore("ctx_loaded"))
        gmlp_loaded = memory.enter_context(nc.semaphore("gmlp_loaded"))
        stored = memory.enter_context(nc.semaphore("stored"))
        slot_loaded = [memory.enter_context(nc.semaphore(f"slot_loaded_{i}")) for i in range(RING)]
        s5_loaded = [memory.enter_context(nc.semaphore(f"s5_loaded_{i}")) for i in range(4)]
        lam_loaded = memory.enter_context(nc.semaphore("lam_loaded"))
        table_loaded = memory.enter_context(nc.semaphore("table_loaded"))
        lags_moved = [memory.enter_context(nc.semaphore(f"lags_moved_{i}")) for i in range(4)]

        def sb(stack, name, shape):
            return stack.enter_context(nc.sbuf_tensor(name, [P] + shape, F32))

        ring = sb(memory, "ring", [RING, SLOT])
        const = sb(memory, "const", [N_CONST])
        cols = sb(memory, "cols", [N_COLUMNS])
        xT = sb(memory, "xT", [KD, T])
        eps = sb(memory, "eps", [4])
        MISC = 3 * KD * 4 + 64
        misc = sb(memory, "misc", [MISC])

        def mask(name):
            n = MASKS.index(name)
            return const[:, n * P:(n + 1) * P]

        reset = const[:, len(MASKS) * P:len(MASKS) * P + T]
        rope = const[:, len(MASKS) * P + T:len(MASKS) * P + 2 * T]

        def col(name, i=None):
            a, n = COLUMN_AT[name]
            return cols[:, a:a + n] if i is None else cols[:, a + i:a + i + 1]

        def slot(key):
            return ring[:, slot_of[key] % RING, :]

        def tile_w(key, k, width=P):
            return slot(key)[:, k * width:(k + 1) * width]

        def need_slot(e, key):
            n = slot_of[key]
            e.wait_ge(slot_loaded[n % RING], 16 * (n // RING + 1))

        def bank(n, a=0, b=BANK):
            return psum[:, n, a:b]

        def flat(a, b):
            return psum[:, :, :].rearrange("p b n -> p (b n)")[:, a:b]

        def over(ap, n):
            return ap.unsqueeze(1).broadcast_to([P, n, ap.shape[-1]])

        def along(ap, n):
            return ap.unsqueeze(2).broadcast_to([P, ap.shape[-1], n])


        def modulation_pe(pe, name, vec, n_vec):
            pe.wait_ge(*at(name, "vec"))
            for i in range(3 * KD):
                need_slot(pe, (name, i))
                for k in range(KD):
                    ins = nc.tensor.matmul(bank(0, n_vec * i, n_vec * (i + 1)), tile_w((name, i), k),
                                           vec[:, k, :], start=(k == 0), stop=(k == KD - 1))
                ins.then_inc(pe_done, 1)
                pe_count.up("free", slot_of[(name, i)])
            pe_count.mark(name, "sums")

        def layer_norm_cm(name, z, tokens, sq, stat, gain, shift, eps_col, out, out_view):
            parts = [(flat(5 * BANK, 5 * BANK + T), 0, T)]
            if tokens > T:
                parts = [(flat(5 * BANK - CTX, 5 * BANK), 0, CTX), (flat(5 * BANK, 5 * BANK + T), CTX, T)]
            sums = flat(5 * BANK + T - tokens, 5 * BANK + T)

            def pe_part(pe):
                for what, src in (("mean", z), ("var", sq)):
                    for k in range(KD):
                        pe.wait_ge(*at(name, "z" if what == "mean" else "sq", k))
                    for o, a, n in parts:
                        for k in range(KD):
                            ins = nc.tensor.matmul(o, mask("ones"), src[:, k, a:a + n],
                                                   start=(k == 0), stop=(k == KD - 1))
                    ins.then_inc(pe_done, 1)
                    pe_count.up(name, what)

            def act_part(act):
                for k in range(KD):
                    act.wait_ge(*at(name, "centred", k))
                    nc.scalar.activation(sq[:, k, :], z[:, k, :], ACT.Square).then_inc(act_done, 1)
                    act.wait_ge(act_done, act_count.up(name, "sq", k))
                act.wait_ge(*at(name, "var"))
                nc.scalar.activation(stat[:, 0, :], sums, ACT.Sqrt, bias=eps_col, scale=1.0 / D).then_inc(act_done, 1)
                act.wait_ge(act_done, act_count.up(name, "std"))

            def dve_part(dve):
                dve.wait_ge(*at(name, "mean"))
                nc.vector.tensor_scalar(stat[:, 1, :], sums, 1.0 / D, None, ALU.mult).then_inc(dve_done, 1)
                dve.wait_ge(dve_done, dve_count.up())
                for k in range(KD):
                    nc.vector.tensor_tensor(z[:, k, :], z[:, k, :], stat[:, 1, :], ALU.subtract).then_inc(dve_done, 1)
                    dve.wait_ge(dve_done, dve_count.up(name, "centred", k))
                dve.wait_ge(*at(name, "std"))
                nc.vector.reciprocal(stat[:, 1, :], stat[:, 0, :]).then_inc(dve_done, 1)
                dve.wait_ge(dve_done, dve_count.up())
                for k in range(KD):
                    nc.vector.tensor_tensor(z[:, k, :], z[:, k, :], stat[:, 1, :], ALU.mult).then_inc(dve_done, 1)
                    dve.wait_ge(dve_done, dve_count.up())
                    nc.vector.tensor_scalar(out_view(out, k), out_view(z, k), gain(k), shift(k),
                                            ALU.mult, ALU.add).then_inc(dve_done, 1)
                    dve.wait_ge(dve_done, dve_count.up(name, "out", k))
            return pe_part, act_part, dve_part

        def phase_end(engine, count, phase):
            count.mark("end", phase, count.semaphore)
            for who in ("pe", "act", "dve", "pool"):
                if who != count.semaphore and known.get(("end", phase, who), ("", 1))[1] > 0:
                    engine.wait_ge(*at("end", phase, who))

        mod = misc[:, 0:6 * KD]

        def start_dve(dve):
            for i, v in enumerate((LN_EPS, GN_EPS, NORM_EPS, 1e-12)):
                nc.vector.memset(eps[:, i:i + 1], v).then_inc(dve_done, 1)
                dve.wait_ge(dve_done, dve_count.up())
            dve.wait_ge(small_loaded, 32)
            dve_count.mark("eps")


        first = ExitStack()
        hT = sb(first, "hT", [KD, T])
        silu_c = misc[:, 6 * KD:7 * KD].unsqueeze(2)
        ada = misc[:, 0:3 * KD]

        def ada_act(act):
            act.wait_ge(small_loaded, 32)
            nc.scalar.activation(silu_c[:, :, 0], col("c"), ACT.Silu).then_inc(act_done, 1)
            act.wait_ge(act_done, act_count.up("ada", "vec"))

        def ada_dve(dve):
            dve.wait_ge(*at("ada", "sums"))
            nc.vector.tensor_tensor(ada, bank(0, 0, 3 * KD), col("b_ada"), ALU.add).then_inc(dve_done, 1)
            dve.wait_ge(dve_done, dve_count.up())
            nc.vector.tensor_scalar(ada[:, KD:2 * KD], ada[:, KD:2 * KD], 1.0, None, ALU.add).then_inc(dve_done, 1)
            dve.wait_ge(dve_done, dve_count.up())
            dve.wait_ge(x_loaded, 16)
            for k in range(KD):
                nc.vector.tensor_scalar(hT[:, k, :], xT[:, k, :], ada[:, KD + k:KD + k + 1],
                                        ada[:, k:k + 1], ALU.mult, ALU.add).then_inc(dve_done, 1)
                dve.wait_ge(dve_done, dve_count.up("hT", k))


        rkvg = sb(first, "rkvg", [16, T])
        wdad = sb(first, "wdad", [T])
        gm = ExitStack()
        uT = sb(gm, "uT", [4, T])
        gT = sb(gm, "gT", [4, T])
        vT = sb(gm, "vT", [TT, D_A])
        vsq = sb(gm, "vsq", [TT, D_A])
        vstat = sb(gm, "vstat", [4, 32])
        lnv = sb(gm, "lnv", [2, D_A])
        b_sp = sb(gm, "b_sp", [4, P])
        w_sp = sb(gm, "w_sp", [8, P])
        prev = sb(gm, "prev", [2, T + 1])
        diff = sb(gm, "diff", [T])
        mixT = hT

        def project_pe(pe):
            for job, m in enumerate(IN_ORDER):
                b = 1 + job % 5
                need_slot(pe, ("in", m))
                if job >= 5:
                    pe.wait_ge(*at("in", "evac", job - 5))
                if 4 <= m < 8:
                    for tt in range(TT):
                        for k in range(KD):
                            pe.wait_ge(*at("hT", k))
                            ins = nc.tensor.matmul(bank(b, tt * P, (tt + 1) * P), hT[:, k, tt * P:(tt + 1) * P],
                                                   tile_w(("in", m), k), start=(k == 0), stop=(k == KD - 1))
                else:
                    for k in range(KD):
                        ins = nc.tensor.matmul(bank(b), tile_w(("in", m), k), hT[:, k, :],
                                               start=(k == 0), stop=(k == KD - 1))
                ins.then_inc(pe_done, 1)
                pe_count.up("in", "mm", job)
                pe_count.mark("free", slot_of[("in", m)])

        def project_dve(dve):
            for i in range(2):
                nc.vector.memset(prev[:, i, 0:1], 0.0).then_inc(dve_done, 1)
                dve.wait_ge(dve_done, dve_count.up("prev_zero"))
            gmlp_norm(dve)
            for i in range(17):
                dve.wait_ge(*at("raw", i))
                nc.vector.tensor_tensor(diff[:, :], prev[:, i % 2, 0:T], prev[:, i % 2, 1:T + 1],
                                        ALU.subtract).then_inc(dve_done, 1)
                dve.wait_ge(dve_done, dve_count.up())
                dst = rkvg[:, i, :] if i < 16 else wdad[:, :]
                nc.vector.scalar_tensor_tensor(out=dst, in0=diff[:, :], scalar=col("mu_b", i),
                                               in1=prev[:, i % 2, 1:T + 1], op0=ALU.mult, op1=ALU.add).then_inc(dve_done, 1)
                dve.wait_ge(dve_done, dve_count.up("shifted", i))

        def gmlp_norm(dve):
            v3 = vT[:, :, :].rearrange("p t (g d) -> p (t g) d", d=HEAD)
            s3 = vsq[:, :, :].rearrange("p t (g d) -> p (t g) d", d=HEAD)
            dve.wait_ge(*at("v_gelu"))
            nc.vector.tensor_reduce(vstat[:, 0, :], v3, AX.X, ALU.add).then_inc(dve_done, 1)
            dve.wait_ge(dve_done, dve_count.up())
            nc.vector.tensor_scalar(vstat[:, 1, :], vstat[:, 0, :], 1.0 / HEAD, None, ALU.mult).then_inc(dve_done, 1)
            dve.wait_ge(dve_done, dve_count.up())
            nc.vector.tensor_tensor(v3, v3, along(vstat[:, 1, :], HEAD), ALU.subtract).then_inc(dve_done, 1)
            dve.wait_ge(dve_done, dve_count.up())
            nc.vector.tensor_tensor(s3, v3, v3, ALU.mult).then_inc(dve_done, 1)
            dve.wait_ge(dve_done, dve_count.up())
            nc.vector.tensor_reduce(vstat[:, 2, :], s3, AX.X, ALU.add).then_inc(dve_done, 1)
            dve.wait_ge(dve_done, dve_count.up("v_squares"))
            dve.wait_ge(*at("v_std"))
            nc.vector.reciprocal(vstat[:, 0, :], vstat[:, 3, :]).then_inc(dve_done, 1)
            dve.wait_ge(dve_done, dve_count.up())
            nc.vector.tensor_tensor(v3, v3, along(vstat[:, 0, :], HEAD), ALU.mult).then_inc(dve_done, 1)
            dve.wait_ge(dve_done, dve_count.up())
            dve.wait_ge(gmlp_loaded, 16 * 4)
            nc.vector.tensor_tensor(vT[:, :, :], vT[:, :, :], over(lnv[:, 0, :], TT), ALU.mult).then_inc(dve_done, 1)
            dve.wait_ge(dve_done, dve_count.up())
            nc.vector.tensor_tensor(vT[:, :, :], vT[:, :, :], over(lnv[:, 1, :], TT), ALU.add).then_inc(dve_done, 1)
            dve.wait_ge(dve_done, dve_count.up("v_norm"))

        def v_std_act(act):
            act.wait_ge(*at("v_squares"))
            nc.scalar.activation(vstat[:, 3, :], vstat[:, 2, :], ACT.Sqrt, bias=eps[:, 0:1],
                                 scale=1.0 / HEAD).then_inc(act_done, 1)
            act.wait_ge(act_done, act_count.up("v_std"))

        def project_act(act):
            for job, m in enumerate(IN_ORDER):
                project_one(act, job, m)
                if job == 11:
                    v_std_act(act)

        def project_one(act, job, m):
            b = 1 + job % 5
            act.wait_ge(*at("in", "mm", job))
            if m < 4:
                nc.scalar.activation(uT[:, m, :], bank(b), ACT.Gelu_apprx_tanh).then_inc(act_done, 1)
                act.wait_ge(act_done, act_count.up("in", "evac", job))
            elif m < 8:
                nc.scalar.activation(vT[:, :, (m - 4) * P:(m - 3) * P],
                                     bank(b).rearrange("p (t d) -> p t d", t=TT),
                                     ACT.Gelu_apprx_tanh).then_inc(act_done, 1)
                act.wait_ge(act_done, act_count.up("in", "evac", job))
                if m == 7:
                    act_count.mark("v_gelu")
            elif m < 12:
                nc.scalar.activation(gT[:, m - 8, :], bank(b), ACT.Silu).then_inc(act_done, 1)
                act.wait_ge(act_done, act_count.up("in", "evac", job))
                act_count.mark("silu_g", m - 8)
            else:
                i = m - 12
                if i >= 2:
                    act.wait_ge(*at("shifted", i - 2))
                else:
                    act.wait_ge(*at("prev_zero"))
                nc.scalar.activation(prev[:, i % 2, 1:T + 1], bank(b), ACT.Copy).then_inc(act_done, 1)
                act.wait_ge(act_done, act_count.up("in", "evac", job))
                act_count.mark("raw", i)

        def mask_pool(pool):
            pool.wait_ge(gmlp_loaded, 16 * 4)
            nc.gpsimd.affine_select(out=w_sp[:, :, :], in_=w_sp[:, :, :], compare_op=ALU.is_ge,
                                    fill=0.0, base=0, pattern=[[0, 8], [1, P]],
                                    channel_multiplier=-1).then_inc(pool_done, 1)
            pool.wait_ge(pool_done, pool_count.up("w_sp"))

        def mixing_pe(pe):
            pe.wait_ge(*at("w_sp"))
            pe.wait_ge(*at("v_norm"))
            for q in range(4):
                if q < 2:
                    pe.wait_ge(*at("in", "evac", W_IN_TILES - 1))
                else:
                    pe.wait_ge(*at("mixed", q - 2))
                for e in range(2):
                    g = 2 * q + e
                    for tt in range(TT):
                        ins = nc.tensor.matmul(psum[64 * e:64 * e + 64, 6 + q % 2, tt * P:(tt + 1) * P],
                                               vT[:, tt, g * HEAD:(g + 1) * HEAD], w_sp[:, g, :],
                                               start=True, stop=True)
                ins.then_inc(pe_done, 1)
                pe_count.up("mixing", q)

        def mixing_dve(dve):
            dve.wait_ge(*at("in", "mm", W_IN_TILES - 1))
            for q in range(4):
                dve.wait_ge(*at("mixing", q))
                m3 = mixT[:, q, :].rearrange("p (t c) -> p t c", t=TT)
                nc.vector.tensor_tensor(m3, bank(6 + q % 2).rearrange("p (t c) -> p t c", t=TT),
                                        over(b_sp[:, q, :], TT), ALU.add).then_inc(dve_done, 1)
                dve.wait_ge(dve_done, dve_count.up("mixed", q))
                nc.vector.tensor_tensor(mixT[:, q, :], mixT[:, q, :], uT[:, q, :], ALU.mult).then_inc(dve_done, 1)
                dve.wait_ge(dve_done, dve_count.up())
                dve.wait_ge(*at("silu_g", q))
                nc.vector.tensor_tensor(mixT[:, q, :], mixT[:, q, :], gT[:, q, :], ALU.mult).then_inc(dve_done, 1)
                dve.wait_ge(dve_done, dve_count.up("mixT", q))

        gm.close()

        rw = ExitStack()
        up = sb(rw, "up", [D_B])
        kscale = sb(rw, "kscale", [2, NPAIR])
        a_cm = sb(rw, "a_cm", [T])
        g_cm = sb(rw, "g_cm", [T])
        k_cm = sb(rw, "k_cm", [T])
        ke_cm = sb(rw, "ke_cm", [T])
        b_rate = sb(rw, "b_rate", [T])
        kk = sb(rw, "kk", [T])
        tmp = sb(rw, "tmp", [T])
        k_new = sb(rw, "k_new", [T])
        b_cm = sb(rw, "b_cm", [T])
        be_cm = sb(rw, "be_cm", [T])
        tm = sb(rw, "tm", [TT, 4, P])
        unit = {}
        for e in range(2):
            for name in ("Z", "ZT", "AT", "U", "RBT", "RKT", "AKT", "W"):
                unit[name, e] = sb(rw, f"{name}_{e}", [TT, P])
            unit["AL", e] = sb(rw, f"AL_{e}", [2, TT, P])
            unit["AKV", e] = sb(rw, f"AKV_{e}", [TT, HEAD])
        r_read = sb(rw, "r_read", [T])
        carry = sb(rw, "carry", [NCHUNK, P])
        inject = sb(rw, "inject", [NCHUNK, HEAD])
        states = sb(rw, "states", [NCHUNK, P])

        def half(e):
            return slice(64 * e, 64 * e + 64)

        def tt4(ap):
            return ap.rearrange("p (t c) -> p t c", t=TT)

        def rwkv_start_dve(dve):
            nc.vector.tensor_scalar(kscale[:, 0, :], col("k_a"), -1.0, 1.0, ALU.mult, ALU.add).then_inc(dve_done, 1)
            dve.wait_ge(dve_done, dve_count.up())
            nc.vector.memset(carry[:, :, :], 0.0).then_inc(dve_done, 1)
            dve.wait_ge(dve_done, dve_count.up())
            nc.vector.memset(states[:, :, :], 0.0).then_inc(dve_done, 1)
            dve.wait_ge(dve_done, dve_count.up("states_zero"))

        def rwkv_start_act(act):
            nc.scalar.activation(wdad[0:64, :], wdad[0:64, :], ACT.Tanh).then_inc(act_done, 1)
            act.wait_ge(act_done, act_count.up("tanh_wd"))

        def rwkv_prep_pe(pe, q):
            if q == 0:
                pe.wait_ge(*at("tanh_wd"))
                pe.wait_ge(gmlp_loaded, 16 * 6)
            cs = slice(q * P, (q + 1) * P)
            if q > 0:
                pe.wait_ge(*at("rw", q - 1, "y_copied"))
                pe.wait_ge(*at("rw", q - 1, "state_added", NCHUNK - 1))
            nc.tensor.matmul(bank(0), up[0:64, cs], wdad[0:64, :], start=True, stop=True).then_inc(pe_done, 1)
            pe_count.up("rw", q, "w_raw")
            nc.tensor.matmul(bank(1), up[64:128, cs], wdad[64:128, :], start=True, stop=True).then_inc(pe_done, 1)
            pe_count.up("rw", q, "a_raw")
            pe.wait_ge(*at("rw", q, "k_sq"))
            nc.tensor.matmul(bank(2), mask("block_ones"), tmp[:, :], start=True, stop=True).then_inc(pe_done, 1)
            pe_count.up("rw", q, "k_ss")
            pe.wait_ge(*at("rw", q, "rk"))
            nc.tensor.matmul(bank(3), mask("block_ones"), tmp[:, :], start=True, stop=True).then_inc(pe_done, 1)
            pe_count.up("rw", q, "rk_sum")
            pe.wait_ge(*at("rw", q, "operands"))
            for tt in range(TT):
                ts = slice(tt * P, (tt + 1) * P)
                for n, src in enumerate((a_cm[:, ts], be_cm[:, ts], ke_cm[:, ts], rkvg[:, 8 + q, ts])):
                    ins = nc.tensor.transpose(bank(4 + tt, n * P, (n + 1) * P), src, mask("ident"))
                ins.then_inc(pe_done, 1)
                pe_count.up("rw", q, "turned", tt)

        def rwkv_prep_act(act, q):
            act.wait_ge(*at("rw", q, "w_raw"))
            if q > 0:
                act.wait_ge(*at("rw", q - 1, "unit_mm"))
            nc.scalar.activation(a_cm[:, :], bank(0), ACT.Sigmoid, bias=col("w0", q)).then_inc(act_done, 1)
            act.wait_ge(act_done, act_count.up("rw", q, "decay_sig"))
            act.wait_ge(*at("rw", q, "a_raw"))
            nc.scalar.activation(b_rate[:, :], bank(1), ACT.Sigmoid, bias=col("a0", q)).then_inc(act_done, 1)
            act.wait_ge(act_done, act_count.up("rw", q, "rate"))
            act.wait_ge(*at("rw", q, "k_ss"))
            nc.scalar.activation(kk[:, :], bank(2), ACT.Sqrt, bias=eps[:, 3:4]).then_inc(act_done, 1)
            act.wait_ge(act_done, act_count.up("rw", q, "k_norm"))
            act.wait_ge(*at("rw", q, "G"))
            nc.scalar.activation(a_cm[:, :], a_cm[:, :], ACT.Exp).then_inc(act_done, 1)
            act.wait_ge(act_done, act_count.up("rw", q, "exp_Gx"))
            nc.scalar.activation(k_cm[:, :], g_cm[:, :], ACT.Exp, scale=-1.0).then_inc(act_done, 1)
            act.wait_ge(act_done, act_count.up("rw", q, "exp_nG"))
            nc.scalar.activation(ke_cm[:, :], ke_cm[:, :], ACT.Exp).then_inc(act_done, 1)
            act.wait_ge(act_done, act_count.up("rw", q, "exp_Ge"))
            nc.scalar.activation(g_cm[:, :], g_cm[:, :], ACT.Exp).then_inc(act_done, 1)
            act.wait_ge(act_done, act_count.up("rw", q, "exp_G"))
            for tt in range(TT):
                act.wait_ge(*at("rw", q, "turned", tt))
                nc.scalar.activation(tm[:, tt, :, :], bank(4 + tt).rearrange("p (n c) -> p n c", n=4),
                                     ACT.Copy).then_inc(act_done, 1)
                act.wait_ge(act_done, act_count.up("rw", q, "tm", tt))

        def rwkv_prep_dve(dve, q):
            v = nc.vector
            r_, k_, v_ = rkvg[:, q, :], rkvg[:, 4 + q, :], rkvg[:, 8 + q, :]
            if q > 0:
                dve.wait_ge(*at("rw", q - 1, "unit_mm"))
            dve.wait_ge(*at("rw", q, "decay_sig"))
            v.tensor_scalar(a_cm[:, :], a_cm[:, :], -math.exp(-0.5), None, ALU.mult).then_inc(dve_done, 1)
            dve.wait_ge(dve_done, dve_count.up())
            v.tensor_tensor_scan(g_cm[:, :], reset, a_cm[:, :], 0.0, ALU.mult, ALU.add).then_inc(dve_done, 1)
            dve.wait_ge(dve_done, dve_count.up())
            v.tensor_tensor(a_cm[:, :], g_cm[:, :], a_cm[:, :], ALU.subtract).then_inc(dve_done, 1)
            dve.wait_ge(dve_done, dve_count.up())
            g3 = g_cm[:, :].rearrange("p (c t) -> p c t", t=CHUNK)
            v.tensor_tensor(ke_cm[:, :].rearrange("p (c t) -> p c t", t=CHUNK),
                            g3[:, :, CHUNK - 1:CHUNK].broadcast_to([P, NCHUNK, CHUNK]), g3,
                            ALU.subtract).then_inc(dve_done, 1)
            dve.wait_ge(dve_done, dve_count.up("rw", q, "G"))
            v.tensor_scalar(k_new[:, :], k_, col("k_k", q), None, ALU.mult).then_inc(dve_done, 1)
            dve.wait_ge(dve_done, dve_count.up())
            v.tensor_tensor(tmp[:, :], k_new[:, :], k_new[:, :], ALU.mult).then_inc(dve_done, 1)
            dve.wait_ge(dve_done, dve_count.up("rw", q, "k_sq"))
            dve.wait_ge(*at("rw", q, "k_norm"))
            v.reciprocal(tmp[:, :], kk[:, :]).then_inc(dve_done, 1)
            dve.wait_ge(dve_done, dve_count.up())
            v.tensor_tensor(kk[:, :], k_new[:, :], tmp[:, :], ALU.mult).then_inc(dve_done, 1)
            dve.wait_ge(dve_done, dve_count.up())
            dve.wait_ge(*at("rw", q, "rate"))
            v.tensor_scalar(k_new[:, :], b_rate[:, :], col("k_a", q), kscale[:, 0, q:q + 1], ALU.mult, ALU.add).then_inc(dve_done, 1)
            dve.wait_ge(dve_done, dve_count.up())
            v.tensor_tensor(k_new[:, :], k_new[:, :], k_, ALU.mult).then_inc(dve_done, 1)
            dve.wait_ge(dve_done, dve_count.up())
            v.scalar_tensor_tensor(out=tmp[:, :], in0=r_, scalar=col("r_k", q), in1=k_new[:, :],
                                   op0=ALU.mult, op1=ALU.mult).then_inc(dve_done, 1)
            dve.wait_ge(dve_done, dve_count.up("rw", q, "rk"))
            v.tensor_tensor(b_rate[:, :], kk[:, :], b_rate[:, :], ALU.mult).then_inc(dve_done, 1)
            dve.wait_ge(dve_done, dve_count.up())
            dve.wait_ge(*at("rw", q, "exp_G"))
            v.scalar_tensor_tensor(out=a_cm[:, :], in0=kk[:, :], scalar=-1.0, in1=a_cm[:, :],
                                   op0=ALU.mult, op1=ALU.mult).then_inc(dve_done, 1)
            dve.wait_ge(dve_done, dve_count.up())
            v.tensor_tensor(b_cm[:, :], b_rate[:, :], k_cm[:, :], ALU.mult).then_inc(dve_done, 1)
            dve.wait_ge(dve_done, dve_count.up())
            v.tensor_tensor(be_cm[:, :], b_rate[:, :], ke_cm[:, :], ALU.mult).then_inc(dve_done, 1)
            dve.wait_ge(dve_done, dve_count.up())
            v.tensor_tensor(k_cm[:, :], k_new[:, :], k_cm[:, :], ALU.mult).then_inc(dve_done, 1)
            dve.wait_ge(dve_done, dve_count.up())
            v.tensor_tensor(ke_cm[:, :], k_new[:, :], ke_cm[:, :], ALU.mult).then_inc(dve_done, 1)
            dve.wait_ge(dve_done, dve_count.up())
            v.tensor_tensor(r_, r_, g_cm[:, :], ALU.mult).then_inc(dve_done, 1)
            dve.wait_ge(dve_done, dve_count.up("rw", q, "operands"))
            dve.wait_ge(*at("rw", q, "rk_sum"))
            v.tensor_tensor(k_, bank(3), v_, ALU.mult).then_inc(dve_done, 1)
            dve.wait_ge(dve_done, dve_count.up("rw", q, "bonus"))

        def rwkv_unit_pe(pe, q):
            r_ = rkvg[:, q, :]
            mm = nc.tensor.matmul

            def products(e, b, lhs, rhs, name, *waits):
                for w in waits:
                    pe.wait_ge(*at(*w))
                for tt in range(TT):
                    ts = slice(tt * P, (tt + 1) * P)
                    ins = mm(bank(b, tt * P, (tt + 1) * P), lhs[half(e), ts], rhs[half(e), ts], start=True, stop=True)
                ins.then_inc(pe_done, 1)
                pe_count.up("rw", q, name, e)

            def turns(e, b, lhs, rhs, name, *waits, out=None, width=P):
                for w in waits:
                    pe.wait_ge(*at(*w))
                for tt in range(TT):
                    o = bank(b, tt * width, (tt + 1) * width) if out is None else out(tt)
                    ins = mm(o, lhs(tt), rhs(tt), start=True, stop=True)
                ins.then_inc(pe_done, 1)
                pe_count.up("rw", q, name, e)

            pe.wait_ge(*at("rw", q, "bonus"))
            pe.wait_ge(*at("rw", q, "tm", TT - 1))
            for e in range(2):
                b = 4 * e
                products(e, b + 0, a_cm, b_cm, "A")
                products(e, b + 1, b_cm, a_cm, "AT")
                products(e, b + 2, b_cm, r_, "RBT")
                products(e, b + 3, k_cm, r_, "RKT")
            for e in range(2):
                products(e, 4 * e, k_cm, a_cm, "AKT", ("rw", q, "Z0", e))
            for level in range(1, LEVELS + 1):
                last = level == LEVELS
                for e in range(2):
                    b = 4 * e
                    Z, ZT, U = unit["Z", e], unit["ZT", e], unit["U", e]
                    AL = unit["AL", e]
                    pe.wait_ge(*at("rw", q, "AT_copied", e))
                    turns(e, b + 1, lambda tt: AL[:, level % 2, tt, :], lambda tt: Z[:, tt, :], ("U", level),
                          ("rw", q, ("AL", level), e), ("rw", q, ("Z", level - 1), e))
                for e in range(2):
                    b = 4 * e
                    Z, ZT, U = unit["Z", e], unit["ZT", e], unit["U", e]
                    waits = [("rw", q, ("U_copied", level), e), ("rw", q, ("ZT", level - 1), e)]
                    if level == 1:
                        waits += [("rw", q, "RBT_masked", e), ("rw", q, "RKT_masked", e)]
                    if not last:
                        turns(e, b + 2, lambda tt: ZT[:, tt, :], lambda tt: U[:, tt, :], ("dZ", level), *waits)
                    turns(e, b + 3, lambda tt: U[:, tt, :], lambda tt: ZT[:, tt, :], ("dZT", level), *waits)
            vt = lambda tt, e: tm[:, tt, 3, half(e)]
            for e in range(2):
                turns(e, 4 * e, lambda tt: unit["AKT", e][:, tt, :], lambda tt: vt(tt, e), "AKV",
                      ("rw", q, "AKT_masked", e), width=HEAD)
            for e in range(2):
                b = 4 * e + 1
                ZT = unit["ZT", e]
                pe.wait_ge(*at("rw", q, "AKV_copied", e))
                pe.wait_ge(*at("rw", q, ("ZT", LEVELS), e))
                for tt in range(TT):
                    mm(bank(b, tt * P, tt * P + HEAD), ZT[:, tt, :], tm[:, tt, 0, half(e)], start=True, stop=True)
                    ins = mm(bank(b, tt * P + HEAD, (tt + 1) * P), ZT[:, tt, :], unit["AKV", e][:, tt, :],
                             start=True, stop=True)
                ins.then_inc(pe_done, 1)
                pe_count.up("rw", q, "W", e)
            for e in range(2):
                W, RBT, RKT = unit["W", e], unit["RBT", e], unit["RKT", e]
                turns(e, 2, lambda tt: W[:, tt, 0:HEAD], lambda tt: RBT[:, tt, :], "r_read",
                      ("rw", q, "W_copied", e), ("rw", q, ("Z", LEVELS - 1), 0), ("rw", q, ("Z", LEVELS - 1), 1),
                      out=lambda tt: psum[half(e), 2, tt * P:(tt + 1) * P])
                for tt in range(TT):
                    o = psum[half(e), 3, tt * P:(tt + 1) * P]
                    mm(o, W[:, tt, HEAD:P], RBT[:, tt, :], start=(tt == 0), stop=False, skip_group_check=True)
                    mm(o, vt(tt, e), RKT[:, tt, :], start=False, stop=False, skip_group_check=True)
                for odd in range(2):
                    rows = half(odd)
                    for tt in range(TT):
                        o = psum[half(e), 4 * odd, tt * HEAD:(tt + 1) * HEAD]
                        mm(o, W[rows, tt, 0:HEAD], tm[rows, tt, 1, half(e)], start=True, stop=True)
                        o = psum[half(e), 4 * odd, 256 + tt * HEAD:256 + (tt + 1) * HEAD]
                        mm(o, tm[rows, tt, 1, half(e)], W[rows, tt, HEAD:P], start=True, stop=False)
                        ins = mm(o, tm[rows, tt, 2, half(e)], tm[rows, tt, 3, half(e)], start=False, stop=True)
                ins.then_inc(pe_done, 1)
                pe_count.up("rw", q, "chunks", e)
            pe_count.mark("rw", q, "unit_mm")
            for c in range(NCHUNK):
                if c > 0:
                    pe.wait_ge(*at("rw", q, "state_added", c))
                else:
                    pe.wait_ge(*at("states_zero"))
                    pe.wait_ge(*at("rw", q, "r_read_copied"))
                ins = mm(bank(3, c * CHUNK, (c + 1) * CHUNK), states[:, c, :], r_read[:, c * CHUNK:(c + 1) * CHUNK],
                         start=False, stop=(c == NCHUNK - 1), skip_group_check=True)
                if c == NCHUNK - 1:
                    ins.then_inc(pe_done, 1)
                    pe_count.up("rw", q, "y")
                if c < NCHUNK - 1:
                    pe.wait_ge(*at("rw", q, "carry", c))
                    o = bank(7, c * HEAD, (c + 1) * HEAD)
                    for e in range(2):
                        ins = mm(o, carry[:, c, :], states[:, c, e * HEAD:(e + 1) * HEAD],
                                 start=(e == 0), stop=(e == 1))
                    ins.then_inc(pe_done, 1)
                    pe_count.up("rw", q, "state_mm", c)

        def rwkv_unit_act(act, q):
            for e in range(2):
                act.wait_ge(*at("rw", q, "AT", e))
                nc.scalar.activation(unit["AT", e][:, :, :], tt4(bank(4 * e + 1)), ACT.Copy).then_inc(act_done, 1)
                act.wait_ge(act_done, act_count.up("rw", q, "AT_copied", e))
            for level in range(1, LEVELS + 1):
                for e in range(2):
                    act.wait_ge(*at("rw", q, ("U", level), e))
                    nc.scalar.activation(unit["U", e][:, :, :], tt4(bank(4 * e + 1)), ACT.Copy).then_inc(act_done, 1)
                    act.wait_ge(act_done, act_count.up("rw", q, ("U_copied", level), e))
            for e in range(2):
                act.wait_ge(*at("rw", q, "AKV", e))
                nc.scalar.activation(unit["AKV", e][:, :, :], tt4(bank(4 * e, 0, 256)), ACT.Copy).then_inc(act_done, 1)
                act.wait_ge(act_done, act_count.up("rw", q, "AKV_copied", e))
            for e in range(2):
                act.wait_ge(*at("rw", q, "W", e))
                nc.scalar.activation(unit["W", e][:, :, :], tt4(bank(4 * e + 1)), ACT.Copy).then_inc(act_done, 1)
                act.wait_ge(act_done, act_count.up("rw", q, "W_copied", e))
            act.wait_ge(*at("rw", q, "y"))
            nc.scalar.activation(rkvg[:, q, :], bank(3), ACT.Copy).then_inc(act_done, 1)
            act.wait_ge(act_done, act_count.up("rw", q, "y_copied"))

        def rwkv_unit_pool(pool, q):
            for level in range(1, LEVELS + 1):
                for e in range(2):
                    pool.wait_ge(*at("rw", q, "AT_copied", e))
                    if level > 2:
                        pool.wait_ge(*at("rw", q, ("U", level - 2), e))
                    elif q > 0:
                        pool.wait_ge(*at("rw", q - 1, "unit_mm"))
                    nc.gpsimd.tensor_tensor(unit["AL", e][:, level % 2, :, :], unit["AT", e][:, :, :],
                                            over(mask(f"level{level}"), TT), ALU.mult).then_inc(pool_done, 1)
                    pool.wait_ge(pool_done, pool_count.up("rw", q, ("AL", level), e))

        def rwkv_unit_dve(dve, q):
            v = nc.vector
            for e in range(2):
                b = 4 * e
                Z, ZT = unit["Z", e], unit["ZT", e]
                dve.wait_ge(*at("rw", q, "A", e))
                v.tensor_tensor(Z[:, :, :], tt4(bank(b)), over(mask("diag2_lower"), TT), ALU.mult).then_inc(dve_done, 1)
                dve.wait_ge(dve_done, dve_count.up())
                v.tensor_tensor(Z[:, :, :], Z[:, :, :], over(mask("ident"), TT), ALU.add).then_inc(dve_done, 1)
                dve.wait_ge(dve_done, dve_count.up("rw", q, "Z0", e))
                dve_count.mark("rw", q, ("Z", 0), e)
                dve.wait_ge(*at("rw", q, "AT_copied", e))
                v.tensor_tensor(ZT[:, :, :], unit["AT", e][:, :, :], over(mask("diag2_upper"), TT), ALU.mult).then_inc(dve_done, 1)
                dve.wait_ge(dve_done, dve_count.up())
                v.tensor_tensor(ZT[:, :, :], ZT[:, :, :], over(mask("ident"), TT), ALU.add).then_inc(dve_done, 1)
                dve.wait_ge(dve_done, dve_count.up("rw", q, ("ZT", 0), e))
            for e in range(2):
                b = 4 * e
                dve.wait_ge(*at("rw", q, "RKT", e))
                v.tensor_tensor(unit["RBT", e][:, :, :], tt4(bank(b + 2)), over(mask("incl_upper"), TT),
                                ALU.mult).then_inc(dve_done, 1)
                dve.wait_ge(dve_done, dve_count.up("rw", q, "RBT_masked", e))
                v.tensor_tensor(unit["RKT", e][:, :, :], tt4(bank(b + 3)), over(mask("incl_upper"), TT),
                                ALU.mult).then_inc(dve_done, 1)
                dve.wait_ge(dve_done, dve_count.up("rw", q, "RKT_masked", e))
                dve.wait_ge(*at("rw", q, "AKT", e))
                v.tensor_tensor(unit["AKT", e][:, :, :], tt4(bank(b)), over(mask("strict_upper"), TT),
                                ALU.mult).then_inc(dve_done, 1)
                dve.wait_ge(dve_done, dve_count.up("rw", q, "AKT_masked", e))
            for level in range(1, LEVELS + 1):
                for e in range(2):
                    b = 4 * e
                    Z, ZT = unit["Z", e], unit["ZT", e]
                    dve.wait_ge(*at("rw", q, ("dZT", level), e))
                    if level < LEVELS:
                        v.tensor_tensor(Z[:, :, :], tt4(bank(b + 2)), Z[:, :, :], ALU.add).then_inc(dve_done, 1)
                        dve.wait_ge(dve_done, dve_count.up("rw", q, ("Z", level), e))
                    v.tensor_tensor(ZT[:, :, :], tt4(bank(b + 3)), ZT[:, :, :], ALU.add).then_inc(dve_done, 1)
                    dve.wait_ge(dve_done, dve_count.up("rw", q, ("ZT", level), e))
            dve.wait_ge(*at("rw", q, "r_read", 1))
            v.tensor_tensor(r_read[:, :], bank(2), rkvg[:, q, :], ALU.add).then_inc(dve_done, 1)
            dve.wait_ge(dve_done, dve_count.up("rw", q, "r_read_copied"))
            dve.wait_ge(*at("rw", q, "chunks", 1))
            ends = g_cm[:, :].rearrange("p (c t) -> p c t", t=CHUNK)
            for c in range(NCHUNK):
                src = bank(4 * (c % 2), (c // 2) * HEAD, (c // 2 + 1) * HEAD)
                for e in range(2):
                    v.scalar_tensor_tensor(out=carry[half(e), c, half(e)], in0=mask("ident")[half(e), half(e)],
                                           scalar=ends[half(e), c, CHUNK - 1:CHUNK], in1=src[half(e), :],
                                           op0=ALU.mult, op1=ALU.add).then_inc(dve_done, 1)
                    dve.wait_ge(dve_done, dve_count.up("rw", q, "carry", c))
                if c == 0:
                    for odd in range(2):
                        v.tensor_copy(inject[:, odd:NCHUNK:2, :], tt4(bank(4 * odd, 256, 512))).then_inc(dve_done, 1)
                        dve.wait_ge(dve_done, dve_count.up())
            for c in range(NCHUNK - 1):
                dve.wait_ge(*at("rw", q, "state_mm", c))
                for e in range(2):
                    v.tensor_tensor(states[half(e), c + 1, half(e)], bank(7, c * HEAD, (c + 1) * HEAD)[half(e), :],
                                    inject[half(e), c, :], ALU.add).then_inc(dve_done, 1)
                    dve.wait_ge(dve_done, dve_count.up("rw", q, "state_added", c + 1))

        def group_norm_pe(pe):
            for q in range(NPAIR):
                pe.wait_ge(*at("rw", q, "y_copied"))
                nc.tensor.matmul(bank(2 * (q % 2)), mask("block_ones"), rkvg[:, q, :], start=True, stop=True).then_inc(pe_done, 1)
                pe_count.up("gn", q, "sum")
                pe.wait_ge(*at("gn", q, "sq"))
                nc.tensor.matmul(bank(2 * (q % 2) + 1), mask("block_ones"), tmp[:, :], start=True, stop=True).then_inc(pe_done, 1)
                pe_count.up("gn", q, "ss")

        def group_norm_act(act):
            for q in range(NPAIR):
                act.wait_ge(*at("gn", q, "ss"))
                nc.scalar.activation(kk[:, :], bank(2 * (q % 2) + 1), ACT.Sqrt, bias=eps[:, 1:2], scale=1.0 / HEAD).then_inc(act_done, 1)
                act.wait_ge(act_done, act_count.up("gn", q, "std"))
            for q in range(NPAIR):
                nc.scalar.activation(rkvg[:, 12 + q, :], rkvg[:, 12 + q, :], ACT.Silu).then_inc(act_done, 1)
                act.wait_ge(act_done, act_count.up("gn", q, "gate"))

        def group_norm_dve(dve):
            v = nc.vector
            for q in range(NPAIR):
                y = rkvg[:, q, :]
                dve.wait_ge(*at("gn", q, "sum"))
                v.scalar_tensor_tensor(out=y, in0=bank(2 * (q % 2)), scalar=-1.0 / HEAD, in1=y, op0=ALU.mult, op1=ALU.add).then_inc(dve_done, 1)
                dve.wait_ge(dve_done, dve_count.up())
                v.tensor_tensor(tmp[:, :], y, y, ALU.mult).then_inc(dve_done, 1)
                dve.wait_ge(dve_done, dve_count.up("gn", q, "sq"))
                dve.wait_ge(*at("gn", q, "std"))
                v.reciprocal(k_new[:, :], kk[:, :]).then_inc(dve_done, 1)
                dve.wait_ge(dve_done, dve_count.up())
                v.tensor_tensor(y, y, k_new[:, :], ALU.mult).then_inc(dve_done, 1)
                dve.wait_ge(dve_done, dve_count.up("gn", q, "normed"))
                v.tensor_scalar(y, y, col("gn_g", q), col("gn_b", q), ALU.mult, ALU.add).then_inc(dve_done, 1)
                dve.wait_ge(dve_done, dve_count.up())
                v.tensor_tensor(y, y, rkvg[:, 4 + q, :], ALU.add).then_inc(dve_done, 1)
                dve.wait_ge(dve_done, dve_count.up())
            for q in range(NPAIR):
                dve.wait_ge(*at("gn", q, "gate"))
                v.tensor_tensor(mixT[:, 4 + q, :], rkvg[:, q, :], rkvg[:, 12 + q, :], ALU.mult).then_inc(dve_done, 1)
                dve.wait_ge(dve_done, dve_count.up("mixT", 4 + q))

        rw.close()

        o1 = ExitStack()
        sq = sb(o1, "sq", [KD, T])
        stat = sb(o1, "stat", [2, T])

        def out_pe(pe):
            for m in range(KD):
                need_slot(pe, ("out", m))
                if m >= 4:
                    pe.wait_ge(*at("residual", m - 4))
                for k in range(KD):
                    ins = nc.tensor.matmul(bank(m % 4), tile_w(("out", m), k), mixT[:, k, :], start=(k == 0), stop=(k == KD - 1))
                ins.then_inc(pe_done, 1)
                pe_count.up("free", slot_of[("out", m)])
                pe_count.mark("out", m)

        def out_dve(dve):
            for m in range(KD):
                dve.wait_ge(*at("out", m))
                nc.vector.tensor_scalar(xT[:, m, :], xT[:, m, :], ALPHA_1, None, ALU.mult).then_inc(dve_done, 1)
                dve.wait_ge(dve_done, dve_count.up())
                nc.vector.scalar_tensor_tensor(out=xT[:, m, :], in0=bank(m % 4), scalar=ada[:, 2 * KD + m:2 * KD + m + 1],
                                               in1=xT[:, m, :], op0=ALU.mult, op1=ALU.add).then_inc(dve_done, 1)
                dve.wait_ge(dve_done, dve_count.up("residual", m))
                dve_count.mark("ln1", "z", m)

        ln1_pe, ln1_act, ln1_dve = layer_norm_cm("ln1", xT, T, sq, stat, lambda k: col("ln_g", k), lambda k: col("ln_b", k), eps[:, 0:1],
                            xT, lambda t, k: t[:, k, :])
        o1.close()
        first.close()

        def both(b):
            return flat((b + 1) * BANK - CTX, (b + 1) * BANK + T)

        def parts_of(b):
            return [(flat((b + 1) * BANK - CTX, (b + 1) * BANK), 0, CTX), (flat((b + 1) * BANK, (b + 1) * BANK + T), CTX, T)]

        layers = ExitStack()
        ctxT = sb(layers, "ctxT", [KD, CTX])
        mod2 = misc[:, 0:6 * KD].rearrange("p (i v) -> p i v", v=2)
        vec2 = misc[:, 6 * KD:8 * KD].rearrange("p (i v) -> p i v", v=2)

        def mod2_act(act, name):
            nc.scalar.activation(vec2[:, :, 0], col("c_ctx_2"), ACT.Silu).then_inc(act_done, 1)
            act.wait_ge(act_done, act_count.up())
            nc.scalar.activation(vec2[:, :, 1], col("c_2"), ACT.Silu).then_inc(act_done, 1)
            act.wait_ge(act_done, act_count.up(name, "vec"))

        def mod2_dve(dve, name, b_name):
            dve.wait_ge(*at(name, "sums"))
            nc.vector.tensor_tensor(mod2, bank(0, 0, 6 * KD).rearrange("p (i v) -> p i v", v=2),
                                    along(col(b_name), 2), ALU.add).then_inc(dve_done, 1)
            dve.wait_ge(dve_done, dve_count.up())
            nc.vector.tensor_scalar(mod2[:, KD:2 * KD, :], mod2[:, KD:2 * KD, :], 1.0, None, ALU.add).then_inc(dve_done, 1)
            dve.wait_ge(dve_done, dve_count.up())


        ml = ExitStack()
        h2 = sb(ml, "h2", [KD, TC])
        qn = sb(ml, "qn", [2, TC])
        ckv = sb(ml, "ckv", [TC])
        ckv_tm = sb(ml, "ckv_tm", [6, P])
        kr = sb(ml, "kr", [TC])
        gate2 = sb(ml, "gate2", [KE, TC])
        q_nope = sb(ml, "q_nope", [TC])
        q_abs = sb(ml, "q_abs", [2, TC])
        q_raw = sb(ml, "q_raw", [2, TC])
        q_pos = sb(ml, "q_pos", [2, T])
        o_lat = sb(ml, "o_lat", [TC])
        prob = sb(ml, "prob", [2, TC])
        pt_ctx = sb(ml, "pt_ctx", [2, CTX])
        pt_lat = sb(ml, "pt_lat", [6, T])
        sm = sb(ml, "sm", [2, 4])
        sq3, rms = q_abs, q_raw

        def mla_h_dve(dve):
            dve.wait_ge(ctx_loaded, 16)
            for k in range(KD):
                nc.vector.tensor_scalar(h2[:, k, 0:CTX], ctxT[:, k, :], mod2[:, KD + k, 0:1], mod2[:, k, 0:1],
                                        ALU.mult, ALU.add).then_inc(dve_done, 1)
                dve.wait_ge(dve_done, dve_count.up())
                nc.vector.tensor_scalar(h2[:, k, CTX:TC], xT[:, k, :], mod2[:, KD + k, 1:2], mod2[:, k, 1:2],
                                        ALU.mult, ALU.add).then_inc(dve_done, 1)
                dve.wait_ge(dve_done, dve_count.up("h2", k))

        def mla_in_pe(pe):
            for m in range(20):
                b = 2 * (m % 3)
                need_slot(pe, ("mla_in", m))
                if m >= 3:
                    pe.wait_ge(*at("mla_in", "evac", m - 3))
                for k in range(KD):
                    pe.wait_ge(*at("h2", k))
                for o, a, n in parts_of(b):
                    for k in range(KD):
                        ins = nc.tensor.matmul(o, tile_w(("mla_in", m), k), h2[:, k, a:a + n],
                                               start=(k == 0), stop=(k == KD - 1))
                ins.then_inc(pe_done, 1)
                pe_count.up("mla_in", "mm", m)
                pe_count.mark("free", slot_of[("mla_in", m)])
                if m == 6:
                    pe.wait_ge(*at("kv_sq"))
                    for o, a, n in parts_of(6):
                        ins = nc.tensor.matmul(o, mask("ones"), sq3[:, 0, a:a + n], start=True, stop=True)
                    ins.then_inc(pe_done, 1)
                    pe_count.up("kv_ss")
                if m == 9:
                    pe.wait_ge(*at("q_sq", 1))
                    pe.wait_ge(*at("kv_std"))
                    for o, a, n in parts_of(6):
                        for i in range(2):
                            ins = nc.tensor.matmul(o, mask("ones"), (sq3[:, 1, a:a + n], h2q[:, a:a + n])[i],
                                                   start=(i == 0), stop=(i == 1))
                    ins.then_inc(pe_done, 1)
                    pe_count.up("q_ss")
                if m == 12:
                    pe.wait_ge(*at("kr_rotated"))
                    pe.wait_ge(*at("q_std"))
                    nc.tensor.matmul(bank(6), mask("dup"), q_pos[:, 0, :], start=True, stop=True).then_inc(pe_done, 1)
                    pe_count.up("kr_sum")
                if m == 15:
                    pe.wait_ge(*at("ckv_normed"))
                    pe.wait_ge(*at("kr_copied"))
                    for i in range(6):
                        ins = nc.tensor.transpose(bank(6 + i // 3, (i % 3) * P, (i % 3 + 1) * P),
                                                  ckv[:, i * P:(i + 1) * P], mask("ident"))
                    ins.then_inc(pe_done, 1)
                    pe_count.up("ckv_turned")

        h2q = prob[:, 0, :]

        def mla_in_act(act):
            for m in range(20):
                act.wait_ge(*at("mla_in", "mm", m))
                src = both(2 * (m % 3))
                if m < 2:
                    nc.scalar.activation(qn[:, m, :], src, ACT.Copy).then_inc(act_done, 1)
                    act.wait_ge(act_done, act_count.up("mla_in", "evac", m))
                elif m == 2:
                    nc.scalar.activation(ckv[:, :], src, ACT.Copy).then_inc(act_done, 1)
                    act.wait_ge(act_done, act_count.up("mla_in", "evac", m))
                elif m == 3:
                    nc.scalar.activation(q_nope[:, :], src, ACT.Copy).then_inc(act_done, 1)
                    act.wait_ge(act_done, act_count.up("mla_in", "evac", m))
                    nc.scalar.activation(sq3[:, 0, :], ckv[:, :], ACT.Square).then_inc(act_done, 1)
                    act.wait_ge(act_done, act_count.up("kv_sq"))
                    nc.scalar.activation(sq3[:, 1, :], qn[:, 0, :], ACT.Square).then_inc(act_done, 1)
                    act.wait_ge(act_done, act_count.up("q_sq", 0))
                    nc.scalar.activation(h2q, qn[:, 1, :], ACT.Square).then_inc(act_done, 1)
                    act.wait_ge(act_done, act_count.up("q_sq", 1))
                else:
                    nc.scalar.activation(gate2[:, m - 4, :], src, ACT.Silu).then_inc(act_done, 1)
                    act.wait_ge(act_done, act_count.up("mla_in", "evac", m))
                if m == 9:
                    act.wait_ge(*at("kv_ss"))
                    nc.scalar.activation(rms[:, 0, :], both(6), ACT.Sqrt, bias=eps[:, 2:3], scale=1.0 / KV_RANK).then_inc(act_done, 1)
                    act.wait_ge(act_done, act_count.up("kv_std"))
                    act.wait_ge(*at("q_ss"))
                    nc.scalar.activation(rms[:, 1, :], both(6), ACT.Sqrt, bias=eps[:, 2:3], scale=1.0 / Q_RANK).then_inc(act_done, 1)
                    act.wait_ge(act_done, act_count.up("q_std"))

        def mla_in_dve(dve):
            v = nc.vector
            dve.wait_ge(*at("mla_in", "evac", 3))
            v.tensor_tensor(q_pos[:, 0, :], q_nope[:, CTX:TC], rope, ALU.mult).then_inc(dve_done, 1)
            dve.wait_ge(dve_done, dve_count.up("kr_rotated"))
            v.tensor_copy(kr[0:64, 0:CTX], q_nope[0:64, 0:CTX]).then_inc(dve_done, 1)
            dve.wait_ge(dve_done, dve_count.up())
            v.memset(kr[64:128, 0:CTX], 0.0).then_inc(dve_done, 1)
            dve.wait_ge(dve_done, dve_count.up())
            dve.wait_ge(*at("kv_std"))
            v.reciprocal(o_lat[:, :], rms[:, 0, :]).then_inc(dve_done, 1)
            dve.wait_ge(dve_done, dve_count.up())
            v.scalar_tensor_tensor(out=ckv[:, :], in0=ckv[:, :], scalar=col("kv_norm", 0), in1=o_lat[:, :],
                                   op0=ALU.mult, op1=ALU.mult).then_inc(dve_done, 1)
            dve.wait_ge(dve_done, dve_count.up("ckv_normed"))
            dve.wait_ge(*at("q_std"))
            v.reciprocal(o_lat[:, :], rms[:, 1, :]).then_inc(dve_done, 1)
            dve.wait_ge(dve_done, dve_count.up())
            for i in range(2):
                v.scalar_tensor_tensor(out=qn[:, i, :], in0=qn[:, i, :], scalar=col("q_norm", i), in1=o_lat[:, :],
                                       op0=ALU.mult, op1=ALU.mult).then_inc(dve_done, 1)
                dve.wait_ge(dve_done, dve_count.up("qn"))
            dve.wait_ge(*at("kr_sum"))
            v.tensor_copy(kr[:, CTX:TC], bank(6)).then_inc(dve_done, 1)
            dve.wait_ge(dve_done, dve_count.up("kr_copied"))
            dve.wait_ge(*at("ckv_turned"))
            v.tensor_copy(ckv_tm[:, :, :].rearrange("p (b k) c -> p b k c", b=2),
                          psum[:, 6:8, 0:3 * P].rearrange("p b (k c) -> p b k c", k=3)).then_inc(dve_done, 1)
            dve.wait_ge(dve_done, dve_count.up("ckv_tm"))


        UNITS = 6

        def queries(h, u):
            if u < 2:
                return slice(u * P, (u + 1) * P), q_raw[:, h % 2, u * P:(u + 1) * P]
            return slice(u * P, (u + 1) * P), q_pos[:, h % 2, (u - 2) * P:(u - 1) * P]

        def head_pe(pe, h):
            mm = nc.tensor.matmul

            def scores(u):
                n = UNITS * h + u
                b = 2 + 2 * (n % 2)
                if n >= 2:
                    pe.wait_ge(*at("exp", n - 2))
                pe.wait_ge(*at("q_pos", h))
                pe.wait_ge(*at("q_abs", h))
                cs, rp = queries(h, u)
                keys = parts_of(b)[:1] if u < 2 else parts_of(b)
                for i, (o, a, m) in enumerate(keys):
                    mm(o, q_abs[:, h % 2, cs], ckv[:, a:a + m], start=True, stop=False)
                    r = q_raw[:, h % 2, cs] if i == 0 else rp
                    ins = mm(o, r, kr[:, a:a + m], start=False, stop=True)
                ins.then_inc(pe_done, 1)
                pe_count.up("scores", n)

            def turn(n):
                u = n % UNITS
                if n >= 1:
                    pe.wait_ge(*at("pt", n - 1))
                pe.wait_ge(*at("normed", n))
                for k in range(2 if u < 2 else 6):
                    ins = nc.tensor.transpose(bank(6 + k // 3, (k % 3) * P, (k % 3 + 1) * P),
                                              prob[:, n % 2, k * P:(k + 1) * P], mask("ident"))
                ins.then_inc(pe_done, 1)
                pe_count.up("turned", n)

            def values(hh):
                pe.wait_ge(*at("pt", UNITS * hh + 5))
                if hh + 1 < HEADS:
                    pe.wait_ge(*at("q_raw", hh + 1))
                for o, pt, kt in ((both(0)[:, 0:CTX], pt_ctx, 2), (bank(1), pt_lat, 6)):
                    for k in range(kt):
                        ins = mm(o, ckv_tm[:, k, :], pt[:, k, :], start=(k == 0), stop=(k == kt - 1))
                ins.then_inc(pe_done, 1)
                pe_count.up("values", hh)

            def up_values(hh):
                pe.wait_ge(*at("o_lat", hh))
                for o, a, n in parts_of(0):
                    ins = mm(o, slot(("head", hh))[:, 640:768], o_lat[:, a:a + n], start=True, stop=True)
                ins.then_inc(pe_done, 1)
                pe_count.up("up_values", hh)
                pe_count.mark("free", slot_of[("head", hh)])

            def project(hh, what):
                if hh >= HEADS:
                    return
                w = slot(("head", hh))
                if what == "nope":
                    need_slot(pe, ("head", hh))
                    if hh == 0:
                        pe.wait_ge(*at("qn"))
                        pe.wait_ge(*at("ckv_tm"))
                        pe.wait_ge(*at("mla_in", "evac", 19))
                    if hh >= 2:
                        pe.wait_ge(*at("gated", hh - 2))
                if what == "abs":
                    pe.wait_ge(*at("q_nope", hh))
                if what == "rope":
                    pe.wait_ge(*at("q_abs", hh))
                for o, a, n in parts_of(0):
                    if what == "abs":
                        ins = mm(o, w[:, 512:640], q_nope[:, a:a + n], start=True, stop=True)
                    else:
                        c = 0 if what == "nope" else P
                        for k in range(2):
                            ins = mm(o, w[:, k * 256 + c:k * 256 + c + P], qn[:, k, a:a + n], start=(k == 0), stop=(k == 1))
                ins.then_inc(pe_done, 1)
                pe_count.up("proj", what, hh)

            if h < 0:
                for what in ("nope", "abs", "rope"):
                    project(0, what)
                return
            if h < HEADS:
                scores(0)
            if h > 0:
                turn(UNITS * h - 1)
                values(h - 1)
            if h == HEADS:
                up_values(h - 1)
                return
            scores(1)
            turn(UNITS * h)
            scores(2)
            turn(UNITS * h + 1)
            if h > 0:
                up_values(h - 1)
            scores(3)
            turn(UNITS * h + 2)
            if h > 0 and h + 1 < HEADS:
                pe.wait_ge(*at("gated", h - 1))
            project(h + 1, "nope")
            scores(4)
            turn(UNITS * h + 3)
            project(h + 1, "abs")
            scores(5)
            turn(UNITS * h + 4)
            project(h + 1, "rope")

        def softmax_dve(dve, n):
            v = nc.vector
            b = 2 + 2 * (n % 2)
            u = n % UNITS
            keys = CTX if u < 2 else TC
            dve.wait_ge(*at("scores", n))
            v.tensor_reduce(sm[:, n % 2, 0:1], both(b)[:, 0:keys], AX.X, ALU.max).then_inc(dve_done, 1)
            dve.wait_ge(dve_done, dve_count.up())
            v.tensor_scalar(sm[:, n % 2, 1:2], sm[:, n % 2, 0:1], -SOFTMAX_SCALE, None, ALU.mult).then_inc(dve_done, 1)
            dve.wait_ge(dve_done, dve_count.up("max", n))

        def normalize_dve(dve, n):
            v = nc.vector
            keys = CTX if n % UNITS < 2 else TC
            dve.wait_ge(*at("exp", n))
            v.reciprocal(sm[:, n % 2, 3:4], sm[:, n % 2, 2:3]).then_inc(dve_done, 1)
            dve.wait_ge(dve_done, dve_count.up())
            v.tensor_scalar(prob[:, n % 2, 0:keys], prob[:, n % 2, 0:keys], sm[:, n % 2, 3:4], None, ALU.mult).then_inc(dve_done, 1)
            dve.wait_ge(dve_done, dve_count.up("normed", n))

        def exp_act(act, n):
            b = 2 + 2 * (n % 2)
            keys = CTX if n % UNITS < 2 else TC
            act.wait_ge(*at("max", n))
            if n >= 2:
                act.wait_ge(*at("turned", n - 2))
            nc.scalar.activation(prob[:, n % 2, 0:keys], both(b)[:, 0:keys], ACT.Exp, bias=sm[:, n % 2, 1:2],
                                 scale=SOFTMAX_SCALE, accum_out=sm[:, n % 2, 2:3]).then_inc(act_done, 1)
            act.wait_ge(act_done, act_count.up("exp", n))

        def pt_act(act, n):
            u = n % UNITS
            act.wait_ge(*at("turned", n))
            if u == 0 and n > 0:
                act.wait_ge(*at("values", n // UNITS - 1))
            if u < 2:
                nc.scalar.activation(pt_ctx[:, :, u * P:(u + 1) * P],
                                     bank(6, 0, 2 * P).rearrange("p (k c) -> p k c", k=2), ACT.Copy).then_inc(act_done, 1)
                act.wait_ge(act_done, act_count.up("pt", n))
            else:
                dst = pt_lat[:, :, (u - 2) * P:(u - 1) * P].rearrange("p (b k) c -> p b k c", b=2)
                nc.scalar.activation(dst, psum[:, 6:8, 0:3 * P].rearrange("p b (k c) -> p b k c", k=3),
                                     ACT.Copy).then_inc(act_done, 1)
                act.wait_ge(act_done, act_count.up("pt", n))

        def proj_act(act, what, h):
            if h >= HEADS:
                return
            act.wait_ge(*at("proj", what, h))
            if what == "nope":
                nc.scalar.activation(q_nope[:, :], both(0), ACT.Copy).then_inc(act_done, 1)
                act.wait_ge(act_done, act_count.up("q_nope", h))
            elif what == "abs":
                nc.scalar.activation(q_abs[:, h % 2, :], both(0), ACT.Copy).then_inc(act_done, 1)
                act.wait_ge(act_done, act_count.up("q_abs", h))
            else:
                nc.scalar.activation(q_raw[:, h % 2, :], both(0), ACT.Copy).then_inc(act_done, 1)
                act.wait_ge(act_done, act_count.up("q_raw", h))

        def head_act(act, h):
            if h < 0:
                for what in ("nope", "abs", "rope"):
                    proj_act(act, what, 0)
                return
            if h == HEADS:
                pt_act(act, UNITS * h - 1)
                act.wait_ge(*at("values", h - 1))
                nc.scalar.activation(o_lat[:, :], both(0), ACT.Copy).then_inc(act_done, 1)
                act.wait_ge(act_done, act_count.up("o_lat", h - 1))
                return
            for u in range(UNITS):
                n = UNITS * h + u
                exp_act(act, n)
                if n > 0:
                    pt_act(act, n - 1)
                if u == 0 and h > 0:
                    act.wait_ge(*at("values", h - 1))
                    nc.scalar.activation(o_lat[:, :], both(0), ACT.Copy).then_inc(act_done, 1)
                    act.wait_ge(act_done, act_count.up("o_lat", h - 1))
                if u >= 3:
                    proj_act(act, ("nope", "abs", "rope")[u - 3], h + 1)

        def head_dve(dve, h):
            def q_pos_of(hh):
                dve.wait_ge(*at("q_raw", hh))
                nc.vector.tensor_tensor(q_pos[:, hh % 2, :], q_raw[:, hh % 2, CTX:TC], rope, ALU.mult).then_inc(dve_done, 1)
                dve.wait_ge(dve_done, dve_count.up("q_pos", hh))

            def gated(hh):
                dve.wait_ge(*at("up_values", hh))
                nc.vector.tensor_tensor(gate2[:, hh, :], both(0), gate2[:, hh, :], ALU.mult).then_inc(dve_done, 1)
                dve.wait_ge(dve_done, dve_count.up("gated", hh))

            if h < 0:
                q_pos_of(0)
                return
            if h == HEADS:
                gated(h - 1)
                return
            for u in range(UNITS):
                n = UNITS * h + u
                softmax_dve(dve, n)
                if u == 3 and h > 0:
                    gated(h - 1)
                normalize_dve(dve, n)
            if h + 1 < HEADS:
                q_pos_of(h + 1)

        def mla_out_pe(pe):
            for m in range(KD):
                b = 2 * (m % 2)
                for i in range(2):
                    need_slot(pe, ("mla_out", 2 * m + i))
                if m >= 2:
                    pe.wait_ge(*at("residual2", m - 2))
                for o, a, n in parts_of(b):
                    for k in range(KE):
                        ins = nc.tensor.matmul(o, tile_w(("mla_out", 2 * m + k // KD), k % KD), gate2[:, k, a:a + n],
                                               start=(k == 0), stop=(k == KE - 1))
                ins.then_inc(pe_done, 1)
                pe_count.up("mla_out", m)
                for i in range(2):
                    pe_count.mark("free", slot_of[("mla_out", 2 * m + i)])

        def mla_out_dve(dve):
            v = nc.vector
            for m in range(KD):
                dve.wait_ge(*at("mla_out", m))
                for i, (src, (o, a, n)) in enumerate(zip((ctxT, xT), parts_of(2 * (m % 2)))):
                    v.tensor_scalar(h2[:, m, a:a + n], src[:, m, :], ALPHA_2, None, ALU.mult).then_inc(dve_done, 1)
                    dve.wait_ge(dve_done, dve_count.up())
                    v.scalar_tensor_tensor(out=h2[:, m, a:a + n], in0=o, scalar=mod2[:, 2 * KD + m, i:i + 1],
                                           in1=h2[:, m, a:a + n], op0=ALU.mult, op1=ALU.add).then_inc(dve_done, 1)
                    dve.wait_ge(dve_done, dve_count.up("residual2", m))
                dve_count.mark("ln2", "z", m)

        sq2 = gate2[:, 0:KD, :]
        ln2_pe, ln2_act, ln2_dve = layer_norm_cm("ln2", h2, TC, sq2, q_raw, lambda k: col("ln_g_20", k), lambda k: col("ln_b_20", k),
                            eps[:, 2:3], h2, lambda t, k: t[:, k, :])

        def ln2_after_gates_act(act):
            act.wait_ge(*at("mla_out", KD - 1))
            ln2_act(act)

        def split_streams_dve(dve):
            for k in range(KD):
                nc.vector.tensor_copy(ctxT[:, k, :], h2[:, k, 0:CTX]).then_inc(dve_done, 1)
                dve.wait_ge(dve_done, dve_count.up())
                nc.vector.tensor_copy(xT[:, k, :], h2[:, k, CTX:TC]).then_inc(dve_done, 1)
                dve.wait_ge(dve_done, dve_count.up("x2", k))

        ml.close()

        h3 = sb(layers, "h3", [KD, STEP, C_ALL])
        yT = sb(layers, "yT", [KE, T])
        s5 = ExitStack()
        NPD = 2 * PAIRS
        TILE_PAIRS = PAIRS // KE
        TPD = 2 * TILE_PAIRS
        power = sb(s5, "power", [2, NPD, STEP + 1])
        b_factor = sb(s5, "b_factor", [2, NPD])
        decay8 = sb(s5, "decay8", [NPD])
        turn8 = sb(s5, "turn8", [2, NPD])
        bc = sb(s5, "bc", [4, TPD, GS])
        b_bar = sb(s5, "b_bar", [2, 2, TPD, GS])
        b_bar_split = sb(s5, "b_bar_split", [2, TPD, 2, GS])
        c_pow = sb(s5, "c_pow", [2, 2, TPD, STEP + 1, GS])
        b_pow = sb(s5, "b_pow", [2, 2, TPD, STEP, GS])
        pool_tmp = sb(s5, "pool_tmp", [512])
        table = sb(s5, "table", [2, 2, TPD, C_ALL])
        dve_tmp = sb(s5, "dve_tmp", [TPD * (STEP + 1) * GS])
        b_pow_t = sb(s5, "b_pow_t", [2, 4, P])
        u_t = sb(s5, "u_t", [2, 2, 2, C_ALL])
        x_in = sb(s5, "x_in", [2, 2, 2, C_LAT])
        lag_m = sb(s5, "lag_m", [2, 2 * TILE_PAIRS, P])
        y_tm = sb(s5, "y_tm", [STEP, P])
        skip = sb(s5, "skip", [PAIRS])
        eye = sb(s5, "eye", [GS])
        u_tm = ctxT[:, :, :].rearrange("p k t -> p (k t)").rearrange("p (b g s i) -> p b g s i", b=2, s=STEP, i=GS)
        b_bar = const[:, N_CONST - 2 * TPD * GS:N_CONST].rearrange("p (r t i) -> p r t i", r=2, i=GS)
        lags = const[:, 4 * P:4 * P + 2 * 4 * 240].rearrange("p (b g n) -> p b g n", b=2, n=240)
        mod_c, mod_s, zs = (dve_tmp[:, i * 4 * C_ALL:(i + 1) * 4 * C_ALL].rearrange("p (d r c) -> p d r c", d=2, r=2)
                            for i in range(3))
        lam = dve_tmp[:, 6 * NPD:9 * NPD].rearrange("p (k n) -> p k n", k=3)
        temp = [dve_tmp[:, i * NPD:(i + 1) * NPD] for i in range(6)]

        def s5_setup_act(act):
            act.wait_ge(lam_loaded, 16)
            nc.scalar.activation(lam[:, 2, :], lam[:, 2, :], ACT.Exp).then_inc(act_done, 1)
            act.wait_ge(act_done, act_count.up("s5", "dt"))
            act.wait_ge(*at("s5", "exponent"))
            nc.scalar.activation(temp[3], temp[0], ACT.Exp).then_inc(act_done, 1)
            act.wait_ge(act_done, act_count.up())
            nc.scalar.activation(decay8[:, :], temp[0], ACT.Exp, scale=float(STEP)).then_inc(act_done, 1)
            act.wait_ge(act_done, act_count.up("s5", "size"))
            act.wait_ge(*at("s5", "angle"))
            nc.scalar.activation(turn8[:, 1, :], temp[1], ACT.Sin).then_inc(act_done, 1)
            act.wait_ge(act_done, act_count.up())
            nc.scalar.activation(turn8[:, 0, :], temp[2], ACT.Sin).then_inc(act_done, 1)
            act.wait_ge(act_done, act_count.up("s5", "sincos"))

        def s5_setup_dve(dve):
            v = nc.vector
            re, im, dt = (lam[:, i, :] for i in range(3))
            mul, add_, sub = ALU.mult, ALU.add, ALU.subtract
            def tt(o, a, b, op):
                v.tensor_tensor(o, a, b, op).then_inc(dve_done, 1)
                dve.wait_ge(dve_done, dve_count.up())

            for k in range(KD):
                v.tensor_scalar(h3[:, k, :, 0:C_CTX], ctxT[:, k, :].rearrange("p (c s) -> p s c", s=STEP),
                                mod2[:, KD + k, 0:1], mod2[:, k, 0:1], mul, add_).then_inc(dve_done, 1)
                dve.wait_ge(dve_done, dve_count.up())
                v.tensor_scalar(h3[:, k, :, C_CTX:C_ALL], xT[:, k, :].rearrange("p (c s) -> p s c", s=STEP),
                                mod2[:, KD + k, 1:2], mod2[:, k, 1:2], mul, add_).then_inc(dve_done, 1)
                dve.wait_ge(dve_done, dve_count.up("h3", k))
            dve.wait_ge(*at("s5", "dt"))
            v.tensor_scalar(re, re, -1e-4, None, ALU.min).then_inc(dve_done, 1)
            dve.wait_ge(dve_done, dve_count.up())
            tt(temp[0], re, dt, mul)
            dve_count.mark("s5", "exponent")
            tt(temp[1], im, dt, mul)
            magic = 1.5 * 2 ** 23
            v.tensor_scalar(temp[2], temp[1], 1 / (2 * math.pi), magic, mul, add_).then_inc(dve_done, 1)
            dve.wait_ge(dve_done, dve_count.up())
            v.tensor_scalar(temp[2], temp[2], magic, None, sub).then_inc(dve_done, 1)
            dve.wait_ge(dve_done, dve_count.up())
            rest = 2 * math.pi
            for part in (6.28125, 0.0019350051879882812):
                v.scalar_tensor_tensor(out=temp[1], in0=temp[2], scalar=-part, in1=temp[1], op0=mul, op1=add_).then_inc(dve_done, 1)
                dve.wait_ge(dve_done, dve_count.up())
                rest -= part
            v.scalar_tensor_tensor(out=temp[1], in0=temp[2], scalar=-rest, in1=temp[1], op0=mul, op1=add_).then_inc(dve_done, 1)
            dve.wait_ge(dve_done, dve_count.up())
            v.tensor_scalar(temp[1], temp[1], 3.1415925, -3.1415925, ALU.min, ALU.max).then_inc(dve_done, 1)
            dve.wait_ge(dve_done, dve_count.up())
            v.scalar_tensor_tensor(out=temp[2], in0=temp[1], scalar=-1.0, in1=temp[1], op0=mul, op1=ALU.max).then_inc(dve_done, 1)
            dve.wait_ge(dve_done, dve_count.up())
            v.tensor_scalar(temp[2], temp[2], -1.0, math.pi / 2, mul, add_).then_inc(dve_done, 1)
            dve.wait_ge(dve_done, dve_count.up("s5", "angle"))
            dve.wait_ge(*at("s5", "size"))
            dve.wait_ge(*at("s5", "sincos"))
            lr, li = temp[4], temp[5]
            tt(lr, temp[3], turn8[:, 0, :], mul)
            tt(li, temp[3], turn8[:, 1, :], mul)
            tt(temp[0], re, re, mul)
            tt(temp[1], im, im, mul)
            tt(temp[0], temp[0], temp[1], add_)
            v.reciprocal(temp[0], temp[0]).then_inc(dve_done, 1)
            dve.wait_ge(dve_done, dve_count.up())
            v.tensor_scalar(temp[1], lr, -1.0, None, add_).then_inc(dve_done, 1)
            dve.wait_ge(dve_done, dve_count.up())
            tt(temp[2], temp[1], re, mul)
            tt(temp[3], li, im, mul)
            tt(temp[2], temp[2], temp[3], add_)
            tt(b_factor[:, 0, :], temp[2], temp[0], mul)
            tt(temp[2], li, re, mul)
            tt(temp[3], temp[1], im, mul)
            tt(temp[2], temp[2], temp[3], sub)
            tt(b_factor[:, 1, :], temp[2], temp[0], mul)
            def power_at(ri, i):
                p4 = power[:, ri, :, :].rearrange("p (g d) i -> p g d i", d=2)
                return p4[:, :, 0, i], p4[:, :, 1, STEP - i]
            two = lambda ap: (ap.rearrange("p (g d) -> p g d", d=2)[:, :, 0], ap.rearrange("p (g d) -> p g d", d=2)[:, :, 1])
            for d in range(2):
                v.memset(power_at(0, 0)[d], 1.0).then_inc(dve_done, 1)
                dve.wait_ge(dve_done, dve_count.up())
                v.memset(power_at(1, 0)[d], 0.0).then_inc(dve_done, 1)
                dve.wait_ge(dve_done, dve_count.up())
                v.tensor_copy(power_at(0, 1)[d], two(lr)[d]).then_inc(dve_done, 1)
                dve.wait_ge(dve_done, dve_count.up())
                v.tensor_copy(power_at(1, 1)[d], two(li)[d]).then_inc(dve_done, 1)
                dve.wait_ge(dve_done, dve_count.up())
                for i in range(2, STEP + 1):
                    a, b = power_at(0, i - 1)[d], power_at(1, i - 1)[d]
                    x, y = two(temp[0])[d], two(temp[1])[d]
                    tt(x, a, two(lr)[d], mul)
                    tt(y, b, two(li)[d], mul)
                    tt(power_at(0, i)[d], x, y, sub)
                    tt(x, a, two(li)[d], mul)
                    tt(y, b, two(lr)[d], mul)
                    tt(power_at(1, i)[d], x, y, add_)
            for _ in range(3):
                c, s = turn8[:, 0, :], turn8[:, 1, :]
                tt(temp[0], c, c, mul)
                tt(temp[1], s, s, mul)
                tt(temp[2], c, s, mul)
                tt(c, temp[0], temp[1], sub)
                v.tensor_scalar(s, temp[2], 2.0, None, mul).then_inc(dve_done, 1)
                dve.wait_ge(dve_done, dve_count.up())
            dve_count.mark("s5", "parameters")
            dve.wait_ge(small_loaded, 48)
            v.tensor_tensor(eye[0:2 * GS, :], mask("ident")[0:2 * GS, 0:GS], mask("ident")[0:2 * GS, GS:2 * GS],
                            add_).then_inc(dve_done, 1)
            dve.wait_ge(dve_done, dve_count.up())


        def tile_cols(m):
            return slice(m * TPD, (m + 1) * TPD)

        def b_bar_pool(pool, m):
            def tt(o, a, b, op, *key):
                nc.gpsimd.tensor_tensor(o, a, b, op).then_inc(pool_done, 1)
                pool.wait_ge(pool_done, pool_count.up(*key))

            if m == 0:
                pool.wait_ge(*at("s5", "parameters"))
            pool.wait_ge(table_loaded, 16 * (m + 1))
            if m >= 1:
                pool.wait_ge(*at("s5", "b_split", m - 1))
            fr, fi = (along(b_factor[:, i, tile_cols(m)], GS) for i in range(2))
            small = pool_tmp[:, 0:TPD * GS].rearrange("p (t i) -> p t i", i=GS)
            for ri, op in ((0, ALU.subtract), (1, ALU.add)):
                tt(b_bar[:, ri, :, :], bc[:, ri, :, :], fr, ALU.mult)
                tt(small, bc[:, 1 - ri, :, :], fi, ALU.mult)
                tt(b_bar[:, ri, :, :], b_bar[:, ri, :, :], small, op, "s5", "b_bar", m)

        def b_pow_pool(pool, m):
            def tt(o, a, b, op, *key):
                nc.gpsimd.tensor_tensor(o, a, b, op).then_inc(pool_done, 1)
                pool.wait_ge(pool_done, pool_count.up(*key))

            if m >= 2:
                pool.wait_ge(*at("s5", "b_turned", TILE_PAIRS * (m - 1) - 1))
            shape = [P, TILE_PAIRS, STEP, GS]
            part = pool_tmp[:, :].rearrange("p (t s i) -> p t s i", t=TILE_PAIRS, s=STEP)
            for d in range(2):
                idx = slice(7, None, -1) if d == 0 else slice(8, 0, -1)
                pr, pi = (power[:, i, m * TPD + d:(m + 1) * TPD:2, idx].unsqueeze(3).broadcast_to(shape) for i in range(2))
                br, bi = (b_bar[:, i, d::2, :].unsqueeze(2).broadcast_to(shape) for i in range(2))
                o_re, o_im = (b_pow[:, m % 2, i, d::2, :, :] for i in range(2))
                tt(o_re, br, pr, ALU.mult)
                tt(part, bi, pi, ALU.mult)
                tt(o_re, o_re, part, ALU.subtract)
                tt(o_im, br, pi, ALU.mult)
                tt(part, bi, pr, ALU.mult)
                tt(o_im, o_im, part, ALU.add, "s5", "b_pow", m)

        def c_pow_dve(dve, m, i):
            if m >= KE:
                return
            if i == 0:
                dve.wait_ge(table_loaded, 16 * (m + 1))
                if m >= 2:
                    dve.wait_ge(*at("s5", "y", TILE_PAIRS * (m - 1) - 1))
            n = STEP + 1
            shape = [P, TPD, n, GS]
            part = dve_tmp[:, :].rearrange("p (t s i) -> p t s i", t=TPD, s=n)
            pr, pi = (power[:, r, tile_cols(m), :].unsqueeze(3).broadcast_to(shape) for r in range(2))
            cr, ci = (bc[:, 2 + r, :, :].unsqueeze(2).broadcast_to(shape) for r in range(2))
            re, im = (c_pow[:, m % 2, r, :, :, :] for r in range(2))
            if i < 5:
                o, a, b, op = ((part, ci, pi, ALU.mult), (re, cr, pr, ALU.mult), (re, re, part, ALU.subtract),
                               (part, ci, pr, ALU.mult), (im, cr, pi, ALU.mult))[i]
                nc.vector.tensor_tensor(o, a, b, op).then_inc(dve_done, 1)
                dve.wait_ge(dve_done, dve_count.up())
            else:
                nc.vector.scalar_tensor_tensor(out=im, in0=im, scalar=-1.0, in1=part, op0=ALU.mult,
                                               op1=ALU.subtract).then_inc(dve_done, 1)
                dve.wait_ge(dve_done, dve_count.up("s5", "c_pow", m))

        def table_level(engine, e, done_sem, count, m, n, tmp):
            c, s = table[:, m % 2, 0, :, :], table[:, m % 2, 1, :, :]
            w = min(n, C_ALL - 1 - n)
            cn = c[:, :, n:n + 1].broadcast_to([P, TPD, w])
            sn = s[:, :, n:n + 1].broadcast_to([P, TPD, w])
            x, y = (tmp[:, i * TPD * w:(i + 1) * TPD * w].rearrange("p (t n) -> p t n", n=w) for i in range(2))
            for o, a, b, op in ((x, c[:, :, 1:1 + w], cn, ALU.mult), (y, s[:, :, 1:1 + w], sn, ALU.mult),
                                (c[:, :, n + 1:n + 1 + w], x, y, ALU.subtract),
                                (x, s[:, :, 1:1 + w], cn, ALU.mult), (y, c[:, :, 1:1 + w], sn, ALU.mult),
                                (s[:, :, n + 1:n + 1 + w], x, y, ALU.add)):
                e.tensor_tensor(o, a, b, op).then_inc(done_sem, 1)
                engine.wait_ge(done_sem, count.up())
            count.mark("s5", "table", m, n)

        def table_pool(pool, m):
            if m >= 2:
                pool.wait_ge(*at("s5", "x_in", TILE_PAIRS * (m - 1) - 1))
            nc.gpsimd.memset(table[:, m % 2, 0, :, 0:1], 1.0).then_inc(pool_done, 1)
            pool.wait_ge(pool_done, pool_count.up())
            nc.gpsimd.memset(table[:, m % 2, 1, :, 0:1], 0.0).then_inc(pool_done, 1)
            pool.wait_ge(pool_done, pool_count.up())
            nc.gpsimd.tensor_copy(table[:, m % 2, :, :, 1], turn8[:, :, tile_cols(m)]).then_inc(pool_done, 1)
            pool.wait_ge(pool_done, pool_count.up())
            for level in range(6):
                table_level(pool, nc.gpsimd, pool_done, pool_count, m, 2 ** level, pool_tmp)

        def table_dve(dve, m):
            if m >= KE:
                return
            dve.wait_ge(*at("s5", "table", m, 32))
            table_level(dve, nc.vector, dve_done, dve_count, m, 64, dve_tmp)

        def u_project_pe(pe, m, s):
            if m >= KE:
                return
            need_slot(pe, ("s5_in", m))
            if s == 0 and m == 0:
                pe.wait_ge(*at("h3", KD - 1))
            if s % 4 == 0 and m > 0:
                pe.wait_ge(*at("s5", "u", m - 1, s // 4))
            for k in range(KD):
                ins = nc.tensor.matmul(psum[0:C_ALL, s // 4, (s % 4) * P:(s % 4 + 1) * P], h3[:, k, s, :],
                                       tile_w(("s5_in", m), k), start=(k == 0), stop=(k == KD - 1))
            if s % 4 == 3:
                ins.then_inc(pe_done, 1)
                pe_count.up("s5", "u_mm", m, s // 4)
                if s == STEP - 1:
                    pe_count.mark("free", slot_of[("s5_in", m)])

        def u_act(act, m, hf):
            if m >= KE:
                return
            act.wait_ge(*at("s5", "u_mm", m, hf))
            if m >= 2:
                act.wait_ge(*at("s5", "u_turned", TILE_PAIRS * (m - 1) - 1))
            src = psum[0:C_ALL, hf, :].rearrange("p (s g i) -> p g s i", s=4, i=GS)
            for j in range(4):
                nc.scalar.activation(u_tm[0:C_ALL, m % 2, :, 4 * hf + j, :], src[:, :, j, :], ACT.Copy).then_inc(act_done, 1)
                act.wait_ge(act_done, act_count.up("s5", "u", m, hf))

        def b_split_act(act, m):
            if m >= KE:
                return
            act.wait_ge(*at("s5", "b_bar", m))
            if m >= 1:
                act.wait_ge(*at("s5", "lag_mm", m - 1, 1))
            for e in range(2):
                nc.scalar.activation(b_bar_split[:, :, :, e, :], b_bar, ACT.Copy,
                                     scale=mask("block_ones")[:, 64 * e:64 * e + 1]).then_inc(act_done, 1)
                act.wait_ge(act_done, act_count.up("s5", "b_split", m))

        def lags_pe(pe, m, hf):
            if m >= KE:
                return
            if hf == 0:
                pe.wait_ge(*at("s5", "c_pow", m))
                pe.wait_ge(*at("s5", "b_split", m))
            if m + hf >= 1:
                pe.wait_ge(*at("s5", "lag_copy", m - 1 + hf, 1 - hf))
            for pair in (2 * hf, 2 * hf + 1):
                for i, (d, lo) in enumerate(((1, 1), (0, 0))):
                    a = 256 * (pair % 2) + 112 * i
                    for ri in range(2):
                        ins = nc.tensor.matmul(psum[0:2 * GS, 4, a:a + P], b_bar_split[:, ri, 2 * pair + d, :, :],
                                               c_pow[:, m % 2, ri, 2 * pair + d, lo:lo + STEP, :],
                                               start=(i == 0 and ri == 0), stop=(i == 1 and ri == 1), skip_group_check=True)
            ins.then_inc(pe_done, 1)
            pe_count.up("s5", "lag_mm", m, hf)

        def lags_dve(dve, m):
            if m >= KE:
                return
            rows = slice(0, 2 * GS)
            for hf in range(2):
                dve.wait_ge(*at("s5", "lag_mm", m, hf))
                if hf == 0 and m >= 2:
                    dve.wait_ge(lags_moved[m % 2], 32 * (m // 2))
                src = psum[rows, 4, :].rearrange("p (g n) -> p g n", g=2)[:, :, 0:240]
                nc.vector.tensor_copy(lags[rows, m % 2, 2 * hf:2 * hf + 2, :], src).then_inc(dve_done, 1)
                dve.wait_ge(dve_done, dve_count.up("s5", "lag_copy", m, hf))
            shape = [2 * GS, TILE_PAIRS, GS]
            diagonal = dve_tmp[rows, 0:TILE_PAIRS * GS].rearrange("p (g i) -> p g i", i=GS)
            zero_lag = lags[rows, m % 2, :, 112:128]
            nc.vector.tensor_tensor(diagonal, eye[rows, :].unsqueeze(1).broadcast_to(shape),
                                    skip[rows, TILE_PAIRS * m:TILE_PAIRS * (m + 1)].unsqueeze(2).broadcast_to(shape),
                                    ALU.mult).then_inc(dve_done, 1)
            dve.wait_ge(dve_done, dve_count.up())
            nc.vector.tensor_tensor(zero_lag, zero_lag, diagonal, ALU.add).then_inc(dve_done, 1)
            dve.wait_ge(dve_done, dve_count.up("s5", "lag", m))

        def turn_pe(pe, n):
            m, pair = divmod(n, TILE_PAIRS)
            if m >= KE:
                return
            pe.wait_ge(*at("s5", "b_pow", m))
            if n >= 1:
                pe.wait_ge(*at("s5", "b_pow_t", n - 1))
            if pair == 2 and m > 0:
                pe.wait_ge(*at("s5", "yT", m - 1))
            for d in range(2):
                for ri in range(2):
                    j = 2 * d + ri
                    ins = nc.tensor.transpose(bank(2, j * P, (j + 1) * P),
                                              b_pow[:, m % 2, ri, 2 * pair + d, :, :].rearrange("p s i -> p (s i)"), mask("ident"))
            ins.then_inc(pe_done, 1)
            pe_count.up("s5", "b_turned", n)
            pe.wait_ge(*at("s5", "u", m, 1))
            if n >= 1:
                pe.wait_ge(*at("s5", "u_t", n - 1))
            for e in range(2):
                src = u_tm[0:C_ALL, m % 2, 2 * pair + e, :, :].rearrange("p s i -> p (s i)")
                ins = nc.tensor.transpose(bank(3, e * C_ALL, (e + 1) * C_ALL), src, mask("ident")[0:C_ALL, 0:C_ALL])
            ins.then_inc(pe_done, 1)
            pe_count.up("s5", "u_turned", n)

        def turn_act(act, n):
            if n >= PAIRS:
                return
            act.wait_ge(*at("s5", "b_turned", n))
            if n >= 2:
                act.wait_ge(*at("s5", "x", n - 2))
            nc.scalar.activation(b_pow_t[:, n % 2, :, :], bank(2).rearrange("p (j c) -> p j c", j=4), ACT.Copy).then_inc(act_done, 1)
            act.wait_ge(act_done, act_count.up("s5", "b_pow_t", n))
            act.wait_ge(*at("s5", "u_turned", n))
            if n >= 2:
                act.wait_ge(*at("s5", "y", n - 2))
            src = bank(3, 0, 2 * C_ALL).rearrange("p (e c) -> p e c", e=2)
            nc.scalar.activation(u_t[:, n % 2, 0, :, :], src, ACT.Copy).then_inc(act_done, 1)
            act.wait_ge(act_done, act_count.up())
            nc.scalar.activation(u_t[:, n % 2, 1, :, 0:C_CTX], src[:, :, C_CTX - 1::-1], ACT.Copy).then_inc(act_done, 1)
            act.wait_ge(act_done, act_count.up())
            nc.scalar.activation(u_t[:, n % 2, 1, :, C_CTX:C_ALL], src[:, :, C_ALL - 1:C_CTX - 1:-1], ACT.Copy).then_inc(act_done, 1)
            act.wait_ge(act_done, act_count.up("s5", "u_t", n))

        def x_pe(pe, n):
            if n >= PAIRS:
                return
            pe.wait_ge(*at("s5", "u_t", n))
            if n >= 1:
                pe.wait_ge(*at("s5", "x_read", n - 1))
            for d in range(2):
                for ri in range(2):
                    j = 2 * d + ri
                    for e in range(2):
                        ins = nc.tensor.matmul(psum[half(e), 6, j * C_ALL:(j + 1) * C_ALL],
                                               b_pow_t[:, n % 2, j, half(e)], u_t[:, n % 2, d, e, :], start=True, stop=True)
            ins.then_inc(pe_done, 1)
            pe_count.up("s5", "x", n)

        def state_dve(dve, n):
            v = nc.vector
            m, pair = divmod(n, TILE_PAIRS)
            def tt(o, a, b, op, *key):
                v.tensor_tensor(o, a, b, op).then_inc(dve_done, 1)
                dve.wait_ge(dve_done, dve_count.up(*key))

            x = bank(6, 0, 4 * C_ALL).rearrange("p (d r c) -> p d r c", d=2, r=2)
            both_parts = lambda i, a, b: (table[:, m % 2, i, 2 * pair:2 * pair + 2, a:b].unsqueeze(2)
                                          .broadcast_to([P, 2, 2, b - a]))
            dve.wait_ge(*at("s5", "x", n))
            tt(mod_c, x, both_parts(0, 0, C_ALL), ALU.mult)
            tt(mod_s, x, both_parts(1, 0, C_ALL), ALU.mult, "s5", "x_read", n)
            tt(mod_c[:, :, 0, :], mod_c[:, :, 0, :], mod_s[:, :, 1, :], ALU.add)
            tt(mod_c[:, :, 1, :], mod_c[:, :, 1, :], mod_s[:, :, 0, :], ALU.subtract)
            for d in range(2):
                decay = decay8[:, 2 * n + d:2 * n + d + 1].broadcast_to([P, C_ALL])
                for ri in range(2):
                    v.tensor_tensor_scan(zs[:, d, ri, :], decay, mod_c[:, d, ri, :], 0.0, ALU.mult, ALU.add).then_inc(dve_done, 1)
                    dve.wait_ge(dve_done, dve_count.up())
            a, b = C_CTX - 1, C_ALL - 1
            tt(mod_c[:, :, :, 0:C_LAT], zs[:, :, :, a:b], both_parts(0, a, b), ALU.mult)
            tt(mod_s[:, :, :, 0:C_LAT], zs[:, :, :, a:b], both_parts(1, a, b), ALU.mult)
            if n >= 2:
                dve.wait_ge(*at("s5", "y", n - 2))
            for d in range(2):
                for ri, op in enumerate((ALU.subtract, ALU.add)):
                    o = x_in[:, n % 2, d, ri, :]
                    o = o if d == 0 else o[:, ::-1]
                    tt(o, mod_c[:, d, ri, 0:C_LAT], mod_s[:, d, 1 - ri, 0:C_LAT], op, "s5", "x_in", n)

        def y_pe(pe, n):
            m, pair = divmod(n, TILE_PAIRS)
            pe.wait_ge(*at("s5", "x_in", n))
            if n >= 1:
                pe.wait_ge(*at("s5", "y_tm", n - 1))
            if pair == 0:
                pe.wait_ge(lags_moved[2 + m % 2], 16 * 8 * (m // 2 + 1))
            cp = c_pow[:, m % 2, :, :, :, :]
            for e in range(2):
                o = psum[0:C_LAT, 5 + 2 * e, 0:P]
                nc.tensor.matmul(o, u_t[:, n % 2, 0, e, C_CTX:C_ALL], lag_m[:, m % 2, 2 * pair + e, :], start=True, stop=False)
                for d, lo in ((0, 1), (1, 0)):
                    for ri in range(2):
                        ins = nc.tensor.matmul(o, x_in[half(e), n % 2, d, ri, :], cp[half(e), ri, 2 * pair + d, lo:lo + STEP, :],
                                               start=False, stop=(d == 1 and ri == 1))
            ins.then_inc(pe_done, 1)
            pe_count.up("s5", "y", n)

        def y_act(act, n):
            m, pair = divmod(n, TILE_PAIRS)
            act.wait_ge(*at("s5", "y", n))
            if pair == 0 and m > 0:
                act.wait_ge(*at("s5", "y_turned", m - 1))
            for e in range(2):
                g = 2 * pair + e
                nc.scalar.activation(y_tm[0:C_LAT, :, g * GS:(g + 1) * GS],
                                     psum[0:C_LAT, 5 + 2 * e, 0:P].rearrange("p (t i) -> p t i", i=GS), ACT.Copy).then_inc(act_done, 1)
                act.wait_ge(act_done, act_count.up("s5", "y_tm", n))

        def y_turn_pe(pe, m):
            pe.wait_ge(*at("s5", "y_tm", TILE_PAIRS * (m + 1) - 1))
            pe.wait_ge(*at("s5", "b_pow_t", min(TILE_PAIRS * (m + 1) + 1, PAIRS - 1)))
            for s in range(STEP):
                ins = nc.tensor.transpose(bank(2, s * C_LAT, (s + 1) * C_LAT), y_tm[0:C_LAT, s, :], mask("ident")[0:C_LAT, 0:C_LAT])
            ins.then_inc(pe_done, 1)
            pe_count.up("s5", "y_turned", m)

        def y_turn_act(act, m):
            act.wait_ge(*at("s5", "y_turned", m))
            nc.scalar.activation(yT[:, m, :], bank(2), ACT.Gelu_apprx_tanh).then_inc(act_done, 1)
            act.wait_ge(act_done, act_count.up("s5", "yT", m))

        TOKENS = ((0, 1, 2), (3, 4, 5), (6, 7), ())

        def s5_pe(pe):
            for s in range(STEP):
                u_project_pe(pe, 0, s)
            for hf in range(2):
                lags_pe(pe, 0, hf)
            turn_pe(pe, 0)
            x_pe(pe, 0)
            for m in range(KE):
                for pair in range(TILE_PAIRS):
                    n = m * TILE_PAIRS + pair
                    turn_pe(pe, n + 1)
                    for s in TOKENS[pair]:
                        u_project_pe(pe, m + 1, s)
                    if pair == 0 and m > 0:
                        y_turn_pe(pe, m - 1)
                    if pair == TILE_PAIRS - 1:
                        lags_pe(pe, m + 1, 0)
                    x_pe(pe, n + 1)
                    if pair == TILE_PAIRS - 1:
                        lags_pe(pe, m + 1, 1)
                    y_pe(pe, n)
            y_turn_pe(pe, KE - 1)

        def s5_act(act):
            u_act(act, 0, 0)
            u_act(act, 0, 1)
            b_split_act(act, 0)
            turn_act(act, 0)
            for m in range(KE):
                for pair in range(TILE_PAIRS):
                    n = m * TILE_PAIRS + pair
                    turn_act(act, n + 1)
                    if pair == 0 and m > 0:
                        y_turn_act(act, m - 1)
                    if pair == 1:
                        u_act(act, m + 1, 0)
                    if pair == 2:
                        u_act(act, m + 1, 1)
                        b_split_act(act, m + 1)
                    y_act(act, n)
            y_turn_act(act, KE - 1)

        def s5_dve(dve):
            for i in range(6):
                c_pow_dve(dve, 0, i)
            lags_dve(dve, 0)
            table_dve(dve, 0)
            for m in range(KE):
                for pair in range(TILE_PAIRS):
                    state_dve(dve, m * TILE_PAIRS + pair)
                    if pair == 0:
                        for i in range(3):
                            c_pow_dve(dve, m + 1, i)
                    if pair == 1:
                        for i in range(3, 6):
                            c_pow_dve(dve, m + 1, i)
                    if pair == TILE_PAIRS - 1:
                        lags_dve(dve, m + 1)
                        table_dve(dve, m + 1)

        def s5_pool(pool):
            for m in range(KE):
                b_bar_pool(pool, m)
                b_pow_pool(pool, m)
                table_pool(pool, m)

        s5.close()

        gl = ExitStack()
        gates = sb(gl, "gates", [KE, T])
        sig = sb(gl, "sig", [2, T])
        glu_tmp = sb(gl, "glu_tmp", [2, T])
        sq_3 = sb(gl, "sq_3", [KD, T])
        stat_3 = sb(gl, "stat_3", [2, T])

        def gates_pe(pe):
            for i in range(KE):
                need_slot(pe, ("s5_in", KE + i))
                if i >= 2:
                    pe.wait_ge(*at("gates", i - 2))
                for k in range(KD):
                    ins = nc.tensor.matmul(bank(i % 2), tile_w(("s5_in", KE + i), k), h3[:, k, :, C_CTX:C_ALL],
                                           start=(k == 0), stop=(k == KD - 1))
                ins.then_inc(pe_done, 1)
                pe_count.up("gates_mm", i)
                pe_count.mark("free", slot_of[("s5_in", KE + i)])

        def gates_act(act):
            for i in range(KE):
                act.wait_ge(*at("gates_mm", i))
                nc.scalar.activation(gates[:, i, :], bank(i % 2), ACT.Silu).then_inc(act_done, 1)
                act.wait_ge(act_done, act_count.up("gates", i))

        def glu_pe(pe):
            for i in range(KE):
                b = 2 + 2 * (i % 3)
                if i >= 3:
                    pe.wait_ge(*at("glu", i - 3))
                for hf in range(2):
                    for k in range(KE):
                        key = ("glu", hf * 2 * KE + 2 * i + k // KD)
                        need_slot(pe, key)
                        ins = nc.tensor.matmul(bank(b + hf), tile_w(key, k % KD), yT[:, k, :], start=(k == 0), stop=(k == KE - 1))
                    ins.then_inc(pe_done, 1)
                    pe_count.up("glu_mm", i, hf)
                    for j in range(2):
                        pe_count.mark("free", slot_of[("glu", hf * 2 * KE + 2 * i + j)])

        def glu_act(act):
            for i in range(KE):
                act.wait_ge(*at("glu_mm", i, 1))
                if i >= 2:
                    act.wait_ge(*at("glu", i - 2))
                nc.scalar.activation(sig[:, i % 2, :], bank(3 + 2 * (i % 3)), ACT.Sigmoid, bias=col("b_glu", KE + i)).then_inc(act_done, 1)
                act.wait_ge(act_done, act_count.up("glu_sig", i))

        def glu_dve(dve):
            for i in range(KE):
                dve.wait_ge(*at("glu_sig", i))
                nc.vector.scalar_tensor_tensor(out=glu_tmp[:, i % 2, :], in0=bank(2 + 2 * (i % 3)), scalar=col("b_glu", i),
                                               in1=sig[:, i % 2, :], op0=ALU.add, op1=ALU.mult).then_inc(dve_done, 1)
                dve.wait_ge(dve_done, dve_count.up("glu", i))
                nc.vector.tensor_tensor(gates[:, i, :], gates[:, i, :], glu_tmp[:, i % 2, :], ALU.mult).then_inc(dve_done, 1)
                dve.wait_ge(dve_done, dve_count.up("glu_out", i))

        def s5_out_pe(pe):
            for m in range(KD):
                if m >= 2:
                    pe.wait_ge(*at("residual3", m - 2))
                for k in range(KE):
                    if m == 0:
                        pe.wait_ge(*at("glu_out", k))
                    key = ("s5_out", 2 * m + k // KD)
                    need_slot(pe, key)
                    ins = nc.tensor.matmul(bank(m % 2), tile_w(key, k % KD), gates[:, k, :], start=(k == 0), stop=(k == KE - 1))
                ins.then_inc(pe_done, 1)
                pe_count.up("s5_out", m)
                for i in range(2):
                    pe_count.mark("free", slot_of[("s5_out", 2 * m + i)])

        z3 = h3[:, :, :, :].rearrange("p k s c -> p (k s c)")[:, 0:KD * T].rearrange("p (k t) -> p k t", k=KD)

        def s5_out_dve(dve):
            for m in range(KD):
                dve.wait_ge(*at("s5_out", m))
                z = z3[:, m, :].rearrange("p (s c) -> p s c", s=STEP)
                nc.vector.tensor_scalar(z, xT[:, m, :].rearrange("p (c s) -> p s c", s=STEP), ALPHA_2, None, ALU.mult).then_inc(dve_done, 1)
                dve.wait_ge(dve_done, dve_count.up())
                nc.vector.scalar_tensor_tensor(out=z3[:, m, :], in0=bank(m % 2), scalar=mod2[:, 2 * KD + m, 1:2],
                                               in1=z3[:, m, :], op0=ALU.mult, op1=ALU.add).then_inc(dve_done, 1)
                dve.wait_ge(dve_done, dve_count.up("residual3", m))
                dve_count.mark("ln3", "z", m)

        ln3_pe, ln3_act, ln3_dve = layer_norm_cm("ln3", z3, T, sq_3, stat_3, lambda k: col("ln_g_21", k), lambda k: col("ln_b_21", k), eps[:, 2:3],
                            z3, lambda t, k: t[:, k, :])
        gl.close()

        def output_sync(sp):
            for k in range(KD):
                sp.wait_ge(*at("ln3", "out", k))
                sp.dma_start(io["out"][:, k, :], z3[:, k, :]).then_inc(stored, 16)
            sp.wait_ge(stored, 16 * KD)

        block = memory.enter_context(nc.Block())

        @block.sync
        def _(sp):
            sp.dma_start(const[:, :], io["const"]).then_inc(small_loaded, 16)
            sp.dma_start(cols[:, :], io["cols"]).then_inc(small_loaded, 16)
            sp.dma_start(xT[:, :, :], io["xT"]).then_inc(x_loaded, 16)
            for n, (tensor, i, floats, _) in enumerate(stream):
                if n == 8:
                    sp.dma_start(lnv[:, :, :], io["lnv"].partition_broadcast(P)).then_inc(gmlp_loaded, 16)
                    sp.dma_start(w_sp[:, :, :], io["w_sp"]).then_inc(gmlp_loaded, 16)
                    for e2 in range(2):
                        sp.dma_start(b_sp[64 * e2:64 * e2 + 64, :, :], io["b_sp"][e2].partition_broadcast(64)).then_inc(gmlp_loaded, 16)
                if n == slot_of[("out", 0)]:
                    for who in ("pe", "act", "dve"):
                        sp.wait_ge(*at("end", "projections", who))
                    for e2 in range(2):
                        sp.dma_start(up[64 * e2:64 * e2 + 64, :], io["up"][64 * e2:64 * e2 + 64, :]).then_inc(gmlp_loaded, 16)
                if n == slot_of[("mod0", 1)]:
                    sp.wait_ge(*at("end", "first_block", "dve"))
                    sp.wait_ge(*at("end", "first_block", "pe"))
                    sp.wait_ge(*at("end", "first_block", "act"))
                    sp.dma_start(ctxT[:, :, :], io["ctxT"]).then_inc(ctx_loaded, 16)
                if n == slot_of[("s5_in", 0)]:
                    for who in ("pe", "act", "dve"):
                        sp.wait_ge(*at("end", "mla", who))
                    sp.dma_start(lam, io["lam"]).then_inc(lam_loaded, 16)
                    sp.dma_start(skip[0:2 * GS, :], io["skip"]).then_inc(small_loaded, 16)
                    sp.dma_start(bc[:, :, :, :], io["bc"][0]).then_inc(table_loaded, 16)
                tile = n - slot_of[("s5_in", 0)] - RING + 1
                if 0 <= tile < KE:
                    if tile + 1 < KE:
                        sp.wait_ge(*at("s5", "b_bar", tile))
                        sp.wait_ge(*at("s5", "c_pow", tile))
                        sp.dma_start(bc[:, :, :, :], io["bc"][tile + 1]).then_inc(table_loaded, 16)
                    sp.wait_ge(*at("s5", "lag", tile))
                    for e2 in range(2):
                        sp.dma_start(io["lags"][tile % 2][:, e2::2, :],
                                     lags[GS * e2:GS * (e2 + 1), tile % 2, :, :]).then_inc(lags_moved[tile % 2], 16)
                    sp.wait_ge(lags_moved[tile % 2], 32 * (tile // 2 + 1))
                    if tile >= 2:
                        sp.wait_ge(*at("s5", "y", TILE_PAIRS * (tile - 1) - 1))
                    for s in range(STEP):
                        sp.dma_start(lag_m[GS * s:GS * (s + 1), tile % 2, :, :],
                                     io["lags"][tile % 2][:, :, (7 - s) * GS:(7 - s) * GS + P]).then_inc(lags_moved[2 + tile % 2], 16)
                if n >= RING:
                    sp.wait_ge(*at("free", n - RING))
                sp.dma_start(ring[:, n % RING, 0:floats], io[tensor][i]).then_inc(slot_loaded[n % RING], 16)
            output_sync(sp)

        @block.tensor
        def _(pe):
            modulation_pe(pe, "ada", silu_c, 1)
            project_pe(pe)
            mixing_pe(pe)
            phase_end(pe, pe_count, "projections")
            for q in range(NPAIR):
                rwkv_prep_pe(pe, q)
                rwkv_unit_pe(pe, q)
            group_norm_pe(pe)
            phase_end(pe, pe_count, "rwkv")
            out_pe(pe)
            ln1_pe(pe)
            phase_end(pe, pe_count, "first_block")
            modulation_pe(pe, "mod0", vec2, 2)
            mla_in_pe(pe)
            for h in range(-1, HEADS + 1):
                head_pe(pe, h)
            phase_end(pe, pe_count, "heads")
            mla_out_pe(pe)
            ln2_pe(pe)
            phase_end(pe, pe_count, "mla")
            modulation_pe(pe, "mod1", vec2, 2)
            s5_pe(pe)
            phase_end(pe, pe_count, "s5")
            gates_pe(pe)
            glu_pe(pe)
            s5_out_pe(pe)
            ln3_pe(pe)

        @block.scalar
        def _(act):
            ada_act(act)
            project_act(act)
            phase_end(act, act_count, "projections")
            rwkv_start_act(act)
            for q in range(NPAIR):
                rwkv_prep_act(act, q)
                rwkv_unit_act(act, q)
            group_norm_act(act)
            phase_end(act, act_count, "rwkv")
            ln1_act(act)
            phase_end(act, act_count, "first_block")
            mod2_act(act, "mod0")
            mla_in_act(act)
            for h in range(-1, HEADS + 1):
                head_act(act, h)
            phase_end(act, act_count, "heads")
            ln2_after_gates_act(act)
            phase_end(act, act_count, "mla")
            mod2_act(act, "mod1")
            s5_setup_act(act)
            s5_act(act)
            phase_end(act, act_count, "s5")
            gates_act(act)
            glu_act(act)
            ln3_act(act)

        @block.vector
        def _(dve):
            start_dve(dve)
            ada_dve(dve)
            project_dve(dve)
            mixing_dve(dve)
            phase_end(dve, dve_count, "projections")
            rwkv_start_dve(dve)
            for q in range(NPAIR):
                rwkv_prep_dve(dve, q)
                rwkv_unit_dve(dve, q)
            group_norm_dve(dve)
            phase_end(dve, dve_count, "rwkv")
            out_dve(dve)
            ln1_dve(dve)
            phase_end(dve, dve_count, "first_block")
            mod2_dve(dve, "mod0", "b_mod_0")
            mla_h_dve(dve)
            mla_in_dve(dve)
            for h in range(-1, HEADS + 1):
                head_dve(dve, h)
            phase_end(dve, dve_count, "heads")
            mla_out_dve(dve)
            ln2_dve(dve)
            split_streams_dve(dve)
            phase_end(dve, dve_count, "mla")
            mod2_dve(dve, "mod1", "b_mod_1")
            s5_setup_dve(dve)
            s5_dve(dve)
            phase_end(dve, dve_count, "s5")
            glu_dve(dve)
            s5_out_dve(dve)
            ln3_dve(dve)

        @block.gpsimd
        def _(pool):
            mask_pool(pool)
            phase_end(pool, pool_count, "projections")
            for q in range(NPAIR):
                rwkv_unit_pool(pool, q)
            phase_end(pool, pool_count, "rwkv")
            phase_end(pool, pool_count, "first_block")
            phase_end(pool, pool_count, "heads")
            phase_end(pool, pool_count, "mla")
            s5_pool(pool)
            phase_end(pool, pool_count, "s5")

        layers.close()
    return steps


def tiles(w, k_tiles):
    k, m = w.shape
    t = w.reshape(k // P, P, m // P, P).transpose(2, 1, 0, 3)
    n = k // P // k_tiles
    t = t.reshape(m // P, P, n, k_tiles, P).transpose(0, 2, 1, 3, 4)
    return np.ascontiguousarray(t).reshape(m // P * n, P, k_tiles * P)


def per_channel(v):
    return v.reshape(-1, P).T


def rope_columns(w):
    a, b, c, d = np.split(w, 4, axis=-1)
    return np.concatenate([w, b, a, d, c], axis=-1)


def lay_out(i):
    o = {"const": constants()}
    o["xT"] = np.ascontiguousarray(i["x"][0].T.reshape(KD, P, T).transpose(1, 0, 2))
    o["ctxT"] = np.ascontiguousarray(i["ctx_2"][0].T.reshape(KD, P, CTX).transpose(1, 0, 2))
    v = {
        "c": i["c"][0], "b_ada": i["b_ada"], "mu_b": i["mu_b"], "w0": i["w0"], "a0": i["a0"], "k_k": i["k_k"],
        "k_a": i["k_a"], "r_k": i["r_k"].reshape(-1), "gn_g": i["gn_g"].reshape(-1), "gn_b": i["gn_b"].reshape(-1),
        "ln_g": i["ln_g"], "ln_b": i["ln_b"], "c_2": i["c_2"][0], "c_ctx_2": i["c_ctx_2"],
        "b_mod_0": i["b_mod_2"][0], "b_mod_1": i["b_mod_2"][1], "ln_g_20": i["ln_g_2"][0], "ln_b_20": i["ln_b_2"][0],
        "ln_g_21": i["ln_g_2"][1], "ln_b_21": i["ln_b_2"][1], "q_norm": i["mla_q_norm_2"][0],
        "kv_norm": i["mla_kv_norm_2"][0], "s5_d": i["s5_d_2"][0], "b_glu": i["s5_b_glu_2"][0],
    }
    o["cols"] = np.ascontiguousarray(np.concatenate([per_channel(v[k]) for k, _ in COLUMNS], axis=1))
    o["lnv"] = np.ascontiguousarray(np.stack([i["ln_v_g"].reshape(-1), i["ln_v_b"].reshape(-1)]))
    o["w_sp"] = np.ascontiguousarray(i["w_spatial"].transpose(2, 0, 1))
    o["b_sp"] = np.ascontiguousarray(i["b_spatial"].reshape(4, 2, P).transpose(1, 0, 2))
    o["up"] = np.ascontiguousarray(np.concatenate([i["w_up"], i["a_up"]]))
    o["w_ada"] = tiles(i["w_ada"], KD)
    o["w_in"] = tiles(i["w_in"], KD)
    o["w_out"] = tiles(i["w_out"], KD)
    o["w_mod_0"] = tiles(i["w_mod_2"][0], KD)
    o["w_mod_1"] = tiles(i["w_mod_2"][1], KD)
    w = i["mla_w_in_2"][0]
    r = Q_RANK + KV_RANK
    w = np.concatenate([w[:, :r], rope_columns(w[:, r:r + ROPE]), w[:, r + ROPE:]], axis=1)
    o["mla_in"] = tiles(w, KD)
    uq = i["mla_w_uq_2"][0].reshape(2, P, HEADS, 192)
    uq = np.concatenate([uq[..., :128], rope_columns(uq[..., 128:])], axis=-1)
    uq = uq.transpose(2, 1, 0, 3).reshape(HEADS, P, 512)
    uk = i["mla_w_uk_2"][0].transpose(1, 2, 0)
    uv = i["mla_w_uv_2"][0].transpose(1, 0, 2)
    o["mla_head"] = np.ascontiguousarray(np.concatenate([uq, uk, uv], axis=2))
    o["mla_out"] = tiles(i["mla_w_out_2"][0], KD)
    o["s5_in"] = tiles(i["s5_w_in_2"][0], KD)
    o["s5_glu"] = tiles(i["s5_w_glu_2"][0], KD)
    o["s5_out"] = tiles(i["s5_w_out_2"][0], KD)
    lam = lambda a: a[0].reshape(2, PAIRS, P).transpose(2, 1, 0)
    dt = np.repeat(i["s5_log_dt_2"][0][:, :, None], STATE, axis=2)
    lams = np.stack([lam(i["s5_lam_re_2"]), lam(i["s5_lam_im_2"]), lam(dt[None])], axis=1)
    o["lam"] = np.ascontiguousarray(lams).reshape(P, 3, 2 * PAIRS)
    b = lambda a: a[0].reshape(2, KE, 4, P, GS).transpose(1, 3, 2, 0, 4)
    cm = lambda a: b(a.transpose(0, 1, 2, 4, 3))
    bc = np.stack([b(i["s5_b_re_2"]), b(i["s5_b_im_2"]), cm(i["s5_c_re_2"]), cm(i["s5_c_im_2"])], axis=2)
    o["bc"] = np.ascontiguousarray(bc).reshape(KE, P, 4, 8, GS)
    o["skip"] = np.ascontiguousarray(i["s5_d_2"][0].reshape(PAIRS, 2 * GS).T)
    return o


OUT_SHAPE = (P, KD, T)


def program(nc, shapes, known):
    io = {name: nc.dram_tensor(f"in_{name}", shape, F32, kind="ExternalInput").ap() for name, shape in shapes.items()}
    io["lags"] = nc.dram_tensor("lags", (2, GS, 8, 240), F32, kind="Internal").ap()
    io["out"] = nc.dram_tensor("outT", OUT_SHAPE, F32, kind="ExternalOutput").ap()
    return build(nc, io, known)


def kernel(**inputs):
    import concourse.bacc as bacc
    from concourse.bass_utils import run_bass_kernel_spmd as run

    arrays = lay_out({k: np.asarray(v) for k, v in inputs.items()})
    shapes = {k: v.shape for k, v in arrays.items()}
    known = program(bacc.Bacc("TRN2", target_bir_lowering=False, num_devices=1), shapes, {})
    nc = bacc.Bacc("TRN2", target_bir_lowering=False, num_devices=1)
    program(nc, shapes, known)
    result = run(nc, [{f"in_{k}": v for k, v in arrays.items()}], core_ids=[0]).results[0]["outT"]
    out = result.reshape(P, KD, STEP, C_LAT).transpose(3, 2, 1, 0)
    return np.ascontiguousarray(out).reshape(1, T, D)
```

```python
import math
from contextlib import ExitStack

import numpy as np
import concourse.bass as bass
from concourse import mybir

ALU = mybir.AluOpType
ACT = mybir.ActivationFunctionType
AX = mybir.AxisListType
F32 = mybir.dt.float32
F32R = mybir.dt.float32r

P = 128
BANK = 512
D = 1024
KD = D // P
T = 512
CTX = 256
TC = T + CTX
HALF = TC // 2
TT = T // P

D_A = D_B = D // 2
HEAD = 64
NPAIR = D_B // P
CHUNK = 64
NCHUNK = T // CHUNK
W_IN_TILES = 29
IN_ORDER = [*range(4, 8), *range(0, 4), *range(8, W_IN_TILES)]
LEVELS = 5
LN_EPS, GN_EPS, NORM_EPS = 1e-5, 64e-5, 1e-6
ALPHA_1 = 2.0 ** 0.25
ALPHA_2 = 4.0 ** 0.25

HEADS = 16
Q_RANK, KV_RANK, ROPE = 256, 128, 64
E_BRANCH = 2048
KE = E_BRANCH // P
SOFTMAX_SCALE = (128 + 64) ** -0.5

GROUPS, STATE, GS = 128, 64, 16
PAIRS = GROUPS // 2
STEP = 8
C_LAT, C_CTX = T // STEP, CTX // STEP
C_ALL = C_CTX + C_LAT

SLOT = KD * P
RING = 6

MASKS = ["ident", "ones", "block_ones", "dup", "diag2_lower", "diag2_upper", "incl_upper",
         "strict_upper", "level1", "level2", "level3", "level4", "level5"]
TABLES = {"reset": T, "rope": T}

COLUMNS = [
    ("c", KD), ("b_ada", 3 * KD), ("mu_b", 17), ("w0", NPAIR), ("a0", NPAIR), ("k_k", NPAIR),
    ("k_a", NPAIR), ("r_k", NPAIR), ("gn_g", NPAIR), ("gn_b", NPAIR), ("ln_g", KD), ("ln_b", KD),
    ("c_2", KD), ("c_ctx_2", KD), ("b_mod_0", 3 * KD), ("b_mod_1", 3 * KD), ("ln_g_20", KD),
    ("ln_b_20", KD), ("ln_g_21", KD), ("ln_b_21", KD), ("q_norm", 2), ("kv_norm", 1),
    ("s5_d", KE), ("b_glu", 2 * KE),
]
COLUMN_AT, N_COLUMNS = {}, 0
for _name, _n in COLUMNS:
    COLUMN_AT[_name] = (N_COLUMNS, _n)
    N_COLUMNS += _n


def constants():
    r = np.arange(P)
    row, col = r[:, None], r[None, :]
    same = lambda n: row // n == col // n
    masks = {
        "ident": row == col,
        "ones": np.ones((P, P)),
        "block_ones": same(64),
        "dup": row % 64 == col % 64,
        "diag2_lower": same(2) & (col < row),
        "diag2_upper": same(2) & (row < col),
        "incl_upper": same(CHUNK) & (row <= col),
        "strict_upper": same(CHUNK) & (row < col),
    }
    for level in range(1, LEVELS + 1):
        n = 2 ** level
        masks[f"level{level}"] = same(2 * n) & (row // n < col // n)
    out = {k: np.asarray(masks[k], np.float32) for k in MASKS}
    out["reset"] = np.tile((np.arange(T) % CHUNK != 0).astype(np.float32), (P, 1))
    pos = np.arange(T, dtype=np.float32)
    inv = (np.float32(10000.0) ** (-np.arange(16, dtype=np.float32) / np.float32(16))).astype(np.float32)
    ang_r = np.floor(pos / 64)[:, None] * inv
    ang_c = (pos % 64)[:, None] * inv
    ang = np.concatenate([ang_r, ang_r, ang_c, ang_c], axis=-1).astype(np.float32)
    sign = np.repeat(np.array([-1, 1, -1, 1], np.float32), 16)
    out["rope"] = np.concatenate([np.cos(ang).T, (np.sin(ang) * sign).T]).astype(np.float32)
    return np.ascontiguousarray(np.concatenate([out[k] for k in MASKS + list(TABLES)], axis=1))


N_CONST = len(MASKS) * P + sum(TABLES.values())


def weight_stream():
    s = [("w_ada", i, SLOT, ("ada", i)) for i in range(3 * KD)]
    s += [("w_in", i, SLOT, ("in", i)) for i in IN_ORDER]
    s += [("w_mod_0", i, SLOT, ("mod0", i)) for i in range(3 * KD)]
    s += [("w_mod_1", i, SLOT, ("mod1", i)) for i in range(3 * KD)]
    s += [("w_out", i, SLOT, ("out", i)) for i in range(KD)]
    s += [("mla_in", i, SLOT, ("mla_in", i)) for i in range(4)]
    s += [("mla_in", i, SLOT, ("mla_in", i)) for i in range(4, 20)]
    s += [("mla_head", i, 768, ("head", i)) for i in range(HEADS)]
    s += [("mla_out", i, SLOT, ("mla_out", i)) for i in range(2 * KD)]
    s += [("s5_in", i, SLOT, ("s5_in", i)) for i in range(2 * KE)]
    s += [("s5_glu", j, SLOT, ("glu", j)) for i in range(KE) for j in (2 * i, 2 * i + 1, 2 * KE + 2 * i, 2 * KE + 2 * i + 1)]
    s += [("s5_out", i, SLOT, ("s5_out", i)) for i in range(2 * KD)]
    return s


class Count:

    def __init__(self, semaphore, table):
        self.semaphore, self.table, self.value = semaphore, table, 0

    def mark(self, *step):
        self.table[step] = (self.semaphore, self.value)

    def up(self, *step):
        self.value += 1
        if step:
            self.mark(*step)
        return self.value


def build(nc, io, known):
    stream = weight_stream()
    slot_of = {key: n for n, (_, _, _, key) in enumerate(stream)}
    memory = ExitStack()
    with memory:
        psum = memory.enter_context(nc.psum_tensor("psum", [P, 8, BANK], F32))
        pe_done = memory.enter_context(nc.semaphore("pe_done"))
        act_done = memory.enter_context(nc.semaphore("act_done"))
        dve_done = memory.enter_context(nc.semaphore("dve_done"))
        pool_done = memory.enter_context(nc.semaphore("pool_done"))
        done = {"pe": pe_done, "act": act_done, "dve": dve_done, "pool": pool_done}
        steps = {}
        pe_count, act_count = Count("pe", steps), Count("act", steps)
        dve_count, pool_count = Count("dve", steps), Count("pool", steps)

        def at(*step):
            who, count = known.get(step, ("pe", 1))
            return done[who], count

        small_loaded = memory.enter_context(nc.semaphore("small_loaded"))
        x_loaded = memory.enter_context(nc.semaphore("x_loaded"))
        ctx_loaded = memory.enter_context(nc.semaphore("ctx_loaded"))
        gmlp_loaded = memory.enter_context(nc.semaphore("gmlp_loaded"))
        stored = memory.enter_context(nc.semaphore("stored"))
        slot_loaded = [memory.enter_context(nc.semaphore(f"slot_loaded_{i}")) for i in range(RING)]
        s5_loaded = [memory.enter_context(nc.semaphore(f"s5_loaded_{i}")) for i in range(4)]
        lam_loaded = memory.enter_context(nc.semaphore("lam_loaded"))
        table_loaded = memory.enter_context(nc.semaphore("table_loaded"))
        lags_moved = [memory.enter_context(nc.semaphore(f"lags_moved_{i}")) for i in range(4)]

        def sb(stack, name, shape):
            return stack.enter_context(nc.sbuf_tensor(name, [P] + shape, F32))

        ring = sb(memory, "ring", [RING, SLOT])
        const = sb(memory, "const", [N_CONST])
        cols = sb(memory, "cols", [N_COLUMNS])
        xT = sb(memory, "xT", [KD, T])
        eps = sb(memory, "eps", [4])
        misc = sb(memory, "misc", [18 * KD])
        ada = misc[:, 0:3 * KD]
        mods = [misc[:, (3 + 6 * i) * KD:(9 + 6 * i) * KD].rearrange("p (i v) -> p i v", v=2) for i in range(2)]
        vec2 = misc[:, 15 * KD:17 * KD].rearrange("p (i v) -> p i v", v=2)
        silu_c = misc[:, 17 * KD:18 * KD].unsqueeze(2)

        def mask(name):
            n = MASKS.index(name)
            return const[:, n * P:(n + 1) * P]

        reset = const[:, len(MASKS) * P:len(MASKS) * P + T]
        rope = const[:, len(MASKS) * P + T:len(MASKS) * P + 2 * T]

        def col(name, i=None):
            a, n = COLUMN_AT[name]
            return cols[:, a:a + n] if i is None else cols[:, a + i:a + i + 1]

        def slot(key):
            return ring[:, slot_of[key] % RING, :]

        def tile_w(key, k, width=P):
            return slot(key)[:, k * width:(k + 1) * width]

        def need_slot(e, key):
            n = slot_of[key]
            e.wait_ge(slot_loaded[n % RING], 16 * (n // RING + 1))

        def bank(n, a=0, b=BANK):
            return psum[:, n, a:b]

        def flat(a, b):
            return psum[:, :, :].rearrange("p b n -> p (b n)")[:, a:b]

        def over(ap, n):
            return ap.unsqueeze(1).broadcast_to([P, n, ap.shape[-1]])

        def along(ap, n):
            return ap.unsqueeze(2).broadcast_to([P, ap.shape[-1], n])


        MOD_BATCH = 2 * 3 * KD // (2 * NPAIR)

        def mod_batch(n):
            layer, first_tile = divmod(n * MOD_BATCH, 3 * KD)
            return layer, range(first_tile, first_tile + MOD_BATCH)

        def mod2_place(n, j):
            return psum[0:2, 7 - n % 2 - j // 4, (j % 4) * P:(j % 4 + 1) * P]

        def mod2_pe(pe, n, a, b):
            layer, batch = mod_batch(n)
            for j in range(a, b):
                key = (f"mod{layer}", batch[j])
                need_slot(pe, key)
                for k in range(KD):
                    ins = nc.tensor.matmul(mod2_place(n, j), vec2[:, k, :], tile_w(key, k), start=(k == 0), stop=(k == KD - 1))
                ins.then_inc(pe_done, 1)
                pe_count.up("free", slot_of[key])
                pe_count.mark("mod2", n, "row", j)

        def mod2_rows_dve(dve, n):
            for a, b in ((0, 4), (4, MOD_BATCH)):
                dve.wait_ge(*at("mod2", n, "row", MOD_BATCH - 1))
                nc.vector.tensor_copy(mod_row[0:2, n % 2, a * P:b * P],
                                      psum[0:2, 7 - n % 2 - a // 4, 0:(b - a) * P]).then_inc(dve_done, 1)
                dve.wait_ge(dve_done, dve_count.up("mod2", n, "rows"))

        def mod2_turn_pe(pe, n, b):
            pe.wait_ge(*at("mod2", n, "rows"))
            for j in range(MOD_BATCH):
                ins = nc.tensor.matmul(bank(b, 2 * j, 2 * j + 2), mod_row[0:2, n % 2, j * P:(j + 1) * P],
                                       mask("ident")[0:2, 0:2], start=True, stop=True)
            ins.then_inc(pe_done, 1)
            pe_count.up("mod2", n, "turned")

        def mod2_dve(dve, n, bank_no):
            layer, batch = mod_batch(n)
            a, b = batch[0], batch[-1] + 1
            dve.wait_ge(*at("mod2", n, "turned"))
            nc.vector.tensor_tensor(mods[layer][:, a:b, :], bank(bank_no, 0, 2 * MOD_BATCH).rearrange("p (i v) -> p i v", v=2),
                                    along(col(f"b_mod_{layer}")[:, a:b], 2), ALU.add).then_inc(dve_done, 1)
            dve.wait_ge(dve_done, dve_count.up("mod2", n, "added"))
            if b == 3 * KD:
                nc.vector.tensor_scalar(mods[layer][:, KD:2 * KD, :], mods[layer][:, KD:2 * KD, :], 1.0, None,
                                        ALU.add).then_inc(dve_done, 1)
                dve.wait_ge(dve_done, dve_count.up("mod2", n, "added"))

        def layer_norm_cm(name, z, tokens, sq, stat, gain, shift, eps_col, outs):
            parts = [(flat(5 * BANK, 5 * BANK + T), 0, T)]
            if tokens > T:
                parts = [(flat(5 * BANK - CTX, 5 * BANK), 0, CTX), (flat(5 * BANK, 5 * BANK + T), CTX, T)]
            sums = flat(5 * BANK + T - tokens, 5 * BANK + T)

            def pe_part(pe):
                for what, src in (("mean", z), ("var", sq)):
                    for k in range(KD):
                        pe.wait_ge(*at(name, "z" if what == "mean" else "sq", k))
                        for o, a, n in parts:
                            ins = nc.tensor.matmul(o, mask("ones"), src[:, k, a:a + n],
                                                   start=(k == 0), stop=(k == KD - 1))
                    ins.then_inc(pe_done, 1)
                    pe_count.up(name, what)

            def act_part(act):
                for k in range(KD):
                    act.wait_ge(*at(name, "centred", k))
                    nc.scalar.activation(sq[:, k, :], z[:, k, :], ACT.Square).then_inc(act_done, 1)
                    act.wait_ge(act_done, act_count.up(name, "sq", k))
                act.wait_ge(*at(name, "var"))
                nc.scalar.activation(stat[:, 0, :], sums, ACT.Sqrt, bias=eps_col, scale=1.0 / D).then_inc(act_done, 1)
                act.wait_ge(act_done, act_count.up(name, "std"))
                for k in range(KD):
                    act.wait_ge(*at(name, "scaled", k))
                    for dst, src in outs(k):
                        nc.scalar.activation(dst, src, ACT.Identity, bias=shift(k), scale=gain(k)).then_inc(act_done, 1)
                        act.wait_ge(act_done, act_count.up(name, "out", k))

            def dve_part(dve):
                dve.wait_ge(*at(name, "mean"))
                nc.vector.tensor_scalar(stat[:, 1, :], sums, 1.0 / D, None, ALU.mult).then_inc(dve_done, 1)
                dve.wait_ge(dve_done, dve_count.up())
                for k in range(KD):
                    nc.vector.tensor_tensor(z[:, k, :], z[:, k, :], stat[:, 1, :], ALU.subtract).then_inc(dve_done, 1)
                    dve.wait_ge(dve_done, dve_count.up(name, "centred", k))
                dve.wait_ge(*at(name, "std"))
                nc.vector.reciprocal(stat[:, 1, :], stat[:, 0, :]).then_inc(dve_done, 1)
                dve.wait_ge(dve_done, dve_count.up())
                for k in range(KD):
                    nc.vector.tensor_tensor(z[:, k, :], z[:, k, :], stat[:, 1, :], ALU.mult).then_inc(dve_done, 1)
                    dve.wait_ge(dve_done, dve_count.up(name, "scaled", k))
            return pe_part, act_part, dve_part

        def phase_end(engine, count, phase):
            count.mark("end", phase, count.semaphore)
            for who in ("pe", "act", "dve", "pool"):
                if who != count.semaphore and known.get(("end", phase, who), ("", 1))[1] > 0:
                    engine.wait_ge(*at("end", phase, who))

        HALF_SLOT = SLOT // 2
        UNIT_K = KD // 2

        def rounded(ap):
            return ap.bitcast(F32R)

        def split_weights(name, buffers, keys):
            n_buffers = buffers.shape[1]

            def source(u):
                return slot(keys[u // 2])[:, (u % 2) * HALF_SLOT:(u % 2 + 1) * HALF_SLOT]

            def buffer(u, part):
                return buffers[:, u % n_buffers, part, :]

            def act_part(act, u):
                need_slot(act, keys[u // 2])
                if u >= n_buffers:
                    act.wait_ge(*at(name, "used", u - n_buffers))
                nc.scalar.activation(rounded(buffer(u, 0)), source(u), ACT.Copy).then_inc(act_done, 1)
                act.wait_ge(act_done, act_count.up(name, "rounded", u))

            def dve_part(dve, u):
                dve.wait_ge(*at(name, "rounded", u))
                nc.vector.tensor_tensor(rounded(buffer(u, 1)), source(u), buffer(u, 0), ALU.subtract).then_inc(dve_done, 1)
                dve.wait_ge(dve_done, dve_count.up(name, "rest", u))
                if u % 2 == 1:
                    dve_count.mark("free", slot_of[keys[u // 2]])

            def pool_part(pool, u):
                pool.wait_ge(*at(name, "rounded", u))
                nc.gpsimd.tensor_tensor(rounded(buffer(u, 1)), source(u), buffer(u, 0), ALU.subtract).then_inc(pool_done, 1)
                pool.wait_ge(pool_done, pool_count.up(name, "rest", u))
                if u % 2 == 1:
                    pool_count.mark("free", slot_of[keys[u // 2]])

            def pe_part(pe, u, out, values, first, last):
                pe.wait_ge(*at(name, "rest", u))
                for k in range(UNIT_K):
                    ks = slice(k * P, (k + 1) * P)
                    for n, (w, x) in enumerate(((0, 0), (0, 1), (1, 0))):
                        ins = nc.tensor.matmul(out, rounded(buffer(u, w)[:, ks]), values(x, k),
                                               start=(first and k == 0 and n == 0),
                                               stop=(last and k == UNIT_K - 1 and n == 2))
                ins.then_inc(pe_done, 1)
                pe_count.up(name, "used", u)

            return act_part, dve_part, pool_part, pe_part

        def split_values(split):
            return lambda unit: lambda part, k: rounded(split[:, part, unit * UNIT_K + k, :])

        def split_act(act, name, split, source, k):
            nc.scalar.activation(rounded(split[:, 0, k, :]), source[:, k, :], ACT.Copy).then_inc(act_done, 1)
            act.wait_ge(act_done, act_count.up(name, "rounded", k))

        def split_dve(dve, name, split, source, k):
            dve.wait_ge(*at(name, "rounded", k))
            nc.vector.tensor_tensor(rounded(split[:, 1, k, :]), source[:, k, :], split[:, 0, k, :],
                                    ALU.subtract).then_inc(dve_done, 1)
            dve.wait_ge(dve_done, dve_count.up(name, "rest", k))

        def start_dve(dve):
            for i, v in enumerate((LN_EPS, GN_EPS, NORM_EPS, 1e-12)):
                nc.vector.memset(eps[:, i:i + 1], v).then_inc(dve_done, 1)
                dve.wait_ge(dve_done, dve_count.up())
            dve.wait_ge(small_loaded, 32)
            dve_count.mark("eps")


        first = ExitStack()
        hT = sb(first, "hT", [KD, T])
        ada_row = hT[:, 0:6, :].rearrange("p k t -> p (k t)")
        def ada_act(act):
            act.wait_ge(small_loaded, 32)
            nc.scalar.activation(silu_c[:, :, 0], col("c"), ACT.Silu).then_inc(act_done, 1)
            act.wait_ge(act_done, act_count.up())
            for i, name in enumerate(("c_ctx_2", "c_2")):
                nc.scalar.activation(vec2[:, :, i], col(name), ACT.Silu).then_inc(act_done, 1)
                act.wait_ge(act_done, act_count.up("vectors"))

        def ada_pe(pe):
            pe.wait_ge(*at("vectors"))
            for i in range(3 * KD):
                need_slot(pe, ("ada", i))
                for k in range(KD):
                    ins = nc.tensor.matmul(psum[0:1, i // 4, (i % 4) * P:(i % 4 + 1) * P], silu_c[:, k, :],
                                           tile_w(("ada", i), k), start=(k == 0), stop=(k == KD - 1))
                ins.then_inc(pe_done, 1)
                pe_count.up("free", slot_of[("ada", i)])
                pe_count.mark("ada", "sum", i)
            for n in range(6):
                pe.wait_ge(*at("ada", "row", n))
                for i in range(4 * n, 4 * n + 4):
                    ins = nc.tensor.matmul(bank(7, i, i + 1), ada_row[0:1, i * P:(i + 1) * P], mask("ones")[0:1, 0:1],
                                           start=True, stop=True)
            ins.then_inc(pe_done, 1)
            pe_count.up("ada", "turned")

        def ada_dve(dve):
            for n in range(6):
                dve.wait_ge(*at("ada", "sum", 4 * n + 3))
                nc.vector.tensor_copy(ada_row[0:1, n * BANK:(n + 1) * BANK], psum[0:1, n, :]).then_inc(dve_done, 1)
                dve.wait_ge(dve_done, dve_count.up("ada", "row", n))
            dve.wait_ge(*at("ada", "turned"))
            nc.vector.tensor_tensor(ada, bank(7, 0, 3 * KD), col("b_ada"), ALU.add).then_inc(dve_done, 1)
            dve.wait_ge(dve_done, dve_count.up())
            nc.vector.tensor_scalar(ada[:, KD:2 * KD], ada[:, KD:2 * KD], 1.0, None, ALU.add).then_inc(dve_done, 1)
            dve.wait_ge(dve_done, dve_count.up())
            dve.wait_ge(x_loaded, 16)
            for k in range(KD):
                nc.vector.tensor_scalar(hT[:, k, :], xT[:, k, :], ada[:, KD + k:KD + k + 1],
                                        ada[:, k:k + 1], ALU.mult, ALU.add).then_inc(dve_done, 1)
                dve.wait_ge(dve_done, dve_count.up("hT", k))


        rkvg = sb(first, "rkvg", [16, T])
        wdad = sb(first, "wdad", [T])
        gm = ExitStack()
        uT = sb(gm, "uT", [4, T])
        gT = sb(gm, "gT", [4, T])
        vT = sb(gm, "vT", [TT, D_A])
        vsq = sb(gm, "vsq", [TT, D_A])
        vstat = sb(gm, "vstat", [4, 32])
        lnv = sb(gm, "lnv", [2, D_A])
        b_sp = sb(gm, "b_sp", [4, P])
        w_sp = sb(gm, "w_sp", [8, P])
        prev = sb(gm, "prev", [2, T + 1])
        diff = sb(gm, "diff", [T])
        h_split = sb(gm, "h_split", [2, KD, T])
        in_w = sb(gm, "in_w", [4, 2, HALF_SLOT])
        in_w_act, _, in_w_pool, in_w_pe = split_weights("in_w", in_w, [("in", m) for m in IN_ORDER[4:]])
        mixT = hT

        def h_split_act(act):
            for k in range(KD):
                act.wait_ge(*at("hT", k))
                split_act(act, "h_split", h_split, hT, k)

        def h_split_dve(dve):
            for k in range(KD):
                split_dve(dve, "h_split", h_split, hT, k)

        def project_pe(pe):
            values = split_values(h_split)
            for job, m in enumerate(IN_ORDER):
                b = 1 + job % 5
                if job >= 5:
                    pe.wait_ge(*at("in", "evac", job - 5))
                if job < 4:
                    need_slot(pe, ("in", m))
                    for tt in range(TT):
                        for k in range(KD):
                            pe.wait_ge(*at("hT", k))
                            ins = nc.tensor.matmul(bank(b, tt * P, (tt + 1) * P), hT[:, k, tt * P:(tt + 1) * P],
                                                   tile_w(("in", m), k), start=(k == 0), stop=(k == KD - 1))
                    ins.then_inc(pe_done, 1)
                    pe_count.up("in", "mm", job)
                    pe_count.mark("free", slot_of[("in", m)])
                    continue
                for unit in range(2):
                    if job == 4:
                        pe.wait_ge(*at("h_split", "rest", KD - 1))
                    in_w_pe(pe, 2 * (job - 4) + unit, bank(b), values(unit), unit == 0, unit == 1)
                pe_count.mark("in", "mm", job)

        def project_pool(pool):
            for u in range(2 * (W_IN_TILES - 4)):
                in_w_pool(pool, u)

        def project_dve(dve):
            for i in range(2):
                nc.vector.memset(prev[:, i, 0:1], 0.0).then_inc(dve_done, 1)
                dve.wait_ge(dve_done, dve_count.up("prev_zero"))
            gmlp_norm(dve)
            for i in range(17):
                dve.wait_ge(*at("raw", i))
                nc.vector.tensor_tensor(diff[:, :], prev[:, i % 2, 0:T], prev[:, i % 2, 1:T + 1],
                                        ALU.subtract).then_inc(dve_done, 1)
                dve.wait_ge(dve_done, dve_count.up())
                dst = rkvg[:, i, :] if i < 16 else wdad[:, :]
                nc.vector.scalar_tensor_tensor(out=dst, in0=diff[:, :], scalar=col("mu_b", i),
                                               in1=prev[:, i % 2, 1:T + 1], op0=ALU.mult, op1=ALU.add).then_inc(dve_done, 1)
                dve.wait_ge(dve_done, dve_count.up("shifted", i))

        def gmlp_norm(dve):
            v3 = vT[:, :, :].rearrange("p t (g d) -> p (t g) d", d=HEAD)
            s3 = vsq[:, :, :].rearrange("p t (g d) -> p (t g) d", d=HEAD)
            dve.wait_ge(*at("v_gelu"))
            nc.vector.tensor_reduce(vstat[:, 0, :], v3, AX.X, ALU.add).then_inc(dve_done, 1)
            dve.wait_ge(dve_done, dve_count.up())
            nc.vector.tensor_scalar(vstat[:, 1, :], vstat[:, 0, :], 1.0 / HEAD, None, ALU.mult).then_inc(dve_done, 1)
            dve.wait_ge(dve_done, dve_count.up())
            nc.vector.tensor_tensor(v3, v3, along(vstat[:, 1, :], HEAD), ALU.subtract).then_inc(dve_done, 1)
            dve.wait_ge(dve_done, dve_count.up())
            nc.vector.tensor_tensor(s3, v3, v3, ALU.mult).then_inc(dve_done, 1)
            dve.wait_ge(dve_done, dve_count.up())
            nc.vector.tensor_reduce(vstat[:, 2, :], s3, AX.X, ALU.add).then_inc(dve_done, 1)
            dve.wait_ge(dve_done, dve_count.up("v_squares"))
            dve.wait_ge(*at("v_std"))
            nc.vector.reciprocal(vstat[:, 0, :], vstat[:, 3, :]).then_inc(dve_done, 1)
            dve.wait_ge(dve_done, dve_count.up())
            nc.vector.tensor_tensor(v3, v3, along(vstat[:, 0, :], HEAD), ALU.mult).then_inc(dve_done, 1)
            dve.wait_ge(dve_done, dve_count.up())
            dve.wait_ge(gmlp_loaded, 16 * 4)
            nc.vector.tensor_tensor(vT[:, :, :], vT[:, :, :], over(lnv[:, 0, :], TT), ALU.mult).then_inc(dve_done, 1)
            dve.wait_ge(dve_done, dve_count.up())
            nc.vector.tensor_tensor(vT[:, :, :], vT[:, :, :], over(lnv[:, 1, :], TT), ALU.add).then_inc(dve_done, 1)
            dve.wait_ge(dve_done, dve_count.up("v_norm"))

        def v_std_act(act):
            act.wait_ge(*at("v_squares"))
            nc.scalar.activation(vstat[:, 3, :], vstat[:, 2, :], ACT.Sqrt, bias=eps[:, 0:1],
                                 scale=1.0 / HEAD).then_inc(act_done, 1)
            act.wait_ge(act_done, act_count.up("v_std"))

        def project_act(act):
            for job in range(W_IN_TILES + 1):
                if 4 <= job < W_IN_TILES:
                    in_w_act(act, 2 * (job - 4))
                    in_w_act(act, 2 * (job - 4) + 1)
                if job > 0:
                    project_one(act, job - 1, IN_ORDER[job - 1])
                if job == 12:
                    v_std_act(act)

        def project_one(act, job, m):
            b = 1 + job % 5
            act.wait_ge(*at("in", "mm", job))
            if m < 4:
                nc.scalar.activation(uT[:, m, :], bank(b), ACT.Gelu_apprx_tanh).then_inc(act_done, 1)
                act.wait_ge(act_done, act_count.up("in", "evac", job))
            elif m < 8:
                nc.scalar.activation(vT[:, :, (m - 4) * P:(m - 3) * P],
                                     bank(b).rearrange("p (t d) -> p t d", t=TT),
                                     ACT.Gelu_apprx_tanh).then_inc(act_done, 1)
                act.wait_ge(act_done, act_count.up("in", "evac", job))
                if m == 7:
                    act_count.mark("v_gelu")
            elif m < 12:
                nc.scalar.activation(gT[:, m - 8, :], bank(b), ACT.Silu).then_inc(act_done, 1)
                act.wait_ge(act_done, act_count.up("in", "evac", job))
                act_count.mark("silu_g", m - 8)
            else:
                i = m - 12
                if i >= 2:
                    act.wait_ge(*at("shifted", i - 2))
                else:
                    act.wait_ge(*at("prev_zero"))
                nc.scalar.activation(prev[:, i % 2, 1:T + 1], bank(b), ACT.Copy).then_inc(act_done, 1)
                act.wait_ge(act_done, act_count.up("in", "evac", job))
                act_count.mark("raw", i)

        def mask_pool(pool):
            pool.wait_ge(gmlp_loaded, 16 * 4)
            nc.gpsimd.affine_select(out=w_sp[:, :, :], in_=w_sp[:, :, :], compare_op=ALU.is_ge,
                                    fill=0.0, base=0, pattern=[[0, 8], [1, P]],
                                    channel_multiplier=-1).then_inc(pool_done, 1)
            pool.wait_ge(pool_done, pool_count.up("w_sp"))

        def mixing_pe(pe):
            pe.wait_ge(*at("w_sp"))
            pe.wait_ge(*at("v_norm"))
            for q in range(4):
                if q < 2:
                    pe.wait_ge(*at("in", "evac", W_IN_TILES - 1))
                else:
                    pe.wait_ge(*at("mixed", q - 2))
                for e in range(2):
                    g = 2 * q + e
                    for tt in range(TT):
                        ins = nc.tensor.matmul(psum[64 * e:64 * e + 64, 6 + q % 2, tt * P:(tt + 1) * P],
                                               vT[:, tt, g * HEAD:(g + 1) * HEAD], w_sp[:, g, :],
                                               start=True, stop=True)
                ins.then_inc(pe_done, 1)
                pe_count.up("mixing", q)

        def mixing_dve(dve):
            dve.wait_ge(*at("in", "mm", W_IN_TILES - 1))
            for q in range(4):
                dve.wait_ge(*at("mixing", q))
                m3 = mixT[:, q, :].rearrange("p (t c) -> p t c", t=TT)
                nc.vector.tensor_tensor(m3, bank(6 + q % 2).rearrange("p (t c) -> p t c", t=TT),
                                        over(b_sp[:, q, :], TT), ALU.add).then_inc(dve_done, 1)
                dve.wait_ge(dve_done, dve_count.up("mixed", q))
                nc.vector.tensor_tensor(mixT[:, q, :], mixT[:, q, :], uT[:, q, :], ALU.mult).then_inc(dve_done, 1)
                dve.wait_ge(dve_done, dve_count.up())
                dve.wait_ge(*at("silu_g", q))
                nc.vector.tensor_tensor(mixT[:, q, :], mixT[:, q, :], gT[:, q, :], ALU.mult).then_inc(dve_done, 1)
                dve.wait_ge(dve_done, dve_count.up("mixT", q))

        gm.close()

        rw = ExitStack()
        mod_row = sb(rw, "mod_row", [2, MOD_BATCH * P])
        up = sb(rw, "up", [D_B])
        kscale = sb(rw, "kscale", [2, NPAIR])
        a_cm = sb(rw, "a_cm", [T])
        g_cm = sb(rw, "g_cm", [T])
        k_cm = sb(rw, "k_cm", [T])
        ke_cm = sb(rw, "ke_cm", [T])
        b_rate = sb(rw, "b_rate", [T])
        kk = sb(rw, "kk", [T])
        tmp = sb(rw, "tmp", [T])
        k_new = sb(rw, "k_new", [T])
        b_cm = sb(rw, "b_cm", [T])
        be_cm = sb(rw, "be_cm", [T])
        tm = sb(rw, "tm", [TT, 4, P])
        unit = {}
        for e in range(2):
            for name in ("Z", "ZT", "AT", "U", "RBT", "RKT", "AKT", "W"):
                unit[name, e] = sb(rw, f"{name}_{e}", [TT, P])
            unit["AL", e] = sb(rw, f"AL_{e}", [2, TT, P])
            unit["AKV", e] = sb(rw, f"AKV_{e}", [TT, HEAD])
        r_read = sb(rw, "r_read", [T])
        carry = sb(rw, "carry", [NCHUNK, P])
        inject = sb(rw, "inject", [NCHUNK, HEAD])
        states = sb(rw, "states", [NCHUNK, P])

        def half(e):
            return slice(64 * e, 64 * e + 64)

        def tt4(ap):
            return ap.rearrange("p (t c) -> p t c", t=TT)

        def rwkv_start_dve(dve):
            nc.vector.tensor_scalar(kscale[:, 0, :], col("k_a"), -1.0, 1.0, ALU.mult, ALU.add).then_inc(dve_done, 1)
            dve.wait_ge(dve_done, dve_count.up())
            nc.vector.memset(carry[:, :, :], 0.0).then_inc(dve_done, 1)
            dve.wait_ge(dve_done, dve_count.up())
            nc.vector.memset(states[:, :, :], 0.0).then_inc(dve_done, 1)
            dve.wait_ge(dve_done, dve_count.up("states_zero"))

        def rwkv_start_act(act):
            nc.scalar.activation(wdad[0:64, :], wdad[0:64, :], ACT.Tanh).then_inc(act_done, 1)
            act.wait_ge(act_done, act_count.up("tanh_wd"))

        def rwkv_prep_pe(pe, q):
            if q == 0:
                pe.wait_ge(*at("tanh_wd"))
                pe.wait_ge(gmlp_loaded, 16 * 6)
            cs = slice(q * P, (q + 1) * P)
            if q > 0:
                pe.wait_ge(*at("mod2", 2 * q - 2, "added"))
                pe.wait_ge(*at("rw", q - 1, "y_copied"))
                pe.wait_ge(*at("rw", q - 1, "state_added", NCHUNK - 1))
            nc.tensor.matmul(bank(0), up[0:64, cs], wdad[0:64, :], start=True, stop=True).then_inc(pe_done, 1)
            pe_count.up("rw", q, "w_raw")
            nc.tensor.matmul(bank(1), up[64:128, cs], wdad[64:128, :], start=True, stop=True).then_inc(pe_done, 1)
            pe_count.up("rw", q, "a_raw")
            if q > 0:
                mod2_turn_pe(pe, 2 * q - 1, 4)
            mod2_pe(pe, 2 * q, 0, 1)
            pe.wait_ge(*at("rw", q, "k_sq"))
            nc.tensor.matmul(bank(2), mask("block_ones"), tmp[:, :], start=True, stop=True).then_inc(pe_done, 1)
            pe_count.up("rw", q, "k_ss")
            mod2_pe(pe, 2 * q, 1, MOD_BATCH - 1)
            pe.wait_ge(*at("rw", q, "rk"))
            nc.tensor.matmul(bank(3), mask("block_ones"), tmp[:, :], start=True, stop=True).then_inc(pe_done, 1)
            pe_count.up("rw", q, "rk_sum")
            mod2_pe(pe, 2 * q, MOD_BATCH - 1, MOD_BATCH)
            pe.wait_ge(*at("rw", q, "operands"))
            for tt in range(TT):
                if tt == 0 and q > 0:
                    pe.wait_ge(*at("mod2", 2 * q - 1, "added"))
                if tt == 2:
                    pe.wait_ge(*at("mod2", 2 * q, "rows"))
                ts = slice(tt * P, (tt + 1) * P)
                for n, src in enumerate((a_cm[:, ts], be_cm[:, ts], ke_cm[:, ts], rkvg[:, 8 + q, ts])):
                    ins = nc.tensor.transpose(bank(4 + tt, n * P, (n + 1) * P), src, mask("ident"))
                ins.then_inc(pe_done, 1)
                pe_count.up("rw", q, "turned", tt)

        def rwkv_prep_act(act, q):
            act.wait_ge(*at("rw", q, "w_raw"))
            if q > 0:
                act.wait_ge(*at("rw", q - 1, "unit_mm"))
            nc.scalar.activation(a_cm[:, :], bank(0), ACT.Sigmoid, bias=col("w0", q)).then_inc(act_done, 1)
            act.wait_ge(act_done, act_count.up("rw", q, "decay_sig"))
            act.wait_ge(*at("rw", q, "a_raw"))
            nc.scalar.activation(b_rate[:, :], bank(1), ACT.Sigmoid, bias=col("a0", q)).then_inc(act_done, 1)
            act.wait_ge(act_done, act_count.up("rw", q, "rate"))
            act.wait_ge(*at("rw", q, "k_ss"))
            nc.scalar.activation(kk[:, :], bank(2), ACT.Sqrt, bias=eps[:, 3:4]).then_inc(act_done, 1)
            act.wait_ge(act_done, act_count.up("rw", q, "k_norm"))
            act.wait_ge(*at("rw", q, "G"))
            nc.scalar.activation(a_cm[:, :], a_cm[:, :], ACT.Exp).then_inc(act_done, 1)
            act.wait_ge(act_done, act_count.up("rw", q, "exp_Gx"))
            nc.scalar.activation(k_cm[:, :], g_cm[:, :], ACT.Exp, scale=-1.0).then_inc(act_done, 1)
            act.wait_ge(act_done, act_count.up("rw", q, "exp_nG"))
            nc.scalar.activation(ke_cm[:, :], ke_cm[:, :], ACT.Exp).then_inc(act_done, 1)
            act.wait_ge(act_done, act_count.up("rw", q, "exp_Ge"))
            nc.scalar.activation(g_cm[:, :], g_cm[:, :], ACT.Exp).then_inc(act_done, 1)
            act.wait_ge(act_done, act_count.up("rw", q, "exp_G"))
            for tt in range(TT):
                act.wait_ge(*at("rw", q, "turned", tt))
                nc.scalar.activation(tm[:, tt, :, :], bank(4 + tt).rearrange("p (n c) -> p n c", n=4),
                                     ACT.Copy).then_inc(act_done, 1)
                act.wait_ge(act_done, act_count.up("rw", q, "tm", tt))

        def rwkv_prep_dve(dve, q):
            v = nc.vector
            r_, k_, v_ = rkvg[:, q, :], rkvg[:, 4 + q, :], rkvg[:, 8 + q, :]
            if q > 0:
                dve.wait_ge(*at("rw", q - 1, "unit_mm"))
            dve.wait_ge(*at("rw", q, "decay_sig"))
            v.tensor_scalar(a_cm[:, :], a_cm[:, :], -math.exp(-0.5), None, ALU.mult).then_inc(dve_done, 1)
            dve.wait_ge(dve_done, dve_count.up())
            v.tensor_tensor_scan(g_cm[:, :], reset, a_cm[:, :], 0.0, ALU.mult, ALU.add).then_inc(dve_done, 1)
            dve.wait_ge(dve_done, dve_count.up())
            v.tensor_tensor(a_cm[:, :], g_cm[:, :], a_cm[:, :], ALU.subtract).then_inc(dve_done, 1)
            dve.wait_ge(dve_done, dve_count.up())
            g3 = g_cm[:, :].rearrange("p (c t) -> p c t", t=CHUNK)
            v.tensor_tensor(ke_cm[:, :].rearrange("p (c t) -> p c t", t=CHUNK),
                            g3[:, :, CHUNK - 1:CHUNK].broadcast_to([P, NCHUNK, CHUNK]), g3,
                            ALU.subtract).then_inc(dve_done, 1)
            dve.wait_ge(dve_done, dve_count.up("rw", q, "G"))
            v.tensor_scalar(k_new[:, :], k_, col("k_k", q), None, ALU.mult).then_inc(dve_done, 1)
            dve.wait_ge(dve_done, dve_count.up())
            v.tensor_tensor(tmp[:, :], k_new[:, :], k_new[:, :], ALU.mult).then_inc(dve_done, 1)
            dve.wait_ge(dve_done, dve_count.up("rw", q, "k_sq"))
            dve.wait_ge(*at("rw", q, "k_norm"))
            v.reciprocal(tmp[:, :], kk[:, :]).then_inc(dve_done, 1)
            dve.wait_ge(dve_done, dve_count.up())
            v.tensor_tensor(kk[:, :], k_new[:, :], tmp[:, :], ALU.mult).then_inc(dve_done, 1)
            dve.wait_ge(dve_done, dve_count.up())
            dve.wait_ge(*at("rw", q, "rate"))
            v.tensor_scalar(k_new[:, :], b_rate[:, :], col("k_a", q), kscale[:, 0, q:q + 1], ALU.mult, ALU.add).then_inc(dve_done, 1)
            dve.wait_ge(dve_done, dve_count.up())
            v.tensor_tensor(k_new[:, :], k_new[:, :], k_, ALU.mult).then_inc(dve_done, 1)
            dve.wait_ge(dve_done, dve_count.up())
            v.scalar_tensor_tensor(out=tmp[:, :], in0=r_, scalar=col("r_k", q), in1=k_new[:, :],
                                   op0=ALU.mult, op1=ALU.mult).then_inc(dve_done, 1)
            dve.wait_ge(dve_done, dve_count.up("rw", q, "rk"))
            v.tensor_tensor(b_rate[:, :], kk[:, :], b_rate[:, :], ALU.mult).then_inc(dve_done, 1)
            dve.wait_ge(dve_done, dve_count.up())
            dve.wait_ge(*at("rw", q, "exp_G"))
            v.scalar_tensor_tensor(out=a_cm[:, :], in0=kk[:, :], scalar=-1.0, in1=a_cm[:, :],
                                   op0=ALU.mult, op1=ALU.mult).then_inc(dve_done, 1)
            dve.wait_ge(dve_done, dve_count.up())
            v.tensor_tensor(b_cm[:, :], b_rate[:, :], k_cm[:, :], ALU.mult).then_inc(dve_done, 1)
            dve.wait_ge(dve_done, dve_count.up())
            v.tensor_tensor(be_cm[:, :], b_rate[:, :], ke_cm[:, :], ALU.mult).then_inc(dve_done, 1)
            dve.wait_ge(dve_done, dve_count.up())
            v.tensor_tensor(k_cm[:, :], k_new[:, :], k_cm[:, :], ALU.mult).then_inc(dve_done, 1)
            dve.wait_ge(dve_done, dve_count.up())
            v.tensor_tensor(ke_cm[:, :], k_new[:, :], ke_cm[:, :], ALU.mult).then_inc(dve_done, 1)
            dve.wait_ge(dve_done, dve_count.up())
            v.tensor_tensor(r_, r_, g_cm[:, :], ALU.mult).then_inc(dve_done, 1)
            dve.wait_ge(dve_done, dve_count.up("rw", q, "operands"))
            if q > 0:
                mod2_dve(dve, 2 * q - 1, 4)
            dve.wait_ge(*at("rw", q, "rk_sum"))
            v.tensor_tensor(k_, bank(3), v_, ALU.mult).then_inc(dve_done, 1)
            dve.wait_ge(dve_done, dve_count.up("rw", q, "bonus"))
            mod2_rows_dve(dve, 2 * q)

        def rwkv_unit_pe(pe, q):
            r_ = rkvg[:, q, :]
            mm = nc.tensor.matmul

            def products(e, b, lhs, rhs, name, *waits):
                for w in waits:
                    pe.wait_ge(*at(*w))
                for tt in range(TT):
                    ts = slice(tt * P, (tt + 1) * P)
                    ins = mm(bank(b, tt * P, (tt + 1) * P), lhs[half(e), ts], rhs[half(e), ts], start=True, stop=True)
                ins.then_inc(pe_done, 1)
                pe_count.up("rw", q, name, e)

            def turns(e, b, lhs, rhs, name, *waits, out=None, width=P):
                for w in waits:
                    pe.wait_ge(*at(*w))
                for tt in range(TT):
                    o = bank(b, tt * width, (tt + 1) * width) if out is None else out(tt)
                    ins = mm(o, lhs(tt), rhs(tt), start=True, stop=True)
                ins.then_inc(pe_done, 1)
                pe_count.up("rw", q, name, e)

            pe.wait_ge(*at("rw", q, "bonus"))
            pe.wait_ge(*at("rw", q, "tm", TT - 1))
            for e in range(2):
                b = 4 * e
                products(e, b + 0, a_cm, b_cm, "A")
                products(e, b + 1, b_cm, a_cm, "AT")
                products(e, b + 2, b_cm, r_, "RBT")
                products(e, b + 3, k_cm, r_, "RKT")
            for e in range(2):
                products(e, 4 * e, k_cm, a_cm, "AKT", ("rw", q, "Z0", e))
            for level in range(1, LEVELS + 1):
                last = level == LEVELS
                for e in range(2):
                    b = 4 * e
                    Z, ZT, U = unit["Z", e], unit["ZT", e], unit["U", e]
                    AL = unit["AL", e]
                    pe.wait_ge(*at("rw", q, "AT_copied", e))
                    turns(e, b + 1, lambda tt: AL[:, level % 2, tt, :], lambda tt: Z[:, tt, :], ("U", level),
                          ("rw", q, ("AL", level), e), ("rw", q, ("Z", level - 1), e))
                for e in range(2):
                    b = 4 * e
                    Z, ZT, U = unit["Z", e], unit["ZT", e], unit["U", e]
                    waits = [("rw", q, ("U_copied", level), e), ("rw", q, ("ZT", level - 1), e)]
                    if level == 1:
                        waits += [("rw", q, "RBT_masked", e), ("rw", q, "RKT_masked", e)]
                    if not last:
                        turns(e, b + 2, lambda tt: ZT[:, tt, :], lambda tt: U[:, tt, :], ("dZ", level), *waits)
                    turns(e, b + 3, lambda tt: U[:, tt, :], lambda tt: ZT[:, tt, :], ("dZT", level), *waits)
            vt = lambda tt, e: tm[:, tt, 3, half(e)]
            for e in range(2):
                turns(e, 4 * e, lambda tt: unit["AKT", e][:, tt, :], lambda tt: vt(tt, e), "AKV",
                      ("rw", q, "AKT_masked", e), width=HEAD)
            for e in range(2):
                b = 4 * e + 1
                ZT = unit["ZT", e]
                pe.wait_ge(*at("rw", q, "AKV_copied", e))
                pe.wait_ge(*at("rw", q, ("ZT", LEVELS), e))
                for tt in range(TT):
                    mm(bank(b, tt * P, tt * P + HEAD), ZT[:, tt, :], tm[:, tt, 0, half(e)], start=True, stop=True)
                    ins = mm(bank(b, tt * P + HEAD, (tt + 1) * P), ZT[:, tt, :], unit["AKV", e][:, tt, :],
                             start=True, stop=True)
                ins.then_inc(pe_done, 1)
                pe_count.up("rw", q, "W", e)
            for e in range(2):
                W, RBT, RKT = unit["W", e], unit["RBT", e], unit["RKT", e]
                turns(e, 2, lambda tt: W[:, tt, 0:HEAD], lambda tt: RBT[:, tt, :], "r_read",
                      ("rw", q, "W_copied", e), ("rw", q, ("Z", LEVELS - 1), 0), ("rw", q, ("Z", LEVELS - 1), 1),
                      out=lambda tt: psum[half(e), 2, tt * P:(tt + 1) * P])
                for tt in range(TT):
                    o = psum[half(e), 3, tt * P:(tt + 1) * P]
                    mm(o, W[:, tt, HEAD:P], RBT[:, tt, :], start=(tt == 0), stop=False, skip_group_check=True)
                    mm(o, vt(tt, e), RKT[:, tt, :], start=False, stop=False, skip_group_check=True)
                for odd in range(2):
                    rows = half(odd)
                    for tt in range(TT):
                        o = psum[half(e), 4 * odd, tt * HEAD:(tt + 1) * HEAD]
                        mm(o, W[rows, tt, 0:HEAD], tm[rows, tt, 1, half(e)], start=True, stop=True)
                        o = psum[half(e), 4 * odd, 256 + tt * HEAD:256 + (tt + 1) * HEAD]
                        mm(o, tm[rows, tt, 1, half(e)], W[rows, tt, HEAD:P], start=True, stop=False)
                        ins = mm(o, tm[rows, tt, 2, half(e)], tm[rows, tt, 3, half(e)], start=False, stop=True)
                ins.then_inc(pe_done, 1)
                pe_count.up("rw", q, "chunks", e)
            pe_count.mark("rw", q, "unit_mm")
            for c in range(NCHUNK):
                if c > 0:
                    pe.wait_ge(*at("rw", q, "state_added", c))
                else:
                    pe.wait_ge(*at("states_zero"))
                    pe.wait_ge(*at("rw", q, "r_read_copied"))
                ins = mm(bank(3, c * CHUNK, (c + 1) * CHUNK), states[:, c, :], r_read[:, c * CHUNK:(c + 1) * CHUNK],
                         start=False, stop=(c == NCHUNK - 1), skip_group_check=True)
                if c == NCHUNK - 1:
                    ins.then_inc(pe_done, 1)
                    pe_count.up("rw", q, "y")
                if c < NCHUNK - 1:
                    pe.wait_ge(*at("rw", q, "carry", c))
                    o = bank(7, c * HEAD, (c + 1) * HEAD)
                    for e in range(2):
                        ins = mm(o, carry[:, c, :], states[:, c, e * HEAD:(e + 1) * HEAD],
                                 start=(e == 0), stop=(e == 1))
                    ins.then_inc(pe_done, 1)
                    pe_count.up("rw", q, "state_mm", c)
                if c < MOD_BATCH:
                    mod2_pe(pe, 2 * q + 1, c, c + 1)
                if c == NCHUNK - 2:
                    mod2_turn_pe(pe, 2 * q, 1)

        def rwkv_unit_act(act, q):
            for e in range(2):
                act.wait_ge(*at("rw", q, "AT", e))
                nc.scalar.activation(unit["AT", e][:, :, :], tt4(bank(4 * e + 1)), ACT.Copy).then_inc(act_done, 1)
                act.wait_ge(act_done, act_count.up("rw", q, "AT_copied", e))
            for level in range(1, LEVELS + 1):
                for e in range(2):
                    act.wait_ge(*at("rw", q, ("U", level), e))
                    nc.scalar.activation(unit["U", e][:, :, :], tt4(bank(4 * e + 1)), ACT.Copy).then_inc(act_done, 1)
                    act.wait_ge(act_done, act_count.up("rw", q, ("U_copied", level), e))
            for e in range(2):
                act.wait_ge(*at("rw", q, "AKV", e))
                nc.scalar.activation(unit["AKV", e][:, :, :], tt4(bank(4 * e, 0, 256)), ACT.Copy).then_inc(act_done, 1)
                act.wait_ge(act_done, act_count.up("rw", q, "AKV_copied", e))
            for e in range(2):
                act.wait_ge(*at("rw", q, "W", e))
                nc.scalar.activation(unit["W", e][:, :, :], tt4(bank(4 * e + 1)), ACT.Copy).then_inc(act_done, 1)
                act.wait_ge(act_done, act_count.up("rw", q, "W_copied", e))
            act.wait_ge(*at("rw", q, "y"))
            nc.scalar.activation(rkvg[:, q, :], bank(3), ACT.Copy).then_inc(act_done, 1)
            act.wait_ge(act_done, act_count.up("rw", q, "y_copied"))

        def rwkv_unit_pool(pool, q):
            for level in range(1, LEVELS + 1):
                for e in range(2):
                    pool.wait_ge(*at("rw", q, "AT_copied", e))
                    if level > 2:
                        pool.wait_ge(*at("rw", q, ("U", level - 2), e))
                    elif q > 0:
                        pool.wait_ge(*at("rw", q - 1, "unit_mm"))
                    nc.gpsimd.tensor_tensor(unit["AL", e][:, level % 2, :, :], unit["AT", e][:, :, :],
                                            over(mask(f"level{level}"), TT), ALU.mult).then_inc(pool_done, 1)
                    pool.wait_ge(pool_done, pool_count.up("rw", q, ("AL", level), e))

        def rwkv_unit_dve(dve, q):
            v = nc.vector
            for e in range(2):
                b = 4 * e
                Z, ZT = unit["Z", e], unit["ZT", e]
                dve.wait_ge(*at("rw", q, "A", e))
                v.tensor_tensor(Z[:, :, :], tt4(bank(b)), over(mask("diag2_lower"), TT), ALU.mult).then_inc(dve_done, 1)
                dve.wait_ge(dve_done, dve_count.up())
                v.tensor_tensor(Z[:, :, :], Z[:, :, :], over(mask("ident"), TT), ALU.add).then_inc(dve_done, 1)
                dve.wait_ge(dve_done, dve_count.up("rw", q, "Z0", e))
                dve_count.mark("rw", q, ("Z", 0), e)
                dve.wait_ge(*at("rw", q, "AT_copied", e))
                v.tensor_tensor(ZT[:, :, :], unit["AT", e][:, :, :], over(mask("diag2_upper"), TT), ALU.mult).then_inc(dve_done, 1)
                dve.wait_ge(dve_done, dve_count.up())
                v.tensor_tensor(ZT[:, :, :], ZT[:, :, :], over(mask("ident"), TT), ALU.add).then_inc(dve_done, 1)
                dve.wait_ge(dve_done, dve_count.up("rw", q, ("ZT", 0), e))
            for e in range(2):
                b = 4 * e
                dve.wait_ge(*at("rw", q, "RKT", e))
                v.tensor_tensor(unit["RBT", e][:, :, :], tt4(bank(b + 2)), over(mask("incl_upper"), TT),
                                ALU.mult).then_inc(dve_done, 1)
                dve.wait_ge(dve_done, dve_count.up("rw", q, "RBT_masked", e))
                v.tensor_tensor(unit["RKT", e][:, :, :], tt4(bank(b + 3)), over(mask("incl_upper"), TT),
                                ALU.mult).then_inc(dve_done, 1)
                dve.wait_ge(dve_done, dve_count.up("rw", q, "RKT_masked", e))
                dve.wait_ge(*at("rw", q, "AKT", e))
                v.tensor_tensor(unit["AKT", e][:, :, :], tt4(bank(b)), over(mask("strict_upper"), TT),
                                ALU.mult).then_inc(dve_done, 1)
                dve.wait_ge(dve_done, dve_count.up("rw", q, "AKT_masked", e))
            for level in range(1, LEVELS + 1):
                for e in range(2):
                    b = 4 * e
                    Z, ZT = unit["Z", e], unit["ZT", e]
                    dve.wait_ge(*at("rw", q, ("dZT", level), e))
                    if level < LEVELS:
                        v.tensor_tensor(Z[:, :, :], tt4(bank(b + 2)), Z[:, :, :], ALU.add).then_inc(dve_done, 1)
                        dve.wait_ge(dve_done, dve_count.up("rw", q, ("Z", level), e))
                    v.tensor_tensor(ZT[:, :, :], tt4(bank(b + 3)), ZT[:, :, :], ALU.add).then_inc(dve_done, 1)
                    dve.wait_ge(dve_done, dve_count.up("rw", q, ("ZT", level), e))
            dve.wait_ge(*at("rw", q, "r_read", 1))
            v.tensor_tensor(r_read[:, :], bank(2), rkvg[:, q, :], ALU.add).then_inc(dve_done, 1)
            dve.wait_ge(dve_done, dve_count.up("rw", q, "r_read_copied"))
            dve.wait_ge(*at("rw", q, "chunks", 1))
            ends = g_cm[:, :].rearrange("p (c t) -> p c t", t=CHUNK)
            for c in range(NCHUNK):
                src = bank(4 * (c % 2), (c // 2) * HEAD, (c // 2 + 1) * HEAD)
                for e in range(2):
                    v.scalar_tensor_tensor(out=carry[half(e), c, half(e)], in0=mask("ident")[half(e), half(e)],
                                           scalar=ends[half(e), c, CHUNK - 1:CHUNK], in1=src[half(e), :],
                                           op0=ALU.mult, op1=ALU.add).then_inc(dve_done, 1)
                    dve.wait_ge(dve_done, dve_count.up("rw", q, "carry", c))
                if c == 0:
                    for odd in range(2):
                        v.tensor_copy(inject[:, odd:NCHUNK:2, :], tt4(bank(4 * odd, 256, 512))).then_inc(dve_done, 1)
                        dve.wait_ge(dve_done, dve_count.up())
            for c in range(NCHUNK - 1):
                dve.wait_ge(*at("rw", q, "state_mm", c))
                for e in range(2):
                    v.tensor_tensor(states[half(e), c + 1, half(e)], bank(7, c * HEAD, (c + 1) * HEAD)[half(e), :],
                                    inject[half(e), c, :], ALU.add).then_inc(dve_done, 1)
                    dve.wait_ge(dve_done, dve_count.up("rw", q, "state_added", c + 1))
            mod2_rows_dve(dve, 2 * q + 1)
            mod2_dve(dve, 2 * q, 1)

        def group_norm_pe(pe):
            mod2_turn_pe(pe, 2 * NPAIR - 1, 4)
            for q in range(NPAIR):
                pe.wait_ge(*at("rw", q, "y_copied"))
                nc.tensor.matmul(bank(2 * (q % 2)), mask("block_ones"), rkvg[:, q, :], start=True, stop=True).then_inc(pe_done, 1)
                pe_count.up("gn", q, "sum")
                pe.wait_ge(*at("gn", q, "sq"))
                nc.tensor.matmul(bank(2 * (q % 2) + 1), mask("block_ones"), tmp[:, :], start=True, stop=True).then_inc(pe_done, 1)
                pe_count.up("gn", q, "ss")

        def group_norm_act(act):
            for q in range(NPAIR):
                act.wait_ge(*at("gn", q, "ss"))
                nc.scalar.activation(kk[:, :], bank(2 * (q % 2) + 1), ACT.Sqrt, bias=eps[:, 1:2], scale=1.0 / HEAD).then_inc(act_done, 1)
                act.wait_ge(act_done, act_count.up("gn", q, "std"))
            for q in range(NPAIR):
                nc.scalar.activation(rkvg[:, 12 + q, :], rkvg[:, 12 + q, :], ACT.Silu).then_inc(act_done, 1)
                act.wait_ge(act_done, act_count.up("gn", q, "gate"))

        def group_norm_dve(dve):
            mod2_dve(dve, 2 * NPAIR - 1, 4)
            v = nc.vector
            for q in range(NPAIR):
                y = rkvg[:, q, :]
                dve.wait_ge(*at("gn", q, "sum"))
                v.scalar_tensor_tensor(out=y, in0=bank(2 * (q % 2)), scalar=-1.0 / HEAD, in1=y, op0=ALU.mult, op1=ALU.add).then_inc(dve_done, 1)
                dve.wait_ge(dve_done, dve_count.up())
                v.tensor_tensor(tmp[:, :], y, y, ALU.mult).then_inc(dve_done, 1)
                dve.wait_ge(dve_done, dve_count.up("gn", q, "sq"))
                dve.wait_ge(*at("gn", q, "std"))
                v.reciprocal(k_new[:, :], kk[:, :]).then_inc(dve_done, 1)
                dve.wait_ge(dve_done, dve_count.up())
                v.tensor_tensor(y, y, k_new[:, :], ALU.mult).then_inc(dve_done, 1)
                dve.wait_ge(dve_done, dve_count.up("gn", q, "normed"))
                v.tensor_scalar(y, y, col("gn_g", q), col("gn_b", q), ALU.mult, ALU.add).then_inc(dve_done, 1)
                dve.wait_ge(dve_done, dve_count.up())
                v.tensor_tensor(y, y, rkvg[:, 4 + q, :], ALU.add).then_inc(dve_done, 1)
                dve.wait_ge(dve_done, dve_count.up())
            for q in range(NPAIR):
                dve.wait_ge(*at("gn", q, "gate"))
                v.tensor_tensor(mixT[:, 4 + q, :], rkvg[:, q, :], rkvg[:, 12 + q, :], ALU.mult).then_inc(dve_done, 1)
                dve.wait_ge(dve_done, dve_count.up("mixT", 4 + q))

        rw.close()

        o1 = ExitStack()
        sq = sb(o1, "sq", [KD, T])
        mix_split = sb(o1, "mix_split", [2, KD, T])
        out_w = sb(o1, "out_w", [4, 2, HALF_SLOT])
        mix_w_act, _, mix_w_pool, mix_w_pe = split_weights("out_w", out_w, [("out", m) for m in range(KD)])
        stat = sb(o1, "stat", [2, T])

        def out_pe(pe):
            values = split_values(mix_split)
            for m in range(KD):
                if m >= 4:
                    pe.wait_ge(*at("residual", m - 4))
                for unit in range(2):
                    if m == 0:
                        pe.wait_ge(*at("mix_split", "rest", (unit + 1) * UNIT_K - 1))
                    mix_w_pe(pe, 2 * m + unit, bank(m % 4), values(unit), unit == 0, unit == 1)
                pe_count.mark("out", m)

        def out_act(act):
            for k in range(KD):
                split_act(act, "mix_split", mix_split, mixT, k)
                if k < 4:
                    mix_w_act(act, k)
            for u in range(4, 2 * KD):
                mix_w_act(act, u)

        def out_pool(pool):
            for u in range(2 * KD):
                mix_w_pool(pool, u)

        def out_dve(dve):
            for k in range(KD):
                split_dve(dve, "mix_split", mix_split, mixT, k)
            for m in range(KD):
                dve.wait_ge(*at("out", m))
                nc.vector.tensor_scalar(xT[:, m, :], xT[:, m, :], ALPHA_1, None, ALU.mult).then_inc(dve_done, 1)
                dve.wait_ge(dve_done, dve_count.up())
                nc.vector.scalar_tensor_tensor(out=xT[:, m, :], in0=bank(m % 4), scalar=ada[:, 2 * KD + m:2 * KD + m + 1],
                                               in1=xT[:, m, :], op0=ALU.mult, op1=ALU.add).then_inc(dve_done, 1)
                dve.wait_ge(dve_done, dve_count.up("residual", m))
                dve_count.mark("ln1", "z", m)

        ln1_pe, ln1_act, ln1_dve = layer_norm_cm("ln1", xT, T, sq, stat, lambda k: col("ln_g", k), lambda k: col("ln_b", k), eps[:, 0:1],
                            lambda k: [(xT[:, k, :], xT[:, k, :])])
        o1.close()
        first.close()

        def both(b):
            return flat((b + 1) * BANK - CTX, (b + 1) * BANK + T)

        def parts_of(b):
            return [(flat((b + 1) * BANK - CTX, (b + 1) * BANK), 0, CTX), (flat((b + 1) * BANK, (b + 1) * BANK + T), CTX, T)]

        layers = ExitStack()
        ctxT = sb(layers, "ctxT", [KD, CTX])
        NPD = 2 * PAIRS
        power = sb(layers, "power", [2, NPD, STEP + 1])
        b_factor = sb(layers, "b_factor", [2, NPD])
        decay8 = sb(layers, "decay8", [NPD])
        turn8 = sb(layers, "turn8", [2, NPD])
        dve_tmp = sb(layers, "dve_tmp", [2 * PAIRS // KE * (STEP + 1) * GS])
        lam = dve_tmp[:, 6 * NPD:9 * NPD].rearrange("p (k n) -> p k n", k=3)
        temp = [dve_tmp[:, i * NPD:(i + 1) * NPD] for i in range(6)]

        ml = ExitStack()
        h2 = sb(ml, "h2", [KD, TC])
        qn = sb(ml, "qn", [2, TC])
        ckv = sb(ml, "ckv", [TC])
        ckv_tm = sb(ml, "ckv_tm", [6, P])
        kr = sb(ml, "kr", [TC])
        gate2 = sb(ml, "gate2", [KE, TC])
        q_nope = sb(ml, "q_nope", [TC])
        q_abs = sb(ml, "q_abs", [2, TC])
        q_raw = sb(ml, "q_raw", [2, TC])
        q_pos = sb(ml, "q_pos", [2, T])
        o_lat = sb(ml, "o_lat", [TC])
        prob = sb(ml, "prob", [2, TC])
        pt_ctx = sb(ml, "pt_ctx", [2, CTX])
        pt_lat = sb(ml, "pt_lat", [6, T])
        sm = sb(ml, "sm", [3, 4])
        sq3, rms = q_abs, q_raw

        def mla_h_dve(dve):
            dve.wait_ge(ctx_loaded, 16)
            for k in range(KD):
                nc.vector.tensor_scalar(h2[:, k, 0:CTX], ctxT[:, k, :], mods[0][:, KD + k, 0:1], mods[0][:, k, 0:1],
                                        ALU.mult, ALU.add).then_inc(dve_done, 1)
                dve.wait_ge(dve_done, dve_count.up())
                nc.vector.tensor_scalar(h2[:, k, CTX:TC], xT[:, k, :], mods[0][:, KD + k, 1:2], mods[0][:, k, 1:2],
                                        ALU.mult, ALU.add).then_inc(dve_done, 1)
                dve.wait_ge(dve_done, dve_count.up("h2", k))

        def mla_in_pe(pe):
            for m in range(20):
                b = 2 * (m % 3)
                need_slot(pe, ("mla_in", m))
                if m >= 3:
                    pe.wait_ge(*at("mla_in", "evac", m - 3))
                for k in range(KD):
                    pe.wait_ge(*at("h2", k))
                for o, a, n in parts_of(b):
                    for k in range(KD):
                        ins = nc.tensor.matmul(o, tile_w(("mla_in", m), k), h2[:, k, a:a + n],
                                               start=(k == 0), stop=(k == KD - 1))
                ins.then_inc(pe_done, 1)
                pe_count.up("mla_in", "mm", m)
                pe_count.mark("free", slot_of[("mla_in", m)])
                if m == 6:
                    pe.wait_ge(*at("kv_sq"))
                    for o, a, n in parts_of(6):
                        ins = nc.tensor.matmul(o, mask("ones"), sq3[:, 0, a:a + n], start=True, stop=True)
                    ins.then_inc(pe_done, 1)
                    pe_count.up("kv_ss")
                if m == 9:
                    pe.wait_ge(*at("q_sq", 1))
                    pe.wait_ge(*at("kv_std"))
                    for o, a, n in parts_of(6):
                        for i in range(2):
                            ins = nc.tensor.matmul(o, mask("ones"), (sq3[:, 1, a:a + n], h2q[:, a:a + n])[i],
                                                   start=(i == 0), stop=(i == 1))
                    ins.then_inc(pe_done, 1)
                    pe_count.up("q_ss")
                if m == 12:
                    pe.wait_ge(*at("kr_rotated"))
                    pe.wait_ge(*at("q_std"))
                    nc.tensor.matmul(bank(6), mask("dup"), q_pos[:, 0, :], start=True, stop=True).then_inc(pe_done, 1)
                    pe_count.up("kr_sum")
                if m == 15:
                    pe.wait_ge(*at("ckv_normed"))
                    pe.wait_ge(*at("kr_copied"))
                    for i in range(6):
                        ins = nc.tensor.transpose(bank(6 + i // 3, (i % 3) * P, (i % 3 + 1) * P),
                                                  ckv[:, i * P:(i + 1) * P], mask("ident"))
                    ins.then_inc(pe_done, 1)
                    pe_count.up("ckv_turned")

        h2q = prob[:, 0, :]

        def s5_dt_act(act):
            act.wait_ge(lam_loaded, 16)
            nc.scalar.activation(lam[:, 2, :], lam[:, 2, :], ACT.Exp).then_inc(act_done, 1)
            act.wait_ge(act_done, act_count.up("s5", "dt"))

        def s5_setup_act(act):
            act.wait_ge(*at("s5", "exponent"))
            nc.scalar.activation(temp[3], temp[0], ACT.Exp).then_inc(act_done, 1)
            act.wait_ge(act_done, act_count.up())
            nc.scalar.activation(decay8[:, :], temp[0], ACT.Exp, scale=float(STEP)).then_inc(act_done, 1)
            act.wait_ge(act_done, act_count.up("s5", "size"))
            act.wait_ge(*at("s5", "angle"))
            nc.scalar.activation(turn8[:, 1, :], temp[1], ACT.Sin).then_inc(act_done, 1)
            act.wait_ge(act_done, act_count.up())
            nc.scalar.activation(turn8[:, 0, :], temp[2], ACT.Sin).then_inc(act_done, 1)
            act.wait_ge(act_done, act_count.up("s5", "sincos"))

        def s5_setup_dve(dve):
            v = nc.vector
            re, im, dt = (lam[:, i, :] for i in range(3))
            mul, add_, sub = ALU.mult, ALU.add, ALU.subtract
            def tt(o, a, b, op):
                v.tensor_tensor(o, a, b, op).then_inc(dve_done, 1)
                dve.wait_ge(dve_done, dve_count.up())

            dve.wait_ge(*at("s5", "dt"))
            v.tensor_scalar(re, re, -1e-4, None, ALU.min).then_inc(dve_done, 1)
            dve.wait_ge(dve_done, dve_count.up())
            tt(temp[0], re, dt, mul)
            dve_count.mark("s5", "exponent")
            tt(temp[1], im, dt, mul)
            magic = 1.5 * 2 ** 23
            v.tensor_scalar(temp[2], temp[1], 1 / (2 * math.pi), magic, mul, add_).then_inc(dve_done, 1)
            dve.wait_ge(dve_done, dve_count.up())
            v.tensor_scalar(temp[2], temp[2], magic, None, sub).then_inc(dve_done, 1)
            dve.wait_ge(dve_done, dve_count.up())
            rest = 2 * math.pi
            for part in (6.28125, 0.0019350051879882812):
                v.scalar_tensor_tensor(out=temp[1], in0=temp[2], scalar=-part, in1=temp[1], op0=mul, op1=add_).then_inc(dve_done, 1)
                dve.wait_ge(dve_done, dve_count.up())
                rest -= part
            v.scalar_tensor_tensor(out=temp[1], in0=temp[2], scalar=-rest, in1=temp[1], op0=mul, op1=add_).then_inc(dve_done, 1)
            dve.wait_ge(dve_done, dve_count.up())
            v.tensor_scalar(temp[1], temp[1], 3.1415925, -3.1415925, ALU.min, ALU.max).then_inc(dve_done, 1)
            dve.wait_ge(dve_done, dve_count.up())
            v.scalar_tensor_tensor(out=temp[2], in0=temp[1], scalar=-1.0, in1=temp[1], op0=mul, op1=ALU.max).then_inc(dve_done, 1)
            dve.wait_ge(dve_done, dve_count.up())
            v.tensor_scalar(temp[2], temp[2], -1.0, math.pi / 2, mul, add_).then_inc(dve_done, 1)
            dve.wait_ge(dve_done, dve_count.up("s5", "angle"))
            dve.wait_ge(*at("s5", "size"))
            dve.wait_ge(*at("s5", "sincos"))
            lr, li = temp[4], temp[5]
            tt(lr, temp[3], turn8[:, 0, :], mul)
            tt(li, temp[3], turn8[:, 1, :], mul)
            tt(temp[0], re, re, mul)
            tt(temp[1], im, im, mul)
            tt(temp[0], temp[0], temp[1], add_)
            v.reciprocal(temp[0], temp[0]).then_inc(dve_done, 1)
            dve.wait_ge(dve_done, dve_count.up())
            v.tensor_scalar(temp[1], lr, -1.0, None, add_).then_inc(dve_done, 1)
            dve.wait_ge(dve_done, dve_count.up())
            tt(temp[2], temp[1], re, mul)
            tt(temp[3], li, im, mul)
            tt(temp[2], temp[2], temp[3], add_)
            tt(b_factor[:, 0, :], temp[2], temp[0], mul)
            tt(temp[2], li, re, mul)
            tt(temp[3], temp[1], im, mul)
            tt(temp[2], temp[2], temp[3], sub)
            tt(b_factor[:, 1, :], temp[2], temp[0], mul)
            def power_at(ri, i):
                p4 = power[:, ri, :, :].rearrange("p (g d) i -> p g d i", d=2)
                return p4[:, :, 0, i], p4[:, :, 1, STEP - i]
            two = lambda ap: (ap.rearrange("p (g d) -> p g d", d=2)[:, :, 0], ap.rearrange("p (g d) -> p g d", d=2)[:, :, 1])
            for d in range(2):
                v.memset(power_at(0, 0)[d], 1.0).then_inc(dve_done, 1)
                dve.wait_ge(dve_done, dve_count.up())
                v.memset(power_at(1, 0)[d], 0.0).then_inc(dve_done, 1)
                dve.wait_ge(dve_done, dve_count.up())
                v.tensor_copy(power_at(0, 1)[d], two(lr)[d]).then_inc(dve_done, 1)
                dve.wait_ge(dve_done, dve_count.up())
                v.tensor_copy(power_at(1, 1)[d], two(li)[d]).then_inc(dve_done, 1)
                dve.wait_ge(dve_done, dve_count.up())
                for i in range(2, STEP + 1):
                    a, b = power_at(0, i - 1)[d], power_at(1, i - 1)[d]
                    x, y = two(temp[0])[d], two(temp[1])[d]
                    tt(x, a, two(lr)[d], mul)
                    tt(y, b, two(li)[d], mul)
                    tt(power_at(0, i)[d], x, y, sub)
                    tt(x, a, two(li)[d], mul)
                    tt(y, b, two(lr)[d], mul)
                    tt(power_at(1, i)[d], x, y, add_)
            for _ in range(3):
                c, s = turn8[:, 0, :], turn8[:, 1, :]
                tt(temp[0], c, c, mul)
                tt(temp[1], s, s, mul)
                tt(temp[2], c, s, mul)
                tt(c, temp[0], temp[1], sub)
                v.tensor_scalar(s, temp[2], 2.0, None, mul).then_inc(dve_done, 1)
                dve.wait_ge(dve_done, dve_count.up())
            dve_count.mark("s5", "parameters")

        def mla_in_act(act):
            for m in range(20):
                act.wait_ge(*at("mla_in", "mm", m))
                src = both(2 * (m % 3))
                if m < 2:
                    nc.scalar.activation(qn[:, m, :], src, ACT.Copy).then_inc(act_done, 1)
                    act.wait_ge(act_done, act_count.up("mla_in", "evac", m))
                    if m == 0:
                        s5_setup_act(act)
                elif m == 2:
                    nc.scalar.activation(ckv[:, :], src, ACT.Copy).then_inc(act_done, 1)
                    act.wait_ge(act_done, act_count.up("mla_in", "evac", m))
                elif m == 3:
                    nc.scalar.activation(q_nope[:, :], src, ACT.Copy).then_inc(act_done, 1)
                    act.wait_ge(act_done, act_count.up("mla_in", "evac", m))
                    nc.scalar.activation(sq3[:, 0, :], ckv[:, :], ACT.Square).then_inc(act_done, 1)
                    act.wait_ge(act_done, act_count.up("kv_sq"))
                    nc.scalar.activation(sq3[:, 1, :], qn[:, 0, :], ACT.Square).then_inc(act_done, 1)
                    act.wait_ge(act_done, act_count.up("q_sq", 0))
                    nc.scalar.activation(h2q, qn[:, 1, :], ACT.Square).then_inc(act_done, 1)
                    act.wait_ge(act_done, act_count.up("q_sq", 1))
                else:
                    nc.scalar.activation(gate2[:, m - 4, :], src, ACT.Silu).then_inc(act_done, 1)
                    act.wait_ge(act_done, act_count.up("mla_in", "evac", m))
                if m == 9:
                    act.wait_ge(*at("kv_ss"))
                    nc.scalar.activation(rms[:, 0, :], both(6), ACT.Sqrt, bias=eps[:, 2:3], scale=1.0 / KV_RANK).then_inc(act_done, 1)
                    act.wait_ge(act_done, act_count.up("kv_std"))
                    act.wait_ge(*at("q_ss"))
                    nc.scalar.activation(rms[:, 1, :], both(6), ACT.Sqrt, bias=eps[:, 2:3], scale=1.0 / Q_RANK).then_inc(act_done, 1)
                    act.wait_ge(act_done, act_count.up("q_std"))

        def mla_in_dve(dve):
            v = nc.vector
            dve.wait_ge(*at("mla_in", "evac", 3))
            v.tensor_tensor(q_pos[:, 0, :], q_nope[:, CTX:TC], rope, ALU.mult).then_inc(dve_done, 1)
            dve.wait_ge(dve_done, dve_count.up("kr_rotated"))
            v.tensor_copy(kr[0:64, 0:CTX], q_nope[0:64, 0:CTX]).then_inc(dve_done, 1)
            dve.wait_ge(dve_done, dve_count.up())
            v.memset(kr[64:128, 0:CTX], 0.0).then_inc(dve_done, 1)
            dve.wait_ge(dve_done, dve_count.up())
            dve.wait_ge(*at("kv_std"))
            v.reciprocal(o_lat[:, :], rms[:, 0, :]).then_inc(dve_done, 1)
            dve.wait_ge(dve_done, dve_count.up())
            v.scalar_tensor_tensor(out=ckv[:, :], in0=ckv[:, :], scalar=col("kv_norm", 0), in1=o_lat[:, :],
                                   op0=ALU.mult, op1=ALU.mult).then_inc(dve_done, 1)
            dve.wait_ge(dve_done, dve_count.up("ckv_normed"))
            dve.wait_ge(*at("q_std"))
            v.reciprocal(o_lat[:, :], rms[:, 1, :]).then_inc(dve_done, 1)
            dve.wait_ge(dve_done, dve_count.up())
            for i in range(2):
                v.scalar_tensor_tensor(out=qn[:, i, :], in0=qn[:, i, :], scalar=col("q_norm", i), in1=o_lat[:, :],
                                       op0=ALU.mult, op1=ALU.mult).then_inc(dve_done, 1)
                dve.wait_ge(dve_done, dve_count.up("qn"))
            dve.wait_ge(*at("kr_sum"))
            v.tensor_copy(kr[:, CTX:TC], bank(6)).then_inc(dve_done, 1)
            dve.wait_ge(dve_done, dve_count.up("kr_copied"))
            dve.wait_ge(*at("ckv_turned"))
            v.tensor_copy(ckv_tm[:, :, :].rearrange("p (b k) c -> p b k c", b=2),
                          psum[:, 6:8, 0:3 * P].rearrange("p b (k c) -> p b k c", k=3)).then_inc(dve_done, 1)
            dve.wait_ge(dve_done, dve_count.up("ckv_tm"))


        UNITS = 6

        def prob_of(n):
            return (prob[:, 0, :], prob[:, 1, :], dve_tmp[:, 0:TC])[n % 3]

        def queries(h, u):
            if u < 2:
                return slice(u * P, (u + 1) * P), q_raw[:, h % 2, u * P:(u + 1) * P]
            return slice(u * P, (u + 1) * P), q_pos[:, h % 2, (u - 2) * P:(u - 1) * P]

        def head_pe(pe, h):
            mm = nc.tensor.matmul

            def scores(u):
                n = UNITS * h + u
                b = 2 + 2 * (n % 2)
                if n >= 2:
                    pe.wait_ge(*at("exp", n - 2))
                pe.wait_ge(*at("q_raw", h))
                if u >= 2:
                    pe.wait_ge(*at("q_pos", h))
                cs, rp = queries(h, u)
                keys = parts_of(b)[:1] if u < 2 else parts_of(b)
                for i, (o, a, m) in enumerate(keys):
                    mm(o, q_abs[:, h % 2, cs], ckv[:, a:a + m], start=True, stop=False)
                    r = q_raw[:, h % 2, cs] if i == 0 else rp
                    ins = mm(o, r, kr[:, a:a + m], start=False, stop=True)
                ins.then_inc(pe_done, 1)
                pe_count.up("scores", n)

            def turn(n):
                u = n % UNITS
                if n >= 1:
                    pe.wait_ge(*at("pt", n - 1))
                pe.wait_ge(*at("normed", n))
                for k in range(2 if u < 2 else 6):
                    ins = nc.tensor.transpose(bank(6 + k // 3, (k % 3) * P, (k % 3 + 1) * P),
                                              prob_of(n)[:, k * P:(k + 1) * P], mask("ident"))
                ins.then_inc(pe_done, 1)
                pe_count.up("turned", n)

            def values(hh):
                pe.wait_ge(*at("pt", UNITS * hh + 5))
                if hh + 1 < HEADS:
                    pe.wait_ge(*at("q_raw", hh + 1))
                for o, pt, kt in ((both(0)[:, 0:CTX], pt_ctx, 2), (bank(1), pt_lat, 6)):
                    for k in range(kt):
                        ins = mm(o, ckv_tm[:, k, :], pt[:, k, :], start=(k == 0), stop=(k == kt - 1))
                ins.then_inc(pe_done, 1)
                pe_count.up("values", hh)

            def up_values(hh):
                pe.wait_ge(*at("o_lat", hh))
                for o, a, n in parts_of(0):
                    ins = mm(o, slot(("head", hh))[:, 640:768], o_lat[:, a:a + n], start=True, stop=True)
                ins.then_inc(pe_done, 1)
                pe_count.up("up_values", hh)
                pe_count.mark("free", slot_of[("head", hh)])

            def project(hh, what):
                if hh >= HEADS:
                    return
                w = slot(("head", hh))
                if what == "nope":
                    need_slot(pe, ("head", hh))
                    if hh == 0:
                        pe.wait_ge(*at("qn"))
                        pe.wait_ge(*at("ckv_tm"))
                        pe.wait_ge(*at("mla_in", "evac", 19))
                    if hh >= 2:
                        pe.wait_ge(*at("gated", hh - 2))
                if what == "abs":
                    pe.wait_ge(*at("q_nope", hh))
                if what == "rope":
                    pe.wait_ge(*at("q_abs", hh))
                for o, a, n in parts_of(0):
                    if what == "abs":
                        ins = mm(o, w[:, 512:640], q_nope[:, a:a + n], start=True, stop=True)
                    else:
                        c = 0 if what == "nope" else P
                        for k in range(2):
                            ins = mm(o, w[:, k * 256 + c:k * 256 + c + P], qn[:, k, a:a + n], start=(k == 0), stop=(k == 1))
                ins.then_inc(pe_done, 1)
                pe_count.up("proj", what, hh)

            if h < 0:
                for what in ("nope", "abs", "rope"):
                    project(0, what)
                return
            if h == HEADS:
                turn(UNITS * h - 2)
                turn(UNITS * h - 1)
                values(h - 1)
                up_values(h - 1)
                return
            for u in range(UNITS):
                n = UNITS * h + u
                if u == 4:
                    project(h + 1, "nope")
                scores(u)
                if u == 2 and h > 0:
                    values(h - 1)
                if u == 3 and h > 0:
                    up_values(h - 1)
                if u == 4:
                    project(h + 1, "abs")
                if u == 5:
                    project(h + 1, "rope")
                if n >= 2:
                    turn(n - 2)

        def softmax_dve(dve, n):
            v = nc.vector
            b = 2 + 2 * (n % 2)
            u = n % UNITS
            keys = CTX if u < 2 else TC
            dve.wait_ge(*at("scores", n))
            v.tensor_reduce(sm[:, n % 3, 0:1], both(b)[:, 0:keys], AX.X, ALU.max).then_inc(dve_done, 1)
            dve.wait_ge(dve_done, dve_count.up())
            v.tensor_scalar(sm[:, n % 3, 1:2], sm[:, n % 3, 0:1], -SOFTMAX_SCALE, None, ALU.mult).then_inc(dve_done, 1)
            dve.wait_ge(dve_done, dve_count.up("max", n))

        def normalize_dve(dve, n):
            v = nc.vector
            keys = CTX if n % UNITS < 2 else TC
            dve.wait_ge(*at("exp", n))
            v.reciprocal(sm[:, n % 3, 3:4], sm[:, n % 3, 2:3]).then_inc(dve_done, 1)
            dve.wait_ge(dve_done, dve_count.up())
            v.tensor_scalar(prob_of(n)[:, 0:keys], prob_of(n)[:, 0:keys], sm[:, n % 3, 3:4], None, ALU.mult).then_inc(dve_done, 1)
            dve.wait_ge(dve_done, dve_count.up("normed", n))

        def exp_act(act, n):
            b = 2 + 2 * (n % 2)
            keys = CTX if n % UNITS < 2 else TC
            act.wait_ge(*at("max", n))
            if n >= 3:
                act.wait_ge(*at("turned", n - 3))
            nc.scalar.activation(prob_of(n)[:, 0:keys], both(b)[:, 0:keys], ACT.Exp, bias=sm[:, n % 3, 1:2],
                                 scale=SOFTMAX_SCALE, accum_out=sm[:, n % 3, 2:3]).then_inc(act_done, 1)
            act.wait_ge(act_done, act_count.up("exp", n))

        def pt_act(act, n):
            u = n % UNITS
            act.wait_ge(*at("turned", n))
            if u == 0 and n > 0:
                act.wait_ge(*at("values", n // UNITS - 1))
            if u < 2:
                nc.scalar.activation(pt_ctx[:, :, u * P:(u + 1) * P],
                                     bank(6, 0, 2 * P).rearrange("p (k c) -> p k c", k=2), ACT.Copy).then_inc(act_done, 1)
                act.wait_ge(act_done, act_count.up("pt", n))
            else:
                dst = pt_lat[:, :, (u - 2) * P:(u - 1) * P].rearrange("p (b k) c -> p b k c", b=2)
                nc.scalar.activation(dst, psum[:, 6:8, 0:3 * P].rearrange("p b (k c) -> p b k c", k=3),
                                     ACT.Copy).then_inc(act_done, 1)
                act.wait_ge(act_done, act_count.up("pt", n))

        def proj_act(act, what, h):
            if h >= HEADS:
                return
            act.wait_ge(*at("proj", what, h))
            if what == "nope":
                nc.scalar.activation(q_nope[:, :], both(0), ACT.Copy).then_inc(act_done, 1)
                act.wait_ge(act_done, act_count.up("q_nope", h))
            elif what == "abs":
                nc.scalar.activation(q_abs[:, h % 2, :], both(0), ACT.Copy).then_inc(act_done, 1)
                act.wait_ge(act_done, act_count.up("q_abs", h))
            else:
                nc.scalar.activation(q_raw[:, h % 2, :], both(0), ACT.Copy).then_inc(act_done, 1)
                act.wait_ge(act_done, act_count.up("q_raw", h))

        def head_act(act, h):
            if h < 0:
                for what in ("nope", "abs", "rope"):
                    proj_act(act, what, 0)
                return
            if h == HEADS:
                pt_act(act, UNITS * h - 2)
                pt_act(act, UNITS * h - 1)
                o_lat_act(act, h - 1)
                return
            for u in range(UNITS):
                n = UNITS * h + u
                if u == 4:
                    proj_act(act, "nope", h + 1)
                exp_act(act, n)
                if u == 2 and h > 0:
                    o_lat_act(act, h - 1)
                if u == 4:
                    proj_act(act, "abs", h + 1)
                if u == 5:
                    proj_act(act, "rope", h + 1)
                if n >= 2:
                    pt_act(act, n - 2)

        def o_lat_act(act, h):
            act.wait_ge(*at("values", h))
            nc.scalar.activation(o_lat[:, :], both(0), ACT.Copy).then_inc(act_done, 1)
            act.wait_ge(act_done, act_count.up("o_lat", h))

        def head_dve(dve, h):
            def q_pos_of(hh):
                dve.wait_ge(*at("q_raw", hh))
                nc.vector.tensor_tensor(q_pos[:, hh % 2, :], q_raw[:, hh % 2, CTX:TC], rope, ALU.mult).then_inc(dve_done, 1)
                dve.wait_ge(dve_done, dve_count.up("q_pos", hh))

            def gated(hh):
                dve.wait_ge(*at("up_values", hh))
                nc.vector.tensor_tensor(gate2[:, hh, :], both(0), gate2[:, hh, :], ALU.mult).then_inc(dve_done, 1)
                dve.wait_ge(dve_done, dve_count.up("gated", hh))

            if h < 0:
                q_pos_of(0)
                return
            if h == HEADS:
                normalize_dve(dve, UNITS * h - 1)
                gated(h - 1)
                return
            for u in range(UNITS):
                n = UNITS * h + u
                softmax_dve(dve, n)
                if u == 0 and h > 0:
                    q_pos_of(h)
                if n > 0:
                    normalize_dve(dve, n - 1)
                if u == 3 and h > 0:
                    gated(h - 1)

        def mla_out_pe(pe):
            for m in range(KD):
                b = 2 * (m % 2)
                for i in range(2):
                    need_slot(pe, ("mla_out", 2 * m + i))
                if m >= 2:
                    pe.wait_ge(*at("residual2", m - 2))
                for o, a, n in parts_of(b):
                    for k in range(KE):
                        ins = nc.tensor.matmul(o, tile_w(("mla_out", 2 * m + k // KD), k % KD), gate2[:, k, a:a + n],
                                               start=(k == 0), stop=(k == KE - 1))
                ins.then_inc(pe_done, 1)
                pe_count.up("mla_out", m)
                for i in range(2):
                    pe_count.mark("free", slot_of[("mla_out", 2 * m + i)])

        def mla_out_dve(dve):
            v = nc.vector
            for m in range(KD):
                dve.wait_ge(*at("mla_out", m))
                for i, (src, (o, a, n)) in enumerate(zip((ctxT, xT), parts_of(2 * (m % 2)))):
                    v.tensor_scalar(h2[:, m, a:a + n], src[:, m, :], ALPHA_2, None, ALU.mult).then_inc(dve_done, 1)
                    dve.wait_ge(dve_done, dve_count.up())
                    v.scalar_tensor_tensor(out=h2[:, m, a:a + n], in0=o, scalar=mods[0][:, 2 * KD + m, i:i + 1],
                                           in1=h2[:, m, a:a + n], op0=ALU.mult, op1=ALU.add).then_inc(dve_done, 1)
                    dve.wait_ge(dve_done, dve_count.up("residual2", m))
                dve_count.mark("ln2", "z", m)

        sq2 = gate2[:, 0:KD, :]
        ln2_pe, ln2_act, ln2_dve = layer_norm_cm("ln2", h2, TC, sq2, q_raw, lambda k: col("ln_g_20", k), lambda k: col("ln_b_20", k),
                            eps[:, 2:3],
                            lambda k: [(ctxT[:, k, :], h2[:, k, 0:CTX]), (xT[:, k, :], h2[:, k, CTX:TC])])

        def ln2_after_gates_act(act):
            act.wait_ge(*at("mla_out", KD - 1))
            ln2_act(act)

        ml.close()

        h3 = sb(layers, "h3", [KD, STEP, C_ALL])
        yT = sb(layers, "yT", [KE, T])
        s5 = ExitStack()
        TILE_PAIRS = PAIRS // KE
        TPD = 2 * TILE_PAIRS
        bc = sb(s5, "bc", [4, TPD, GS])
        b_bar = sb(s5, "b_bar", [2, 2, TPD, GS])
        b_bar_split = sb(s5, "b_bar_split", [2, TPD, 2, GS])
        c_pow = sb(s5, "c_pow", [2, 2, TPD, STEP + 1, GS])
        b_pow = sb(s5, "b_pow", [2, 2, TPD, STEP, GS])
        pool_tmp = sb(s5, "pool_tmp", [512])
        table = sb(s5, "table", [2, 2, TPD, C_ALL])
        b_pow_t = sb(s5, "b_pow_t", [2, 4, P])
        u_t = sb(s5, "u_t", [2, 2, 2, C_ALL])
        x_in = sb(s5, "x_in", [2, 2, 2, C_LAT])
        lag_m = sb(s5, "lag_m", [2, 2 * TILE_PAIRS, P])
        y_tm = sb(s5, "y_tm", [STEP, P])
        skip = sb(s5, "skip", [PAIRS])
        eye = sb(s5, "eye", [GS])
        u_tm = ctxT[:, :, :].rearrange("p k t -> p (k t)").rearrange("p (b g s i) -> p b g s i", b=2, s=STEP, i=GS)
        b_bar = const[:, N_CONST - 2 * TPD * GS:N_CONST].rearrange("p (r t i) -> p r t i", r=2, i=GS)
        lags = const[:, 4 * P:4 * P + 2 * 4 * 240].rearrange("p (b g n) -> p b g n", b=2, n=240)
        mod_c, mod_s, zs = (dve_tmp[:, i * 4 * C_ALL:(i + 1) * 4 * C_ALL].rearrange("p (d r c) -> p d r c", d=2, r=2)
                            for i in range(3))

        def s5_start_dve(dve):
            v = nc.vector
            for k in range(KD):
                v.tensor_scalar(h3[:, k, :, 0:C_CTX], ctxT[:, k, :].rearrange("p (c s) -> p s c", s=STEP),
                                mods[1][:, KD + k, 0:1], mods[1][:, k, 0:1], ALU.mult, ALU.add).then_inc(dve_done, 1)
                dve.wait_ge(dve_done, dve_count.up())
                v.tensor_scalar(h3[:, k, :, C_CTX:C_ALL], xT[:, k, :].rearrange("p (c s) -> p s c", s=STEP),
                                mods[1][:, KD + k, 1:2], mods[1][:, k, 1:2], ALU.mult, ALU.add).then_inc(dve_done, 1)
                dve.wait_ge(dve_done, dve_count.up("h3", k))
            dve.wait_ge(small_loaded, 48)
            v.tensor_tensor(eye[0:2 * GS, :], mask("ident")[0:2 * GS, 0:GS], mask("ident")[0:2 * GS, GS:2 * GS],
                            ALU.add).then_inc(dve_done, 1)
            dve.wait_ge(dve_done, dve_count.up())


        def tile_cols(m):
            return slice(m * TPD, (m + 1) * TPD)

        def b_bar_pool(pool, m):
            def tt(o, a, b, op, *key):
                nc.gpsimd.tensor_tensor(o, a, b, op).then_inc(pool_done, 1)
                pool.wait_ge(pool_done, pool_count.up(*key))

            if m == 0:
                pool.wait_ge(*at("s5", "parameters"))
            pool.wait_ge(table_loaded, 16 * (m + 1))
            if m >= 1:
                pool.wait_ge(*at("s5", "b_split", m - 1))
            fr, fi = (along(b_factor[:, i, tile_cols(m)], GS) for i in range(2))
            small = pool_tmp[:, 0:TPD * GS].rearrange("p (t i) -> p t i", i=GS)
            for ri, op in ((0, ALU.subtract), (1, ALU.add)):
                tt(b_bar[:, ri, :, :], bc[:, ri, :, :], fr, ALU.mult)
                tt(small, bc[:, 1 - ri, :, :], fi, ALU.mult)
                tt(b_bar[:, ri, :, :], b_bar[:, ri, :, :], small, op, "s5", "b_bar", m)

        def b_pow_pool(pool, m):
            def tt(o, a, b, op, *key):
                nc.gpsimd.tensor_tensor(o, a, b, op).then_inc(pool_done, 1)
                pool.wait_ge(pool_done, pool_count.up(*key))

            if m >= 2:
                pool.wait_ge(*at("s5", "b_turned", TILE_PAIRS * (m - 1) - 1))
            shape = [P, TILE_PAIRS, STEP, GS]
            part = pool_tmp[:, :].rearrange("p (t s i) -> p t s i", t=TILE_PAIRS, s=STEP)
            for d in range(2):
                idx = slice(7, None, -1) if d == 0 else slice(8, 0, -1)
                pr, pi = (power[:, i, m * TPD + d:(m + 1) * TPD:2, idx].unsqueeze(3).broadcast_to(shape) for i in range(2))
                br, bi = (b_bar[:, i, d::2, :].unsqueeze(2).broadcast_to(shape) for i in range(2))
                o_re, o_im = (b_pow[:, m % 2, i, d::2, :, :] for i in range(2))
                tt(o_re, br, pr, ALU.mult)
                tt(part, bi, pi, ALU.mult)
                tt(o_re, o_re, part, ALU.subtract)
                tt(o_im, br, pi, ALU.mult)
                tt(part, bi, pr, ALU.mult)
                tt(o_im, o_im, part, ALU.add, "s5", "b_pow", m)

        def c_pow_dve(dve, m, i):
            if m >= KE:
                return
            if i == 0:
                dve.wait_ge(table_loaded, 16 * (m + 1))
                if m >= 2:
                    dve.wait_ge(*at("s5", "y", TILE_PAIRS * (m - 1) - 1))
            n = STEP + 1
            shape = [P, TPD, n, GS]
            part = dve_tmp[:, :].rearrange("p (t s i) -> p t s i", t=TPD, s=n)
            pr, pi = (power[:, r, tile_cols(m), :].unsqueeze(3).broadcast_to(shape) for r in range(2))
            cr, ci = (bc[:, 2 + r, :, :].unsqueeze(2).broadcast_to(shape) for r in range(2))
            re, im = (c_pow[:, m % 2, r, :, :, :] for r in range(2))
            if i < 5:
                o, a, b, op = ((part, ci, pi, ALU.mult), (re, cr, pr, ALU.mult), (re, re, part, ALU.subtract),
                               (part, ci, pr, ALU.mult), (im, cr, pi, ALU.mult))[i]
                nc.vector.tensor_tensor(o, a, b, op).then_inc(dve_done, 1)
                dve.wait_ge(dve_done, dve_count.up())
            else:
                nc.vector.scalar_tensor_tensor(out=im, in0=im, scalar=-1.0, in1=part, op0=ALU.mult,
                                               op1=ALU.subtract).then_inc(dve_done, 1)
                dve.wait_ge(dve_done, dve_count.up("s5", "c_pow", m))

        def table_level(engine, e, done_sem, count, m, n, tmp):
            c, s = table[:, m % 2, 0, :, :], table[:, m % 2, 1, :, :]
            w = min(n, C_ALL - 1 - n)
            cn = c[:, :, n:n + 1].broadcast_to([P, TPD, w])
            sn = s[:, :, n:n + 1].broadcast_to([P, TPD, w])
            x, y = (tmp[:, i * TPD * w:(i + 1) * TPD * w].rearrange("p (t n) -> p t n", n=w) for i in range(2))
            for o, a, b, op in ((x, c[:, :, 1:1 + w], cn, ALU.mult), (y, s[:, :, 1:1 + w], sn, ALU.mult),
                                (c[:, :, n + 1:n + 1 + w], x, y, ALU.subtract),
                                (x, s[:, :, 1:1 + w], cn, ALU.mult), (y, c[:, :, 1:1 + w], sn, ALU.mult),
                                (s[:, :, n + 1:n + 1 + w], x, y, ALU.add)):
                e.tensor_tensor(o, a, b, op).then_inc(done_sem, 1)
                engine.wait_ge(done_sem, count.up())
            count.mark("s5", "table", m, n)

        def table_pool(pool, m):
            if m >= 2:
                pool.wait_ge(*at("s5", "x_in", TILE_PAIRS * (m - 1) - 1))
            nc.gpsimd.memset(table[:, m % 2, 0, :, 0:1], 1.0).then_inc(pool_done, 1)
            pool.wait_ge(pool_done, pool_count.up())
            nc.gpsimd.memset(table[:, m % 2, 1, :, 0:1], 0.0).then_inc(pool_done, 1)
            pool.wait_ge(pool_done, pool_count.up())
            nc.gpsimd.tensor_copy(table[:, m % 2, :, :, 1], turn8[:, :, tile_cols(m)]).then_inc(pool_done, 1)
            pool.wait_ge(pool_done, pool_count.up())
            for level in range(6):
                table_level(pool, nc.gpsimd, pool_done, pool_count, m, 2 ** level, pool_tmp)

        def table_dve(dve, m):
            if m >= KE:
                return
            dve.wait_ge(*at("s5", "table", m, 32))
            table_level(dve, nc.vector, dve_done, dve_count, m, 64, dve_tmp)

        def u_project_pe(pe, m, s):
            if m >= KE:
                return
            need_slot(pe, ("s5_in", m))
            if s == 0 and m == 0:
                pe.wait_ge(*at("h3", KD - 1))
            if s % 4 == 0 and m > 0:
                pe.wait_ge(*at("s5", "u", m - 1, s // 4))
            for k in range(KD):
                ins = nc.tensor.matmul(psum[0:C_ALL, s // 4, (s % 4) * P:(s % 4 + 1) * P], h3[:, k, s, :],
                                       tile_w(("s5_in", m), k), start=(k == 0), stop=(k == KD - 1))
            if s % 4 == 3:
                ins.then_inc(pe_done, 1)
                pe_count.up("s5", "u_mm", m, s // 4)
                if s == STEP - 1:
                    pe_count.mark("free", slot_of[("s5_in", m)])

        def u_act(act, m, hf):
            if m >= KE:
                return
            act.wait_ge(*at("s5", "u_mm", m, hf))
            if m >= 2:
                act.wait_ge(*at("s5", "u_turned", TILE_PAIRS * (m - 1) - 1))
            src = psum[0:C_ALL, hf, :].rearrange("p (s g i) -> p g s i", s=4, i=GS)
            for j in range(4):
                nc.scalar.activation(u_tm[0:C_ALL, m % 2, :, 4 * hf + j, :], src[:, :, j, :], ACT.Copy).then_inc(act_done, 1)
                act.wait_ge(act_done, act_count.up("s5", "u", m, hf))

        def b_split_act(act, m):
            if m >= KE:
                return
            act.wait_ge(*at("s5", "b_bar", m))
            if m >= 1:
                act.wait_ge(*at("s5", "lag_mm", m - 1, 1))
            for e in range(2):
                nc.scalar.activation(b_bar_split[:, :, :, e, :], b_bar, ACT.Copy,
                                     scale=mask("block_ones")[:, 64 * e:64 * e + 1]).then_inc(act_done, 1)
                act.wait_ge(act_done, act_count.up("s5", "b_split", m))

        def lags_pe(pe, m, hf):
            if m >= KE:
                return
            if hf == 0:
                pe.wait_ge(*at("s5", "c_pow", m))
                pe.wait_ge(*at("s5", "b_split", m))
            if m + hf >= 1:
                pe.wait_ge(*at("s5", "lag_copy", m - 1 + hf, 1 - hf))
            for pair in (2 * hf, 2 * hf + 1):
                for i, (d, lo) in enumerate(((1, 1), (0, 0))):
                    a = 256 * (pair % 2) + 112 * i
                    for ri in range(2):
                        ins = nc.tensor.matmul(psum[0:2 * GS, 4, a:a + P], b_bar_split[:, ri, 2 * pair + d, :, :],
                                               c_pow[:, m % 2, ri, 2 * pair + d, lo:lo + STEP, :],
                                               start=(i == 0 and ri == 0), stop=(i == 1 and ri == 1), skip_group_check=True)
            ins.then_inc(pe_done, 1)
            pe_count.up("s5", "lag_mm", m, hf)

        def lags_dve(dve, m):
            if m >= KE:
                return
            rows = slice(0, 2 * GS)
            for hf in range(2):
                dve.wait_ge(*at("s5", "lag_mm", m, hf))
                if hf == 0 and m >= 2:
                    dve.wait_ge(lags_moved[m % 2], 32 * (m // 2))
                src = psum[rows, 4, :].rearrange("p (g n) -> p g n", g=2)[:, :, 0:240]
                nc.vector.tensor_copy(lags[rows, m % 2, 2 * hf:2 * hf + 2, :], src).then_inc(dve_done, 1)
                dve.wait_ge(dve_done, dve_count.up("s5", "lag_copy", m, hf))
            shape = [2 * GS, TILE_PAIRS, GS]
            diagonal = dve_tmp[rows, 0:TILE_PAIRS * GS].rearrange("p (g i) -> p g i", i=GS)
            zero_lag = lags[rows, m % 2, :, 112:128]
            nc.vector.tensor_tensor(diagonal, eye[rows, :].unsqueeze(1).broadcast_to(shape),
                                    skip[rows, TILE_PAIRS * m:TILE_PAIRS * (m + 1)].unsqueeze(2).broadcast_to(shape),
                                    ALU.mult).then_inc(dve_done, 1)
            dve.wait_ge(dve_done, dve_count.up())
            nc.vector.tensor_tensor(zero_lag, zero_lag, diagonal, ALU.add).then_inc(dve_done, 1)
            dve.wait_ge(dve_done, dve_count.up("s5", "lag", m))

        def turn_pe(pe, n):
            m, pair = divmod(n, TILE_PAIRS)
            if m >= KE:
                return
            pe.wait_ge(*at("s5", "b_pow", m))
            if n >= 1:
                pe.wait_ge(*at("s5", "b_pow_t", n - 1))
            if pair == 2 and m > 0:
                pe.wait_ge(*at("s5", "yT", m - 1))
            for d in range(2):
                for ri in range(2):
                    j = 2 * d + ri
                    ins = nc.tensor.transpose(bank(2, j * P, (j + 1) * P),
                                              b_pow[:, m % 2, ri, 2 * pair + d, :, :].rearrange("p s i -> p (s i)"), mask("ident"))
            ins.then_inc(pe_done, 1)
            pe_count.up("s5", "b_turned", n)
            pe.wait_ge(*at("s5", "u", m, 1))
            if n >= 1:
                pe.wait_ge(*at("s5", "u_t", n - 1))
            for e in range(2):
                src = u_tm[0:C_ALL, m % 2, 2 * pair + e, :, :].rearrange("p s i -> p (s i)")
                ins = nc.tensor.transpose(bank(3, e * C_ALL, (e + 1) * C_ALL), src, mask("ident")[0:C_ALL, 0:C_ALL])
            ins.then_inc(pe_done, 1)
            pe_count.up("s5", "u_turned", n)

        def turn_act(act, n):
            if n >= PAIRS:
                return
            act.wait_ge(*at("s5", "b_turned", n))
            if n >= 2:
                act.wait_ge(*at("s5", "x", n - 2))
            nc.scalar.activation(b_pow_t[:, n % 2, :, :], bank(2).rearrange("p (j c) -> p j c", j=4), ACT.Copy).then_inc(act_done, 1)
            act.wait_ge(act_done, act_count.up("s5", "b_pow_t", n))
            act.wait_ge(*at("s5", "u_turned", n))
            if n >= 2:
                act.wait_ge(*at("s5", "y", n - 2))
            src = bank(3, 0, 2 * C_ALL).rearrange("p (e c) -> p e c", e=2)
            nc.scalar.activation(u_t[:, n % 2, 0, :, :], src, ACT.Copy).then_inc(act_done, 1)
            act.wait_ge(act_done, act_count.up())
            nc.scalar.activation(u_t[:, n % 2, 1, :, 0:C_CTX], src[:, :, C_CTX - 1::-1], ACT.Copy).then_inc(act_done, 1)
            act.wait_ge(act_done, act_count.up())
            nc.scalar.activation(u_t[:, n % 2, 1, :, C_CTX:C_ALL], src[:, :, C_ALL - 1:C_CTX - 1:-1], ACT.Copy).then_inc(act_done, 1)
            act.wait_ge(act_done, act_count.up("s5", "u_t", n))

        def x_pe(pe, n):
            if n >= PAIRS:
                return
            pe.wait_ge(*at("s5", "u_t", n))
            if n >= 1:
                pe.wait_ge(*at("s5", "x_read", n - 1))
            for d in range(2):
                for ri in range(2):
                    j = 2 * d + ri
                    for e in range(2):
                        ins = nc.tensor.matmul(psum[half(e), 6, j * C_ALL:(j + 1) * C_ALL],
                                               b_pow_t[:, n % 2, j, half(e)], u_t[:, n % 2, d, e, :], start=True, stop=True)
            ins.then_inc(pe_done, 1)
            pe_count.up("s5", "x", n)

        def state_dve(dve, n):
            v = nc.vector
            m, pair = divmod(n, TILE_PAIRS)
            def tt(o, a, b, op, *key):
                v.tensor_tensor(o, a, b, op).then_inc(dve_done, 1)
                dve.wait_ge(dve_done, dve_count.up(*key))

            x = bank(6, 0, 4 * C_ALL).rearrange("p (d r c) -> p d r c", d=2, r=2)
            both_parts = lambda i, a, b: (table[:, m % 2, i, 2 * pair:2 * pair + 2, a:b].unsqueeze(2)
                                          .broadcast_to([P, 2, 2, b - a]))
            dve.wait_ge(*at("s5", "x", n))
            tt(mod_c, x, both_parts(0, 0, C_ALL), ALU.mult)
            tt(mod_s, x, both_parts(1, 0, C_ALL), ALU.mult, "s5", "x_read", n)
            tt(mod_c[:, :, 0, :], mod_c[:, :, 0, :], mod_s[:, :, 1, :], ALU.add)
            tt(mod_c[:, :, 1, :], mod_c[:, :, 1, :], mod_s[:, :, 0, :], ALU.subtract)
            for d in range(2):
                decay = decay8[:, 2 * n + d:2 * n + d + 1].broadcast_to([P, C_ALL])
                for ri in range(2):
                    v.tensor_tensor_scan(zs[:, d, ri, :], decay, mod_c[:, d, ri, :], 0.0, ALU.mult, ALU.add).then_inc(dve_done, 1)
                    dve.wait_ge(dve_done, dve_count.up())
            a, b = C_CTX - 1, C_ALL - 1
            tt(mod_c[:, :, :, 0:C_LAT], zs[:, :, :, a:b], both_parts(0, a, b), ALU.mult)
            tt(mod_s[:, :, :, 0:C_LAT], zs[:, :, :, a:b], both_parts(1, a, b), ALU.mult)
            if n >= 2:
                dve.wait_ge(*at("s5", "y", n - 2))
            for d in range(2):
                for ri, op in enumerate((ALU.subtract, ALU.add)):
                    o = x_in[:, n % 2, d, ri, :]
                    o = o if d == 0 else o[:, ::-1]
                    tt(o, mod_c[:, d, ri, 0:C_LAT], mod_s[:, d, 1 - ri, 0:C_LAT], op, "s5", "x_in", n)

        def y_pe(pe, n):
            m, pair = divmod(n, TILE_PAIRS)
            pe.wait_ge(*at("s5", "x_in", n))
            if n >= 1:
                pe.wait_ge(*at("s5", "y_tm", n - 1))
            if pair == 0:
                pe.wait_ge(lags_moved[2 + m % 2], 16 * 8 * (m // 2 + 1))
            cp = c_pow[:, m % 2, :, :, :, :]
            for e in range(2):
                o = psum[0:C_LAT, 5 + 2 * e, 0:P]
                nc.tensor.matmul(o, u_t[:, n % 2, 0, e, C_CTX:C_ALL], lag_m[:, m % 2, 2 * pair + e, :], start=True, stop=False)
                for d, lo in ((0, 1), (1, 0)):
                    for ri in range(2):
                        ins = nc.tensor.matmul(o, x_in[half(e), n % 2, d, ri, :], cp[half(e), ri, 2 * pair + d, lo:lo + STEP, :],
                                               start=False, stop=(d == 1 and ri == 1))
            ins.then_inc(pe_done, 1)
            pe_count.up("s5", "y", n)

        def y_act(act, n):
            m, pair = divmod(n, TILE_PAIRS)
            act.wait_ge(*at("s5", "y", n))
            if pair == 0 and m > 0:
                act.wait_ge(*at("s5", "y_turned", m - 1))
            for e in range(2):
                g = 2 * pair + e
                nc.scalar.activation(y_tm[0:C_LAT, :, g * GS:(g + 1) * GS],
                                     psum[0:C_LAT, 5 + 2 * e, 0:P].rearrange("p (t i) -> p t i", i=GS), ACT.Copy).then_inc(act_done, 1)
                act.wait_ge(act_done, act_count.up("s5", "y_tm", n))

        def y_turn_pe(pe, m):
            pe.wait_ge(*at("s5", "y_tm", TILE_PAIRS * (m + 1) - 1))
            pe.wait_ge(*at("s5", "b_pow_t", min(TILE_PAIRS * (m + 1) + 1, PAIRS - 1)))
            for s in range(STEP):
                ins = nc.tensor.transpose(bank(2, s * C_LAT, (s + 1) * C_LAT), y_tm[0:C_LAT, s, :], mask("ident")[0:C_LAT, 0:C_LAT])
            ins.then_inc(pe_done, 1)
            pe_count.up("s5", "y_turned", m)

        def y_turn_act(act, m):
            act.wait_ge(*at("s5", "y_turned", m))
            nc.scalar.activation(yT[:, m, :], bank(2), ACT.Gelu_apprx_tanh).then_inc(act_done, 1)
            act.wait_ge(act_done, act_count.up("s5", "yT", m))

        TOKENS = ((0, 1, 2), (3, 4, 5), (6, 7), ())

        def s5_pe(pe):
            for s in range(STEP):
                u_project_pe(pe, 0, s)
            for hf in range(2):
                lags_pe(pe, 0, hf)
            turn_pe(pe, 0)
            x_pe(pe, 0)
            for m in range(KE):
                for pair in range(TILE_PAIRS):
                    n = m * TILE_PAIRS + pair
                    turn_pe(pe, n + 1)
                    for s in TOKENS[pair]:
                        u_project_pe(pe, m + 1, s)
                    if pair == 0 and m > 0:
                        y_turn_pe(pe, m - 1)
                    if pair == TILE_PAIRS - 1:
                        lags_pe(pe, m + 1, 0)
                    x_pe(pe, n + 1)
                    if pair == TILE_PAIRS - 1:
                        lags_pe(pe, m + 1, 1)
                    y_pe(pe, n)
            y_turn_pe(pe, KE - 1)

        def s5_act(act):
            u_act(act, 0, 0)
            u_act(act, 0, 1)
            b_split_act(act, 0)
            turn_act(act, 0)
            for m in range(KE):
                for pair in range(TILE_PAIRS):
                    n = m * TILE_PAIRS + pair
                    turn_act(act, n + 1)
                    if pair == 0 and m > 0:
                        y_turn_act(act, m - 1)
                    if pair == 1:
                        u_act(act, m + 1, 0)
                    if pair == 2:
                        u_act(act, m + 1, 1)
                        b_split_act(act, m + 1)
                    y_act(act, n)
            y_turn_act(act, KE - 1)

        def s5_dve(dve):
            for i in range(6):
                c_pow_dve(dve, 0, i)
            lags_dve(dve, 0)
            table_dve(dve, 0)
            for m in range(KE):
                for pair in range(TILE_PAIRS):
                    state_dve(dve, m * TILE_PAIRS + pair)
                    if pair == 0:
                        for i in range(3):
                            c_pow_dve(dve, m + 1, i)
                    if pair == 1:
                        for i in range(3, 6):
                            c_pow_dve(dve, m + 1, i)
                    if pair == TILE_PAIRS - 1:
                        lags_dve(dve, m + 1)
                        table_dve(dve, m + 1)

        def s5_pool(pool):
            for m in range(KE):
                b_bar_pool(pool, m)
                b_pow_pool(pool, m)
                table_pool(pool, m)

        s5.close()

        gl = ExitStack()
        gates = yT
        split = sb(gl, "split", [2, KE, T])
        w_split = sb(gl, "w_split", [2, 2, HALF_SLOT])
        spare = ctxT[:, :, :].rearrange("p k t -> p (k t)")
        sig = spare[:, 0:2 * T].rearrange("p (b t) -> p b t", b=2)
        glu_tmp = spare[:, 2 * T:4 * T].rearrange("p (b t) -> p b t", b=2)
        sq_3 = yT[:, 0:KD, :]
        stat_3 = yT[:, KD:KD + 2, :]

        def gates_pe(pe):
            for i in range(KE):
                need_slot(pe, ("s5_in", KE + i))
                if i >= 2:
                    pe.wait_ge(*at("gates", i - 2))
                for k in range(KD):
                    ins = nc.tensor.matmul(bank(i % 2), tile_w(("s5_in", KE + i), k), h3[:, k, :, C_CTX:C_ALL],
                                           start=(k == 0), stop=(k == KD - 1))
                ins.then_inc(pe_done, 1)
                pe_count.up("gates_mm", i)
                pe_count.mark("free", slot_of[("s5_in", KE + i)])

        def gates_act(act):
            for i in range(KE):
                split_act(act, "y_split", split, yT, i)
                act.wait_ge(*at("y_split", "rest", i))
                act.wait_ge(*at("gates_mm", i))
                nc.scalar.activation(gates[:, i, :], bank(i % 2), ACT.Silu).then_inc(act_done, 1)
                act.wait_ge(act_done, act_count.up("gates", i))

        def gates_dve(dve):
            for i in range(KE):
                split_dve(dve, "y_split", split, yT, i)

        glu_keys = [("glu", j) for i in range(KE) for j in (2 * i, 2 * i + 1, 2 * KE + 2 * i, 2 * KE + 2 * i + 1)]
        w_act, w_dve, _, w_pe = split_weights("glu_w", w_split, glu_keys)
        out_w_act, out_w_dve, _, out_w_pe = split_weights("s5_out_w", w_split, [("s5_out", i) for i in range(2 * KD)])
        UNITS_OF_ROW = KE // UNIT_K

        split_of = split_values(split)

        def glu_pe(pe):
            for i in range(KE):
                b = 2 + 2 * (i % 3)
                if i == 0:
                    pe.wait_ge(*at("y_split", "rest", KE - 1))
                if i >= 3:
                    pe.wait_ge(*at("glu", i - 3))
                for hf in range(2):
                    for unit in range(UNITS_OF_ROW):
                        w_pe(pe, (2 * i + hf) * UNITS_OF_ROW + unit, bank(b + hf), split_of(unit),
                             unit == 0, unit == UNITS_OF_ROW - 1)
                    pe_count.mark("glu_mm", i, hf)

        def glu_sig_act(act, i):
            act.wait_ge(*at("glu_mm", i, 1))
            if i >= 2:
                act.wait_ge(*at("glu", i - 2))
            nc.scalar.activation(sig[:, i % 2, :], bank(3 + 2 * (i % 3)), ACT.Sigmoid, bias=col("b_glu", KE + i)).then_inc(act_done, 1)
            act.wait_ge(act_done, act_count.up("glu_sig", i))

        def glu_act(act):
            for i in range(KE):
                for unit in range(2 * UNITS_OF_ROW):
                    w_act(act, 2 * i * UNITS_OF_ROW + unit)
                    if unit == 2 and i > 0:
                        glu_sig_act(act, i - 1)
            glu_sig_act(act, KE - 1)

        def glu_out_dve(dve, i):
            dve.wait_ge(*at("glu_sig", i))
            nc.vector.scalar_tensor_tensor(out=glu_tmp[:, i % 2, :], in0=bank(2 + 2 * (i % 3)), scalar=col("b_glu", i),
                                           in1=sig[:, i % 2, :], op0=ALU.add, op1=ALU.mult).then_inc(dve_done, 1)
            dve.wait_ge(dve_done, dve_count.up("glu", i))
            nc.vector.tensor_tensor(gates[:, i, :], gates[:, i, :], glu_tmp[:, i % 2, :], ALU.mult).then_inc(dve_done, 1)
            dve.wait_ge(dve_done, dve_count.up("glu_out", i))

        def glu_dve(dve):
            for i in range(KE):
                for unit in range(2 * UNITS_OF_ROW):
                    w_dve(dve, 2 * i * UNITS_OF_ROW + unit)
                    if unit == 2 and i > 0:
                        glu_out_dve(dve, i - 1)
            glu_out_dve(dve, KE - 1)

        def s5_out_pe(pe):
            for m in range(KD):
                if m >= 2:
                    pe.wait_ge(*at("residual3", m - 2))
                for unit in range(UNITS_OF_ROW):
                    if m == 0:
                        pe.wait_ge(*at("g_split", "rest", (unit + 1) * UNIT_K - 1))
                    out_w_pe(pe, m * UNITS_OF_ROW + unit, bank(m % 2), split_of(unit),
                             unit == 0, unit == UNITS_OF_ROW - 1)
                pe_count.mark("s5_out", m)

        def s5_out_act(act):
            act.wait_ge(*at("glu_mm", KE - 1, 1))
            for unit in range(UNITS_OF_ROW):
                if unit < 2:
                    out_w_act(act, unit)
                for i in range(unit * UNIT_K, (unit + 1) * UNIT_K):
                    act.wait_ge(*at("glu_out", i))
                    split_act(act, "g_split", split, yT, i)
            for u in range(2, KD * UNITS_OF_ROW):
                out_w_act(act, u)

        z3 = h3[:, :, :, :].rearrange("p k s c -> p (k s c)")[:, 0:KD * T].rearrange("p (k t) -> p k t", k=KD)

        def s5_out_dve(dve):
            for unit in range(UNITS_OF_ROW):
                if unit < 2:
                    out_w_dve(dve, unit)
                for i in range(unit * UNIT_K, (unit + 1) * UNIT_K):
                    split_dve(dve, "g_split", split, yT, i)
            for u in range(2, KD * UNITS_OF_ROW):
                out_w_dve(dve, u)
                if u % UNITS_OF_ROW == 1 and u > UNITS_OF_ROW:
                    residual3_dve(dve, u // UNITS_OF_ROW - 1)
            residual3_dve(dve, KD - 1)

        def residual3_dve(dve, m):
            z = z3[:, m, :].rearrange("p (s c) -> p s c", s=STEP)
            nc.vector.tensor_scalar(z, xT[:, m, :].rearrange("p (c s) -> p s c", s=STEP), ALPHA_2, None, ALU.mult).then_inc(dve_done, 1)
            dve.wait_ge(dve_done, dve_count.up())
            dve.wait_ge(*at("s5_out", m))
            nc.vector.scalar_tensor_tensor(out=z3[:, m, :], in0=bank(m % 2), scalar=mods[1][:, 2 * KD + m, 1:2],
                                           in1=z3[:, m, :], op0=ALU.mult, op1=ALU.add).then_inc(dve_done, 1)
            dve.wait_ge(dve_done, dve_count.up("residual3", m))
            dve_count.mark("ln3", "z", m)

        ln3_pe, ln3_act, ln3_dve = layer_norm_cm("ln3", z3, T, sq_3, stat_3, lambda k: col("ln_g_21", k), lambda k: col("ln_b_21", k), eps[:, 2:3],
                            lambda k: [(z3[:, k, :], z3[:, k, :])])
        gl.close()

        def output_sync(sp):
            for k in range(KD):
                sp.wait_ge(*at("ln3", "out", k))
                sp.dma_start(io["out"][:, k, :], z3[:, k, :]).then_inc(stored, 16)
            sp.wait_ge(stored, 16 * KD)

        block = memory.enter_context(nc.Block())

        @block.sync
        def _(sp):
            sp.dma_start(const[:, :], io["const"]).then_inc(small_loaded, 16)
            sp.dma_start(cols[:, :], io["cols"]).then_inc(small_loaded, 16)
            sp.dma_start(xT[:, :, :], io["xT"]).then_inc(x_loaded, 16)
            for n, (tensor, i, floats, _) in enumerate(stream):
                if n == 8:
                    sp.dma_start(lnv[:, :, :], io["lnv"].partition_broadcast(P)).then_inc(gmlp_loaded, 16)
                    sp.dma_start(w_sp[:, :, :], io["w_sp"]).then_inc(gmlp_loaded, 16)
                    for e2 in range(2):
                        sp.dma_start(b_sp[64 * e2:64 * e2 + 64, :, :], io["b_sp"][e2].partition_broadcast(64)).then_inc(gmlp_loaded, 16)
                if n == slot_of[("mod0", RING - 1)]:
                    for who in ("pe", "act", "dve"):
                        sp.wait_ge(*at("end", "projections", who))
                    for e2 in range(2):
                        sp.dma_start(up[64 * e2:64 * e2 + 64, :], io["up"][64 * e2:64 * e2 + 64, :]).then_inc(gmlp_loaded, 16)
                if n == slot_of[("mla_in", 4)]:
                    sp.wait_ge(*at("end", "first_block", "dve"))
                    sp.wait_ge(*at("end", "first_block", "pe"))
                    sp.wait_ge(*at("end", "first_block", "act"))
                    sp.dma_start(ctxT[:, :, :], io["ctxT"]).then_inc(ctx_loaded, 16)
                    sp.dma_start(lam, io["lam"]).then_inc(lam_loaded, 16)
                if n == slot_of[("s5_in", 0)]:
                    for who in ("pe", "act", "dve"):
                        sp.wait_ge(*at("end", "mla", who))
                    sp.dma_start(skip[0:2 * GS, :], io["skip"]).then_inc(small_loaded, 16)
                    sp.dma_start(bc[:, :, :, :], io["bc"][0]).then_inc(table_loaded, 16)
                tile = n - slot_of[("s5_in", 0)] - RING + 1
                if 0 <= tile < KE:
                    if tile + 1 < KE:
                        sp.wait_ge(*at("s5", "b_bar", tile))
                        sp.wait_ge(*at("s5", "c_pow", tile))
                        sp.dma_start(bc[:, :, :, :], io["bc"][tile + 1]).then_inc(table_loaded, 16)
                    sp.wait_ge(*at("s5", "lag", tile))
                    for e2 in range(2):
                        sp.dma_start(io["lags"][tile % 2][:, e2::2, :],
                                     lags[GS * e2:GS * (e2 + 1), tile % 2, :, :]).then_inc(lags_moved[tile % 2], 16)
                    sp.wait_ge(lags_moved[tile % 2], 32 * (tile // 2 + 1))
                    if tile >= 2:
                        sp.wait_ge(*at("s5", "y", TILE_PAIRS * (tile - 1) - 1))
                    for s in range(STEP):
                        sp.dma_start(lag_m[GS * s:GS * (s + 1), tile % 2, :, :],
                                     io["lags"][tile % 2][:, :, (7 - s) * GS:(7 - s) * GS + P]).then_inc(lags_moved[2 + tile % 2], 16)
                if n >= RING:
                    sp.wait_ge(*at("free", n - RING))
                sp.dma_start(ring[:, n % RING, 0:floats], io[tensor][i]).then_inc(slot_loaded[n % RING], 16)
            output_sync(sp)

        @block.tensor
        def _(pe):
            ada_pe(pe)
            project_pe(pe)
            mixing_pe(pe)
            phase_end(pe, pe_count, "projections")
            for q in range(NPAIR):
                rwkv_prep_pe(pe, q)
                rwkv_unit_pe(pe, q)
            group_norm_pe(pe)
            phase_end(pe, pe_count, "rwkv")
            out_pe(pe)
            ln1_pe(pe)
            phase_end(pe, pe_count, "first_block")
            mla_in_pe(pe)
            for h in range(-1, HEADS + 1):
                head_pe(pe, h)
            phase_end(pe, pe_count, "heads")
            mla_out_pe(pe)
            ln2_pe(pe)
            phase_end(pe, pe_count, "mla")
            s5_pe(pe)
            phase_end(pe, pe_count, "s5")
            gates_pe(pe)
            glu_pe(pe)
            s5_out_pe(pe)
            ln3_pe(pe)

        @block.scalar
        def _(act):
            ada_act(act)
            h_split_act(act)
            project_act(act)
            phase_end(act, act_count, "projections")
            rwkv_start_act(act)
            for q in range(NPAIR):
                rwkv_prep_act(act, q)
                rwkv_unit_act(act, q)
            group_norm_act(act)
            phase_end(act, act_count, "rwkv")
            out_act(act)
            ln1_act(act)
            phase_end(act, act_count, "first_block")
            s5_dt_act(act)
            mla_in_act(act)
            for h in range(-1, HEADS + 1):
                head_act(act, h)
            phase_end(act, act_count, "heads")
            ln2_after_gates_act(act)
            phase_end(act, act_count, "mla")
            s5_act(act)
            phase_end(act, act_count, "s5")
            gates_act(act)
            glu_act(act)
            s5_out_act(act)
            ln3_act(act)

        @block.vector
        def _(dve):
            start_dve(dve)
            ada_dve(dve)
            h_split_dve(dve)
            project_dve(dve)
            mixing_dve(dve)
            phase_end(dve, dve_count, "projections")
            rwkv_start_dve(dve)
            for q in range(NPAIR):
                rwkv_prep_dve(dve, q)
                rwkv_unit_dve(dve, q)
            group_norm_dve(dve)
            phase_end(dve, dve_count, "rwkv")
            out_dve(dve)
            ln1_dve(dve)
            phase_end(dve, dve_count, "first_block")
            mla_h_dve(dve)
            s5_setup_dve(dve)
            mla_in_dve(dve)
            for h in range(-1, HEADS + 1):
                head_dve(dve, h)
            phase_end(dve, dve_count, "heads")
            mla_out_dve(dve)
            ln2_dve(dve)
            phase_end(dve, dve_count, "mla")
            s5_start_dve(dve)
            s5_dve(dve)
            phase_end(dve, dve_count, "s5")
            gates_dve(dve)
            glu_dve(dve)
            s5_out_dve(dve)
            ln3_dve(dve)

        @block.gpsimd
        def _(pool):
            project_pool(pool)
            mask_pool(pool)
            phase_end(pool, pool_count, "projections")
            for q in range(NPAIR):
                rwkv_unit_pool(pool, q)
            phase_end(pool, pool_count, "rwkv")
            out_pool(pool)
            phase_end(pool, pool_count, "first_block")
            phase_end(pool, pool_count, "heads")
            phase_end(pool, pool_count, "mla")
            s5_pool(pool)
            phase_end(pool, pool_count, "s5")

        layers.close()
    return steps


def tiles(w, k_tiles):
    k, m = w.shape
    t = w.reshape(k // P, P, m // P, P).transpose(2, 1, 0, 3)
    n = k // P // k_tiles
    t = t.reshape(m // P, P, n, k_tiles, P).transpose(0, 2, 1, 3, 4)
    return np.ascontiguousarray(t).reshape(m // P * n, P, k_tiles * P)


def per_channel(v):
    return v.reshape(-1, P).T


def rope_columns(w):
    a, b, c, d = np.split(w, 4, axis=-1)
    return np.concatenate([w, b, a, d, c], axis=-1)


def lay_out(i):
    o = {"const": constants()}
    o["xT"] = np.ascontiguousarray(i["x"][0].T.reshape(KD, P, T).transpose(1, 0, 2))
    o["ctxT"] = np.ascontiguousarray(i["ctx_2"][0].T.reshape(KD, P, CTX).transpose(1, 0, 2))
    v = {
        "c": i["c"][0], "b_ada": i["b_ada"], "mu_b": i["mu_b"], "w0": i["w0"], "a0": i["a0"], "k_k": i["k_k"],
        "k_a": i["k_a"], "r_k": i["r_k"].reshape(-1), "gn_g": i["gn_g"].reshape(-1), "gn_b": i["gn_b"].reshape(-1),
        "ln_g": i["ln_g"], "ln_b": i["ln_b"], "c_2": i["c_2"][0], "c_ctx_2": i["c_ctx_2"],
        "b_mod_0": i["b_mod_2"][0], "b_mod_1": i["b_mod_2"][1], "ln_g_20": i["ln_g_2"][0], "ln_b_20": i["ln_b_2"][0],
        "ln_g_21": i["ln_g_2"][1], "ln_b_21": i["ln_b_2"][1], "q_norm": i["mla_q_norm_2"][0],
        "kv_norm": i["mla_kv_norm_2"][0], "s5_d": i["s5_d_2"][0], "b_glu": i["s5_b_glu_2"][0],
    }
    o["cols"] = np.ascontiguousarray(np.concatenate([per_channel(v[k]) for k, _ in COLUMNS], axis=1))
    o["lnv"] = np.ascontiguousarray(np.stack([i["ln_v_g"].reshape(-1), i["ln_v_b"].reshape(-1)]))
    o["w_sp"] = np.ascontiguousarray(i["w_spatial"].transpose(2, 0, 1))
    o["b_sp"] = np.ascontiguousarray(i["b_spatial"].reshape(4, 2, P).transpose(1, 0, 2))
    o["up"] = np.ascontiguousarray(np.concatenate([i["w_up"], i["a_up"]]))
    o["w_ada"] = tiles(i["w_ada"], KD)
    o["w_in"] = tiles(i["w_in"], KD)
    o["w_out"] = tiles(i["w_out"], KD)
    o["w_mod_0"] = tiles(i["w_mod_2"][0], KD)
    o["w_mod_1"] = tiles(i["w_mod_2"][1], KD)
    w = i["mla_w_in_2"][0]
    r = Q_RANK + KV_RANK
    w = np.concatenate([w[:, :r], rope_columns(w[:, r:r + ROPE]), w[:, r + ROPE:]], axis=1)
    o["mla_in"] = tiles(w, KD)
    uq = i["mla_w_uq_2"][0].reshape(2, P, HEADS, 192)
    uq = np.concatenate([uq[..., :128], rope_columns(uq[..., 128:])], axis=-1)
    uq = uq.transpose(2, 1, 0, 3).reshape(HEADS, P, 512)
    uk = i["mla_w_uk_2"][0].transpose(1, 2, 0)
    uv = i["mla_w_uv_2"][0].transpose(1, 0, 2)
    o["mla_head"] = np.ascontiguousarray(np.concatenate([uq, uk, uv], axis=2))
    o["mla_out"] = tiles(i["mla_w_out_2"][0], KD)
    o["s5_in"] = tiles(i["s5_w_in_2"][0], KD)
    o["s5_glu"] = tiles(i["s5_w_glu_2"][0], KD)
    o["s5_out"] = tiles(i["s5_w_out_2"][0], KD)
    lam = lambda a: a[0].reshape(2, PAIRS, P).transpose(2, 1, 0)
    dt = np.repeat(i["s5_log_dt_2"][0][:, :, None], STATE, axis=2)
    lams = np.stack([lam(i["s5_lam_re_2"]), lam(i["s5_lam_im_2"]), lam(dt[None])], axis=1)
    o["lam"] = np.ascontiguousarray(lams).reshape(P, 3, 2 * PAIRS)
    b = lambda a: a[0].reshape(2, KE, 4, P, GS).transpose(1, 3, 2, 0, 4)
    cm = lambda a: b(a.transpose(0, 1, 2, 4, 3))
    bc = np.stack([b(i["s5_b_re_2"]), b(i["s5_b_im_2"]), cm(i["s5_c_re_2"]), cm(i["s5_c_im_2"])], axis=2)
    o["bc"] = np.ascontiguousarray(bc).reshape(KE, P, 4, 8, GS)
    o["skip"] = np.ascontiguousarray(i["s5_d_2"][0].reshape(PAIRS, 2 * GS).T)
    return o


OUT_SHAPE = (P, KD, T)


def program(nc, shapes, known):
    io = {name: nc.dram_tensor(f"in_{name}", shape, F32, kind="ExternalInput").ap() for name, shape in shapes.items()}
    io["lags"] = nc.dram_tensor("lags", (2, GS, 8, 240), F32, kind="Internal").ap()
    io["out"] = nc.dram_tensor("outT", OUT_SHAPE, F32, kind="ExternalOutput").ap()
    return build(nc, io, known)


def kernel(**inputs):
    import concourse.bacc as bacc
    from concourse.bass_utils import run_bass_kernel_spmd as run

    arrays = lay_out({k: np.asarray(v) for k, v in inputs.items()})
    shapes = {k: v.shape for k, v in arrays.items()}
    known = program(bacc.Bacc("TRN2", target_bir_lowering=False, num_devices=1), shapes, {})
    nc = bacc.Bacc("TRN2", target_bir_lowering=False, num_devices=1)
    program(nc, shapes, known)
    result = run(nc, [{f"in_{k}": v for k, v in arrays.items()}], core_ids=[0]).results[0]["outT"]
    out = result.reshape(P, KD, STEP, C_LAT).transpose(3, 2, 1, 0)
    return np.ascontiguousarray(out).reshape(1, T, D)
```
